# Optimizing a Trainium2 kernel written in Bass

```python
import jax, jax.numpy as jnp
from jax import lax
import numpy as np

D_MODEL = 1024
BATCH = 1
SEQ = 256
DEPTH = 2

NUM_MIXERS = 4
RMS_EPS = 1e-6
ROPE_THETA = 500000.0
ATTN_BLOCK = 128

SSM_D_INNER = 2 * D_MODEL
SSM_HEAD_DIM = 64
SSM_N_HEADS = SSM_D_INNER // SSM_HEAD_DIM
SSM_D_STATE = 128
SSM_N_GROUPS = 8
SSM_CONV = 4
SSM_CHUNK = 128
SSM_BC_DIM = SSM_N_GROUPS * SSM_D_STATE
SSM_CONV_DIM = SSM_D_INNER + 2 * SSM_BC_DIM
SSM_IN_COLS = SSM_D_INNER + SSM_CONV_DIM + SSM_N_HEADS
SSM_DT_MIN = 0.001
SSM_DT_MAX = 0.1

MLA_N_HEADS = 16
MLA_Q_LORA = 3 * D_MODEL // 8
MLA_KV_LORA = D_MODEL // 4
MLA_NOPE_DIM = 128
MLA_ROPE_DIM = 64
MLA_V_DIM = 128
MLA_QK_DIM = MLA_NOPE_DIM + MLA_ROPE_DIM
MLA_WIDTH = MLA_N_HEADS * MLA_V_DIM
MLA_IN_COLS = MLA_Q_LORA + MLA_KV_LORA + MLA_ROPE_DIM + MLA_WIDTH

FOX_N_HEADS = 16
FOX_HEAD_DIM = 128
FOX_WIDTH = FOX_N_HEADS * FOX_HEAD_DIM
FOX_IN_COLS = 3 * FOX_WIDTH + FOX_N_HEADS + FOX_WIDTH
FOX_F_BIAS_MEAN = 3.0

DIL_CONFIGS = ((128, 1), (512, 4), (2048, 16))
DIL_N_HEADS = 8
DIL_HEAD_DIM = 128
DIL_WIDTH = DIL_N_HEADS * DIL_HEAD_DIM
DIL_ROPE_DIM = DIL_HEAD_DIM // 4
DIL_IN_COLS = 3 * len(DIL_CONFIGS) * DIL_WIDTH + DIL_WIDTH

N_SSM_LAYERS = (DEPTH + 3) // NUM_MIXERS
N_MLA_LAYERS = (DEPTH + 2) // NUM_MIXERS
N_FOX_LAYERS = (DEPTH + 1) // NUM_MIXERS
N_DIL_LAYERS = DEPTH // NUM_MIXERS


def rms_norm(x, w):
    xf = x.astype(jnp.float32)
    return (xf * lax.rsqrt(jnp.mean(xf * xf, axis=-1, keepdims=True) + RMS_EPS)).astype(x.dtype) * w

def rope(x, positions):
    half = x.shape[-1] // 2
    inv_freq = ROPE_THETA ** (-jnp.arange(half, dtype=jnp.float32) / half)
    ang = positions.astype(jnp.float32)[:, None] * inv_freq[None, :]
    cos = jnp.cos(ang)[None, :, None, :]
    sin = jnp.sin(ang)[None, :, None, :]
    x1 = x[..., :half].astype(jnp.float32)
    x2 = x[..., half:].astype(jnp.float32)
    return jnp.concatenate([x1 * cos - x2 * sin, x2 * cos + x1 * sin], axis=-1).astype(x.dtype)

def partial_rope(x, positions):
    return jnp.concatenate([rope(x[..., :DIL_ROPE_DIM], positions), x[..., DIL_ROPE_DIM:]], axis=-1)

def causal_depthwise_conv(x, w, b):
    k = w.shape[0]
    y = lax.conv_general_dilated(x, w[:, None, :], window_strides=(1,), padding=[(k - 1, 0)],
                                 dimension_numbers=('NWC', 'WIO', 'NWC'), feature_group_count=x.shape[-1])
    return y + b

def gated_group_rms_norm(y, z, w, groups):
    g = y * jax.nn.silu(z.astype(jnp.float32))
    shp = g.shape
    gg = g.reshape(shp[:-1] + (groups, shp[-1] // groups))
    gg = gg * lax.rsqrt(jnp.mean(gg * gg, axis=-1, keepdims=True) + RMS_EPS)
    return gg.reshape(shp) * w

def ssd_chunked(xdt, a, b_in, c_out):
    bsz, seq, heads, p = xdt.shape
    g, n = b_in.shape[2], b_in.shape[3]
    r = heads // g
    t = SSM_CHUNK
    nc = seq // t
    xc = xdt.reshape(bsz, nc, t, g, r, p)
    bc = b_in.reshape(bsz, nc, t, g, n)
    cc = c_out.reshape(bsz, nc, t, g, n)
    a_cum = jnp.cumsum(a.reshape(bsz, nc, t, g, r).transpose(0, 3, 4, 1, 2), axis=-1)
    causal = jnp.tril(jnp.ones((t, t), dtype=bool))
    seg = a_cum[..., :, None] - a_cum[..., None, :]
    decay_in = jnp.exp(jnp.where(causal, seg, -jnp.inf))
    cb = jnp.einsum('bctgn,bcsgn->bgcts', cc, bc)
    y_diag = jnp.einsum('bgcts,bgrcts,bcsgrp->bctgrp', cb, decay_in, xc)
    decay_to_end = jnp.exp(a_cum[..., -1:] - a_cum)
    chunk_states = jnp.einsum('bctgn,bgrct,bctgrp->bcgrpn', bc, decay_to_end, xc)
    chunk_decay = jnp.exp(a_cum[..., -1])

    def carry_state(state, inp):
        st, dec = inp
        return state * dec[..., None, None] + st, state

    init = jnp.zeros_like(chunk_states[:, 0])
    _, entering = lax.scan(carry_state, init,
                           (chunk_states.swapaxes(0, 1), chunk_decay.transpose(3, 0, 1, 2)))
    entering = entering.swapaxes(0, 1)
    y_off = jnp.einsum('bctgn,bcgrpn,bgrct->bctgrp', cc, entering, jnp.exp(a_cum))
    return (y_diag + y_off).reshape(bsz, seq, heads, p)

def causal_block_attention(q, k, v, scale, log_forget_cum=None):
    bsz, seq, heads, dk = q.shape
    nb = seq // ATTN_BLOCK
    key_pos = jnp.arange(seq)
    q_blocks = q.reshape(bsz, nb, ATTN_BLOCK, heads, dk).swapaxes(0, 1)
    block_ids = jnp.arange(nb)
    use_decay = log_forget_cum is not None
    if use_decay:
        c_k = log_forget_cum.astype(jnp.float32).transpose(0, 2, 1)
        c_blocks = c_k.reshape(bsz, heads, nb, ATTN_BLOCK).transpose(2, 0, 1, 3)
        xs = (q_blocks, block_ids, c_blocks)
    else:
        xs = (q_blocks, block_ids)

    def attend(args):
        qb, bi = args[0], args[1]
        s = jnp.einsum('bqhd,bkhd->bhqk', qb, k).astype(jnp.float32) * scale
        if use_decay:
            s = s + args[2][..., :, None] - c_k[:, :, None, :]
        q_pos = bi * ATTN_BLOCK + jnp.arange(ATTN_BLOCK)
        s = jnp.where(key_pos[None, :] <= q_pos[:, None], s, -jnp.inf)
        p = jax.nn.softmax(s, axis=-1)
        return jnp.einsum('bhqk,bkhd->bqhd', p.astype(v.dtype), v)

    out = lax.map(attend, xs)
    return out.swapaxes(0, 1).reshape(bsz, seq, heads, v.shape[-1])

def dilated_band_attention(q, k, v, dilation, span):
    bsz, seq, heads, dh = q.shape
    length = seq // dilation
    nseq = bsz * dilation

    def to_residue(u):
        return u.reshape(bsz, length, dilation, heads, dh).transpose(0, 2, 1, 3, 4).reshape(nseq, length, heads, dh)

    blk = min(span, length)
    nb = -(-length // blk)
    padded = nb * blk
    padw = ((0, 0), (0, padded - length), (0, 0), (0, 0))
    qs = jnp.pad(to_residue(q), padw).reshape(nseq, nb, blk, heads, dh)
    ks = jnp.pad(to_residue(k), padw).reshape(nseq, nb, blk, heads, dh)
    vs = jnp.pad(to_residue(v), padw).reshape(nseq, nb, blk, heads, dh)

    def with_prev(u):
        prev = jnp.pad(u, ((0, 0), (1, 0), (0, 0), (0, 0), (0, 0)))[:, :nb]
        return jnp.concatenate([prev, u], axis=2)

    kw, vw = with_prev(ks), with_prev(vs)
    s = jnp.einsum('nbqhd,nbkhd->nbhqk', qs, kw).astype(jnp.float32) * (dh ** -0.5)
    q_idx = jnp.arange(blk)[:, None] + blk
    k_idx = jnp.arange(2 * blk)[None, :]
    dist = q_idx - k_idx
    key_abs = (jnp.arange(nb) * blk - blk)[:, None] + jnp.arange(2 * blk)[None, :]
    valid = ((dist >= 0) & (dist <= span))[None, :, :] & (key_abs >= 0)[:, None, :]
    s = jnp.where(valid[None, :, None, :, :], s, -jnp.inf)
    m = jnp.max(s, axis=-1, keepdims=True)
    p = jnp.exp(s - m)
    den = jnp.sum(p, axis=-1)
    o = jnp.einsum('nbhqk,nbkhd->nbqhd', p, vw.astype(jnp.float32)) / den.transpose(0, 1, 3, 2)[..., None]
    lse = (m[..., 0] + jnp.log(den)).transpose(0, 1, 3, 2)
    o = o.reshape(nseq, padded, heads, dh)[:, :length]
    lse = lse.reshape(nseq, padded, heads)[:, :length]
    o = o.reshape(bsz, dilation, length, heads, dh).transpose(0, 2, 1, 3, 4).reshape(bsz, seq, heads, dh)
    lse = lse.reshape(bsz, dilation, length, heads).transpose(0, 2, 1, 3).reshape(bsz, seq, heads)
    return o, lse

def ssd_mixer(u, in_w, conv_w, conv_b, dt_bias, a_log, d_skip, norm_w, out_w):
    bsz, seq, _ = u.shape
    proj = u @ in_w
    z = proj[..., :SSM_D_INNER]
    xbc = proj[..., SSM_D_INNER:SSM_D_INNER + SSM_CONV_DIM]
    dt_raw = proj[..., SSM_D_INNER + SSM_CONV_DIM:]
    xbc = jax.nn.silu(causal_depthwise_conv(xbc, conv_w, conv_b)).astype(jnp.float32)
    xs = xbc[..., :SSM_D_INNER].reshape(bsz, seq, SSM_N_HEADS, SSM_HEAD_DIM)
    b_in = xbc[..., SSM_D_INNER:SSM_D_INNER + SSM_BC_DIM].reshape(bsz, seq, SSM_N_GROUPS, SSM_D_STATE)
    c_out = xbc[..., SSM_D_INNER + SSM_BC_DIM:].reshape(bsz, seq, SSM_N_GROUPS, SSM_D_STATE)
    dt = jax.nn.softplus(dt_raw.astype(jnp.float32) + dt_bias.astype(jnp.float32))
    a = dt * (-jnp.exp(a_log.astype(jnp.float32)))
    y = ssd_chunked(xs * dt[..., None], a, b_in, c_out)
    y = y + d_skip.astype(jnp.float32)[:, None] * xs
    y = gated_group_rms_norm(y.reshape(bsz, seq, SSM_D_INNER), z, norm_w, SSM_N_GROUPS)
    return y.astype(u.dtype) @ out_w

def mla_mixer(u, positions, in_w, q_norm_w, kv_norm_w, uq_w, ukv_w, out_w):
    bsz, seq, _ = u.shape
    proj = u @ in_w
    o1 = MLA_Q_LORA
    o2 = o1 + MLA_KV_LORA
    o3 = o2 + MLA_ROPE_DIM
    c_q, c_kv, k_r, z = proj[..., :o1], proj[..., o1:o2], proj[..., o2:o3], proj[..., o3:]
    q = (rms_norm(c_q, q_norm_w) @ uq_w).reshape(bsz, seq, MLA_N_HEADS, MLA_QK_DIM)
    kv = (rms_norm(c_kv, kv_norm_w) @ ukv_w).reshape(bsz, seq, MLA_N_HEADS, MLA_NOPE_DIM + MLA_V_DIM)
    q_nope, q_rope = q[..., :MLA_NOPE_DIM], rope(q[..., MLA_NOPE_DIM:], positions)
    k_nope, v = kv[..., :MLA_NOPE_DIM], kv[..., MLA_NOPE_DIM:]
    k_rope = rope(k_r[:, :, None, :], positions)
    q_full = jnp.concatenate([q_nope, q_rope], axis=-1)
    k_full = jnp.concatenate([k_nope, jnp.broadcast_to(k_rope, (bsz, seq, MLA_N_HEADS, MLA_ROPE_DIM))], axis=-1)
    o = causal_block_attention(q_full, k_full, v, MLA_QK_DIM ** -0.5)
    o = o.reshape(bsz, seq, MLA_WIDTH) * jax.nn.silu(z)
    return o @ out_w

def fox_mixer(u, in_w, f_bias, out_w):
    bsz, seq, _ = u.shape
    proj = u @ in_w
    w = FOX_WIDTH
    q = proj[..., :w].reshape(bsz, seq, FOX_N_HEADS, FOX_HEAD_DIM)
    k = proj[..., w:2 * w].reshape(bsz, seq, FOX_N_HEADS, FOX_HEAD_DIM)
    v = proj[..., 2 * w:3 * w].reshape(bsz, seq, FOX_N_HEADS, FOX_HEAD_DIM)
    f_logit = proj[..., 3 * w:3 * w + FOX_N_HEADS]
    z = proj[..., 3 * w + FOX_N_HEADS:]
    log_f = jax.nn.log_sigmoid(f_logit.astype(jnp.float32) + f_bias.astype(jnp.float32))
    c = jnp.cumsum(log_f, axis=1)
    o = causal_block_attention(q, k, v, FOX_HEAD_DIM ** -0.5, log_forget_cum=c)
    o = o.reshape(bsz, seq, FOX_WIDTH) * jax.nn.silu(z)
    return o @ out_w

def dilated_mixer(u, positions, in_w, out_w):
    bsz, seq, _ = u.shape
    proj = u @ in_w
    w = DIL_WIDTH
    outs, lses = [], []
    for gi, (window, dilation) in enumerate(DIL_CONFIGS):
        base = 3 * w * gi
        q = proj[..., base:base + w].reshape(bsz, seq, DIL_N_HEADS, DIL_HEAD_DIM)
        k = proj[..., base + w:base + 2 * w].reshape(bsz, seq, DIL_N_HEADS, DIL_HEAD_DIM)
        v = proj[..., base + 2 * w:base + 3 * w].reshape(bsz, seq, DIL_N_HEADS, DIL_HEAD_DIM)
        o, lse = dilated_band_attention(partial_rope(q, positions), partial_rope(k, positions), v,
                                        dilation, window // dilation)
        outs.append(o)
        lses.append(lse)
    mix = jax.nn.softmax(jnp.stack(lses, axis=0), axis=0)
    o = jnp.sum(mix[..., None] * jnp.stack(outs, axis=0), axis=0)
    z = proj[..., 3 * w * len(DIL_CONFIGS):]
    o = o.reshape(bsz, seq, w).astype(u.dtype) * jax.nn.silu(z)
    return o @ out_w

def first_inputs(seed: int = 0) -> dict:
    key = jax.random.key(seed)
    ks = iter(jax.random.split(key, 32))
    f32 = jnp.float32

    def dense(shape, fan_in):
        return jax.random.normal(next(ks), shape, f32) * (fan_in ** -0.5)

    def gain(shape):
        return 1.0 + 0.02 * jax.random.normal(next(ks), shape, f32)

    x = jax.random.normal(next(ks), (BATCH, SEQ, D_MODEL), f32)
    norm_w = gain((DEPTH, D_MODEL))
    final_norm_w = gain((D_MODEL,))
    ssm_in_w = dense((N_SSM_LAYERS, D_MODEL, SSM_IN_COLS), D_MODEL)
    ssm_conv_w = dense((N_SSM_LAYERS, SSM_CONV, SSM_CONV_DIM), SSM_CONV)
    ssm_conv_b = 0.02 * jax.random.normal(next(ks), (N_SSM_LAYERS, SSM_CONV_DIM), f32)
    dt0 = jnp.exp(jax.random.uniform(next(ks), (N_SSM_LAYERS, SSM_N_HEADS), f32,
                                     minval=np.log(SSM_DT_MIN), maxval=np.log(SSM_DT_MAX)))
    ssm_dt_bias = dt0 + jnp.log(-jnp.expm1(-dt0))
    ssm_A_log = jnp.log(jax.random.uniform(next(ks), (N_SSM_LAYERS, SSM_N_HEADS), f32, minval=1.0, maxval=16.0))
    ssm_D = gain((N_SSM_LAYERS, SSM_N_HEADS))
    ssm_norm_w = gain((N_SSM_LAYERS, SSM_D_INNER))
    ssm_out_w = dense((N_SSM_LAYERS, SSM_D_INNER, D_MODEL), SSM_D_INNER)
    mla_in_w = dense((N_MLA_LAYERS, D_MODEL, MLA_IN_COLS), D_MODEL)
    mla_q_norm_w = gain((N_MLA_LAYERS, MLA_Q_LORA))
    mla_kv_norm_w = gain((N_MLA_LAYERS, MLA_KV_LORA))
    mla_uq_w = dense((N_MLA_LAYERS, MLA_Q_LORA, MLA_N_HEADS * MLA_QK_DIM), MLA_Q_LORA)
    mla_ukv_w = dense((N_MLA_LAYERS, MLA_KV_LORA, MLA_N_HEADS * (MLA_NOPE_DIM + MLA_V_DIM)), MLA_KV_LORA)
    mla_out_w = dense((N_MLA_LAYERS, MLA_WIDTH, D_MODEL), MLA_WIDTH)
    fox_in_w = dense((N_FOX_LAYERS, D_MODEL, FOX_IN_COLS), D_MODEL)
    fox_f_bias = FOX_F_BIAS_MEAN + 0.5 * jax.random.normal(next(ks), (N_FOX_LAYERS, FOX_N_HEADS), f32)
    fox_out_w = dense((N_FOX_LAYERS, FOX_WIDTH, D_MODEL), FOX_WIDTH)
    dil_in_w = dense((N_DIL_LAYERS, D_MODEL, DIL_IN_COLS), D_MODEL)
    dil_out_w = dense((N_DIL_LAYERS, DIL_WIDTH, D_MODEL), DIL_WIDTH)
    return {'x': x, 'norm_w': norm_w, 'final_norm_w': final_norm_w,
            'ssm_in_w': ssm_in_w, 'ssm_conv_w': ssm_conv_w, 'ssm_conv_b': ssm_conv_b,
            'ssm_dt_bias': ssm_dt_bias, 'ssm_A_log': ssm_A_log, 'ssm_D': ssm_D,
            'ssm_norm_w': ssm_norm_w, 'ssm_out_w': ssm_out_w,
            'mla_in_w': mla_in_w, 'mla_q_norm_w': mla_q_norm_w, 'mla_kv_norm_w': mla_kv_norm_w,
            'mla_uq_w': mla_uq_w, 'mla_ukv_w': mla_ukv_w, 'mla_out_w': mla_out_w,
            'fox_in_w': fox_in_w, 'fox_f_bias': fox_f_bias, 'fox_out_w': fox_out_w,
            'dil_in_w': dil_in_w, 'dil_out_w': dil_out_w}

def first_block(x, norm_w, final_norm_w, ssm_in_w, ssm_conv_w, ssm_conv_b, ssm_dt_bias, ssm_A_log, ssm_D,
              ssm_norm_w, ssm_out_w, mla_in_w, mla_q_norm_w, mla_kv_norm_w, mla_uq_w, mla_ukv_w, mla_out_w,
              fox_in_w, fox_f_bias, fox_out_w, dil_in_w, dil_out_w):
    positions = jnp.arange(x.shape[1])
    h = x
    for i in range(DEPTH):
        kind, j = i % NUM_MIXERS, i // NUM_MIXERS
        u = rms_norm(h, norm_w[i])
        if kind == 0:
            y = ssd_mixer(u, ssm_in_w[j], ssm_conv_w[j], ssm_conv_b[j], ssm_dt_bias[j], ssm_A_log[j],
                          ssm_D[j], ssm_norm_w[j], ssm_out_w[j])
        elif kind == 1:
            y = mla_mixer(u, positions, mla_in_w[j], mla_q_norm_w[j], mla_kv_norm_w[j], mla_uq_w[j],
                          mla_ukv_w[j], mla_out_w[j])
        elif kind == 2:
            y = fox_mixer(u, fox_in_w[j], fox_f_bias[j], fox_out_w[j])
        else:
            y = dilated_mixer(u, positions, dil_in_w[j], dil_out_w[j])
        h = h + y.astype(h.dtype)
    return rms_norm(h, final_norm_w)


DEPTH_2 = 1

PLE_DIM = 256
NSA_HEADS = 8
NSA_GROUPS = 2
NSA_HPG = NSA_HEADS // NSA_GROUPS
HEAD_DIM = 64
CMP_LEN = 32
CMP_STRIDE = 16
CMP_HIDDEN = 256
SEL_LEN = 64
SEL_TOP = 16
WINDOW = 512
Q_BLOCK = 128
FORCE_SCORE = 1e4
CONV_CH = 512
CONV_WIDTH = 31
D_FF = 2816
FFN_CONV_WIDTH = 3
EPS = 1e-6
NEG = -1e30

NSA_Q = NSA_HEADS * HEAD_DIM
NSA_KV = 3 * 2 * NSA_GROUPS * HEAD_DIM
NSA_GATE = 3 * NSA_HEADS
CONV_IN = 2 * CONV_CH
MERGE = 2 * D_MODEL
N_IN = NSA_Q + NSA_KV + NSA_GATE + CONV_IN + MERGE
IN_SPLITS = (NSA_Q, NSA_Q + NSA_KV, NSA_Q + NSA_KV + NSA_GATE, NSA_Q + NSA_KV + NSA_GATE + CONV_IN)


def rmsnorm(x, g):
    xf = x.astype(jnp.float32)
    y = xf * lax.rsqrt(jnp.mean(xf * xf, axis=-1, keepdims=True) + EPS)
    return (y * g.astype(jnp.float32)).astype(x.dtype)

def layernorm(x, g, b):
    xf = x.astype(jnp.float32)
    mu = jnp.mean(xf, axis=-1, keepdims=True)
    xc = xf - mu
    y = xc * lax.rsqrt(jnp.mean(xc * xc, axis=-1, keepdims=True) + EPS)
    return (y * g.astype(jnp.float32) + b.astype(jnp.float32)).astype(x.dtype)

def causal_dwconv(x, w, b):
    k = w.shape[0]
    c = x.shape[-1]
    y = lax.conv_general_dilated(x, w[:, None, :].astype(x.dtype), window_strides=(1,),
                                 padding=((k - 1, 0),), dimension_numbers=('NWC', 'WIO', 'NWC'),
                                 feature_group_count=c)
    return y + b

def masked_softmax(logits, mask):
    logits = jnp.where(mask, logits.astype(jnp.float32), NEG)
    return jnp.where(mask, jax.nn.softmax(logits, axis=-1), 0.0)

def compress(kv, pos, w1, w2):
    s = kv.shape[2]
    n_cmp = (s - CMP_LEN) // CMP_STRIDE + 1
    idx = np.arange(n_cmp)[:, None] * CMP_STRIDE + np.arange(CMP_LEN)[None, :]
    blocks = kv[:, :, idx] + pos
    flat = blocks.reshape(blocks.shape[0], blocks.shape[1], n_cmp, CMP_LEN * HEAD_DIM)
    return jax.nn.gelu(flat @ w1) @ w2

def cmp_to_sel_matrix(n_cmp, n_sel):
    c0 = np.arange(n_cmp) * CMP_STRIDE
    j0 = np.arange(n_sel) * SEL_LEN
    lo = np.maximum(c0[:, None], j0[None, :])
    hi = np.minimum(c0[:, None] + CMP_LEN, j0[None, :] + SEL_LEN)
    return (np.maximum(hi - lo, 0) / CMP_LEN).astype(np.float32)

def nsa_attention(q, kc, vc, ks, vs, kw, vw):
    b, g, hg, s, dh = q.shape
    scale = dh ** -0.5
    n_cmp = kc.shape[2]
    n_sel = s // SEL_LEN
    top = min(SEL_TOP, n_sel)
    cmp_end = jnp.arange(n_cmp) * CMP_STRIDE + CMP_LEN - 1
    sel_map = jnp.asarray(cmp_to_sel_matrix(n_cmp, n_sel))
    ks_blk = ks.reshape(b, g, n_sel, SEL_LEN, dh)
    vs_blk = vs.reshape(b, g, n_sel, SEL_LEN, dh)
    kw_pad = jnp.pad(kw, ((0, 0), (0, 0), (WINDOW, 0), (0, 0)))
    vw_pad = jnp.pad(vw, ((0, 0), (0, 0), (WINDOW, 0), (0, 0)))
    bi = jnp.arange(b)[:, None, None, None]
    gi = jnp.arange(g)[None, :, None, None]
    jsel = jnp.arange(n_sel)

    def query_block(qb_idx):
        t0 = qb_idx * Q_BLOCK
        qb = lax.dynamic_slice_in_dim(q, t0, Q_BLOCK, axis=3) * scale
        t = t0 + jnp.arange(Q_BLOCK)
        lc = jnp.einsum('bghqd,bgcd->bghqc', qb, kc)
        pc = masked_softmax(lc, cmp_end[None, :] <= t[:, None])
        o_c = jnp.einsum('bghqc,bgcd->bghqd', pc.astype(vc.dtype), vc)
        imp = jnp.einsum('bghqc,cj->bgqj', pc, sel_map)
        cur = (t // SEL_LEN)[:, None]
        forced = (jsel[None, :] == 0) | (jsel[None, :] == cur) | (jsel[None, :] == cur - 1)
        valid = jsel[None, :] <= cur
        imp = jnp.where(valid, jnp.where(forced, FORCE_SCORE, imp), NEG)
        _, sel_idx = lax.top_k(imp, top)
        kg = ks_blk[bi, gi, sel_idx]
        vg = vs_blk[bi, gi, sel_idx]
        ls = jnp.einsum('bghqd,bgqnkd->bghqnk', qb, kg).reshape(b, g, hg, Q_BLOCK, top * SEL_LEN)
        kpos = sel_idx[..., None] * SEL_LEN + jnp.arange(SEL_LEN)
        ms = (kpos <= t[None, None, :, None, None]).reshape(b, g, 1, Q_BLOCK, top * SEL_LEN)
        ps = masked_softmax(ls, ms).reshape(b, g, hg, Q_BLOCK, top, SEL_LEN)
        o_s = jnp.einsum('bghqnk,bgqnkd->bghqd', ps.astype(vg.dtype), vg)
        kwb = lax.dynamic_slice_in_dim(kw_pad, t0, WINDOW + Q_BLOCK, axis=2)
        vwb = lax.dynamic_slice_in_dim(vw_pad, t0, WINDOW + Q_BLOCK, axis=2)
        spos = t0 - WINDOW + jnp.arange(WINDOW + Q_BLOCK)
        dist = t[:, None] - spos[None, :]
        mw = (dist >= 0) & (dist < WINDOW) & (spos[None, :] >= 0)
        lw = jnp.einsum('bghqd,bgkd->bghqk', qb, kwb)
        pw = masked_softmax(lw, mw)
        o_w = jnp.einsum('bghqk,bgkd->bghqd', pw.astype(vwb.dtype), vwb)
        return (o_c, o_s, o_w)

    o_c, o_s, o_w = lax.map(query_block, jnp.arange(s // Q_BLOCK))

    def unblock(o):
        return jnp.transpose(o, (1, 2, 3, 0, 4, 5)).reshape(b, g, hg, s, dh)

    return (unblock(o_c), unblock(o_s), unblock(o_w))

def second_inputs(seed: int = 0) -> dict:
    key = jax.random.key(seed)
    ks = jax.random.split(key, 32)
    f32 = jnp.float32

    def nrm(k, shape, fan_in):
        return jax.random.normal(k, shape, f32) * (fan_in ** -0.5)

    def gain(k, shape):
        return 1.0 + 0.05 * jax.random.normal(k, shape, f32)

    def small(k, shape):
        return 0.02 * jax.random.normal(k, shape, f32)

    L = DEPTH_2
    return {
        "x": jax.random.normal(ks[0], (BATCH, SEQ, D_MODEL), f32),
        "p": jax.random.normal(ks[1], (DEPTH_2, BATCH, SEQ, PLE_DIM), f32),
        "g_mix": gain(ks[2], (L, D_MODEL)),
        "w_in": nrm(ks[3], (L, D_MODEL, N_IN), D_MODEL),
        "cmp_pos_k": small(ks[4], (L, CMP_LEN, HEAD_DIM)),
        "cmp_pos_v": small(ks[5], (L, CMP_LEN, HEAD_DIM)),
        "w_cmp_k1": nrm(ks[6], (L, CMP_LEN * HEAD_DIM, CMP_HIDDEN), CMP_LEN * HEAD_DIM),
        "w_cmp_k2": nrm(ks[7], (L, CMP_HIDDEN, HEAD_DIM), CMP_HIDDEN),
        "w_cmp_v1": nrm(ks[8], (L, CMP_LEN * HEAD_DIM, CMP_HIDDEN), CMP_LEN * HEAD_DIM),
        "w_cmp_v2": nrm(ks[9], (L, CMP_HIDDEN, HEAD_DIM), CMP_HIDDEN),
        "w_o_nsa": nrm(ks[10], (L, NSA_Q, D_MODEL), NSA_Q),
        "conv_w": nrm(ks[11], (L, CONV_WIDTH, CONV_CH), CONV_WIDTH),
        "conv_b": small(ks[12], (L, CONV_CH)),
        "conv_ln_g": gain(ks[13], (L, CONV_CH)),
        "conv_ln_b": small(ks[14], (L, CONV_CH)),
        "w_conv_out": nrm(ks[15], (L, CONV_CH, D_MODEL), CONV_CH),
        "b_conv_out": small(ks[16], (L, D_MODEL)),
        "w_out": nrm(ks[17], (L, D_MODEL, D_MODEL), D_MODEL),
        "g_ffn": gain(ks[18], (L, D_MODEL)),
        "w_up": nrm(ks[19], (L, D_MODEL, 2 * D_FF), D_MODEL),
        "ffn_conv_w": nrm(ks[20], (L, FFN_CONV_WIDTH, 2 * D_FF), FFN_CONV_WIDTH),
        "ffn_conv_b": small(ks[21], (L, 2 * D_FF)),
        "w_down": nrm(ks[22], (L, D_FF, D_MODEL), D_FF),
        "g_ple": gain(ks[23], (L, D_MODEL)),
        "w_ple_gate": nrm(ks[24], (L, D_MODEL, D_MODEL), D_MODEL),
        "w_ple": nrm(ks[25], (L, PLE_DIM, D_MODEL), PLE_DIM),
        "g_final": gain(ks[26], (D_MODEL,)),
    }

def second_block(x, p, g_mix, w_in, cmp_pos_k, cmp_pos_v, w_cmp_k1, w_cmp_k2, w_cmp_v1, w_cmp_v2,
              w_o_nsa, conv_w, conv_b, conv_ln_g, conv_ln_b, w_conv_out, b_conv_out, w_out,
              g_ffn, w_up, ffn_conv_w, ffn_conv_b, w_down, g_ple, w_ple_gate, w_ple, g_final):
    b, s, _ = x.shape
    h = x
    for i in range(DEPTH_2):
        u = rmsnorm(h, g_mix[i])
        z = u @ w_in[i]
        zq, zkv, zg, zc, zm = jnp.split(z, IN_SPLITS, axis=-1)

        q = jnp.transpose(zq.reshape(b, s, NSA_GROUPS, NSA_HPG, HEAD_DIM), (0, 2, 3, 1, 4))
        kv = jnp.transpose(zkv.reshape(b, s, 6, NSA_GROUPS, HEAD_DIM), (2, 0, 3, 1, 4))
        kc = compress(kv[0], cmp_pos_k[i], w_cmp_k1[i], w_cmp_k2[i])
        vc = compress(kv[1], cmp_pos_v[i], w_cmp_v1[i], w_cmp_v2[i])
        o_c, o_s, o_w = nsa_attention(q, kc, vc, kv[2], kv[3], kv[4], kv[5])
        gates = jnp.transpose(jax.nn.sigmoid(zg.reshape(b, s, 3, NSA_GROUPS, NSA_HPG)),
                              (2, 0, 3, 4, 1))[..., None]
        o = gates[0] * o_c + gates[1] * o_s + gates[2] * o_w
        o = jnp.transpose(o, (0, 3, 1, 2, 4)).reshape(b, s, NSA_Q)
        y_a = o @ w_o_nsa[i]

        c_val, c_gate = jnp.split(zc, 2, axis=-1)
        c = c_val * jax.nn.sigmoid(c_gate)
        c = causal_dwconv(c, conv_w[i], conv_b[i])
        c = jax.nn.silu(layernorm(c, conv_ln_g[i], conv_ln_b[i]))
        y_b = c @ w_conv_out[i] + b_conv_out[i]

        ga, gb = jnp.split(jax.nn.sigmoid(zm), 2, axis=-1)
        h = h + (ga * y_a + gb * y_b) @ w_out[i]

        v = rmsnorm(h, g_ffn[i]) @ w_up[i]
        v = causal_dwconv(v, ffn_conv_w[i], ffn_conv_b[i])
        v_gate, v_val = jnp.split(v, 2, axis=-1)
        h = h + (jax.nn.gelu(v_gate) * v_val) @ w_down[i]

        gate = jax.nn.sigmoid(rmsnorm(h, g_ple[i]) @ w_ple_gate[i])
        h = h + gate * (p[i] @ w_ple[i])
    return rmsnorm(h, g_final)


def setup_inputs(seed=0):
    out = dict(first_inputs(seed))
    for name, value in second_inputs(seed + 1).items():
        if name != "x":
            out[name + "_2"] = value
    return out


def reference(
    x, norm_w, final_norm_w, ssm_in_w, ssm_conv_w, ssm_conv_b, ssm_dt_bias, ssm_A_log, ssm_D,
    ssm_norm_w, ssm_out_w, mla_in_w, mla_q_norm_w, mla_kv_norm_w, mla_uq_w, mla_ukv_w,
    mla_out_w, fox_in_w, fox_f_bias, fox_out_w, dil_in_w, dil_out_w, p_2, g_mix_2, w_in_2,
    cmp_pos_k_2, cmp_pos_v_2, w_cmp_k1_2, w_cmp_k2_2, w_cmp_v1_2, w_cmp_v2_2, w_o_nsa_2,
    conv_w_2, conv_b_2, conv_ln_g_2, conv_ln_b_2, w_conv_out_2, b_conv_out_2, w_out_2, g_ffn_2,
    w_up_2, ffn_conv_w_2, ffn_conv_b_2, w_down_2, g_ple_2, w_ple_gate_2, w_ple_2, g_final_2,
):
    x = first_block(
        x, norm_w, final_norm_w, ssm_in_w, ssm_conv_w, ssm_conv_b, ssm_dt_bias, ssm_A_log,
        ssm_D, ssm_norm_w, ssm_out_w, mla_in_w, mla_q_norm_w, mla_kv_norm_w, mla_uq_w,
        mla_ukv_w, mla_out_w, fox_in_w, fox_f_bias, fox_out_w, dil_in_w, dil_out_w,
    )
    return second_block(
        x, p_2, g_mix_2, w_in_2, cmp_pos_k_2, cmp_pos_v_2, w_cmp_k1_2, w_cmp_k2_2, w_cmp_v1_2,
        w_cmp_v2_2, w_o_nsa_2, conv_w_2, conv_b_2, conv_ln_g_2, conv_ln_b_2, w_conv_out_2,
        b_conv_out_2, w_out_2, g_ffn_2, w_up_2, ffn_conv_w_2, ffn_conv_b_2, w_down_2, g_ple_2,
        w_ple_gate_2, w_ple_2, g_final_2,
    )


_drawn_inputs = setup_inputs


def setup_inputs(seed=0):
    import zlib

    import numpy as np

    out = dict(_drawn_inputs(seed))
    spreads = {}
    factors = {'ssm_D': 5.974,
     'ssm_norm_w': 3.597,
     'mla_q_norm_w': 8.0,
     'mla_kv_norm_w': 8.0,
     'cmp_pos_k_2': 64.0,
     'cmp_pos_v_2': 23.49,
     'conv_b_2': 3.808,
     'conv_ln_g_2': 2.893,
     'conv_ln_b_2': 8.0,
     'b_conv_out_2': 4.987,
     'ffn_conv_b_2': 4.095,
     'g_ple_2': 21.632}
    for name, (base, spread) in spreads.items():
        noise = np.random.default_rng([zlib.crc32(name.encode()), seed]).standard_normal(out[name].shape)
        drawn = base * np.exp(spread * noise) if base else spread * noise
        out[name] = __import__('jax').numpy.asarray(drawn.astype(out[name].dtype))
    for name, factor in factors.items():
        out[name] = (out[name] * factor).astype(out[name].dtype)
    return out
```

```python
from contextlib import ExitStack

import numpy as np

import concourse.bass as bass
from concourse import mybir

P = 128
T = 256
TB = T // P
DM = 1024
KD = DM // P
EPS = 1e-6
SSM_DI, SSM_H, SSM_G, SSM_N = 2048, 32, 8, 128
SSM_PAIRS = SSM_DI // P
SSM_CT = (SSM_DI + 2 * SSM_G * SSM_N) // P
SSM_TAPS = 4
MLA_H, MLA_Q, MLA_KV, MLA_R, MLA_D = 16, 384, 256, 64, 128
NSA_G, NSA_J, NSA_D = 2, 4, 64
CMP_LEN, CMP_STRIDE, CMP_HID = 32, 16, 256
N_CMP = (T - CMP_LEN) // CMP_STRIDE + 1
CPAD = 32
CONV_CT, CONV_TAPS = 4, 31
FF = 2816
KF = FF // P
FF_TAPS = 3
NEG = -1e30

BLK = 8
SLAB = BLK * P
RAW_RING, PART_RING = 6, 6
PROJ_BANKS = 3


def weight_jobs():
    r = np.arange
    jobs = []

    def add(name, array, cols, consumer, kind="F", rows=None):
        jobs.append((name, array, np.asarray(cols), rows, kind, consumer))

    pad = lambda cols: np.concatenate([cols, np.full(P - len(cols), -1)])
    zero = SSM_DI
    add("dt", "ssm_in_w", pad(r(SSM_H) + 2 * SSM_DI + 2 * SSM_G * SSM_N), "dve")
    for c in range(SSM_CT):
        ch = conv_tile(c)
        add(f"xbc{c}", "ssm_in_w", zero + ch * P + r(P), "act")
    for j in range(SSM_PAIRS):
        add(f"sz{j}", "ssm_in_w", j * P + r(P), "dve")
    for n in range(KD):
        add(f"so{n}", "ssm_out_w", n * P + r(P), "dve")
    for n in range(3):
        add(f"cq{n}", "mla_in_w", n * P + r(P), "act")
    for n in range(2):
        add(f"ckv{n}", "mla_in_w", MLA_Q + n * P + r(P), "act")
    kr = MLA_Q + MLA_KV + r(MLA_R)
    add("kr", "mla_in_w", np.concatenate([kr, kr]), "act")
    for n in range(4):
        cols = np.concatenate([(4 * n + i) * 2 * P + P + r(P) for i in range(4)])
        add(f"v{n}", "mla_ukv_w", cols, "act", "V")
    for i in range(MLA_H // 2):
        cols = np.concatenate([(2 * i + e) * 192 + P + r(MLA_R) for e in range(2)])
        add(f"qr{i}", "mla_uq_w", cols, "act")
    zc = MLA_Q + MLA_KV + MLA_R

    def head(h):
        add(f"kn{h}", "mla_ukv_w", h * 2 * P + r(P), "act")
        add(f"qn{h}", "mla_uq_w", h * 192 + r(P), "act")

    head(0)
    for h in range(MLA_H):
        if h + 1 < MLA_H:
            head(h + 1)
        add(f"mz{h}", "mla_in_w", zc + h * P + r(P), "dve")
    for n in range(KD):
        add(f"mo{n}", "mla_out_w", n * P + r(P), "dve")
    conv0 = 512 + 768 + 24
    merge0 = conv0 + 1024
    for i in range(CONV_CT):
        add(f"cg{i}", "w_in_2", conv0 + 512 + i * P + r(P), "act")
        add(f"cv{i}", "w_in_2", conv0 + i * P + r(P), "dve")
    for c in range(2):
        add(f"kvc{c}", "w_in_2", 512 + c * P + r(P), "act")
    for j in range(NSA_J):
        cols = np.concatenate([g * 256 + j * 64 + r(64) for g in range(2)])
        add(f"nq{j}", "w_in_2", cols, "act")
    add("ks", "w_in_2", 512 + 2 * P + r(P), "act")
    add("kw", "w_in_2", 512 + 4 * P + r(P), "act")
    add("vsw", "w_in_2", np.concatenate([512 + 3 * P + r(P), 512 + 5 * P + r(P)]), "act", "V")
    add("gates", "w_in_2", pad(512 + 768 + r(24)), "act", "V")
    for n in range(4):
        add(f"mg{n}", "w_in_2", merge0 + n * P + r(P), "act")
    for s in "kv":
        for n in range(2):
            add(f"h{s}{n}", f"w_cmp_{s}1_2", n * P + r(P), "act")
    for n in range(4, 8):
        add(f"mg{n}", "w_in_2", merge0 + n * P + r(P), "act")
    for s in "kv":
        add(f"c{s}", f"w_cmp_{s}2_2", np.concatenate([r(64), r(64)]), "act")
    for n in range(8, 16):
        add(f"mg{n}", "w_in_2", merge0 + n * P + r(P), "act")
    for n in range(KD):
        add(f"yb{n}", "w_conv_out_2", n * P + r(P), "dve")
    rows = np.concatenate([g * 256 + j * 64 + r(64) for j in range(4) for g in range(2)])
    for n in range(KD):
        add(f"ya{n}", "w_o_nsa_2", n * P + r(P), "dve", rows=rows)
    for n in range(KD):
        add(f"wo{n}", "w_out_2", n * P + r(P), "dve")
    for i in range(KF):
        add(f"fg{i}", "w_up_2", i * P + r(P), "act")
        add(f"fv{i}", "w_up_2", FF + i * P + r(P), "act")
    for n in range(KD):
        add(f"fd{n}", "w_down_2", n * P + r(P), "dve")
    for n in range(KD):
        add(f"pg{n}", "w_ple_gate_2", n * P + r(P), "act")
        add(f"pw{n}", "w_ple_2", n * P + r(P), "dve")
    return jobs


def conv_tile(c):
    return c + SSM_PAIRS if c < 16 else c - 16


K_OF = {"ssm_in_w": 8, "ssm_out_w": 16, "mla_in_w": 8, "mla_uq_w": 3, "mla_ukv_w": 2, "mla_out_w": 16,
        "w_in_2": 8, "w_cmp_k1_2": 16, "w_cmp_v1_2": 16, "w_cmp_k2_2": 2, "w_cmp_v2_2": 2, "w_conv_out_2": 4,
        "w_o_nsa_2": 4, "w_out_2": 8, "w_up_2": 8, "w_down_2": KF, "w_ple_gate_2": 8, "w_ple_2": 2}


class Job:

    def __init__(self, name, kind, kt, wide, block, out, consumer, used):
        self.name, self.kind, self.kt, self.wide, self.block, self.out = name, kind, kt, wide, block, out
        self.consumer, self.used = consumer, used
        self.n_out = 1 if kind == "F" else TB
        self.blocks = kt * wide
        self.slab0, self.slab1 = block // BLK, (block + self.blocks - 1) // BLK


def plan():
    jobs, block, out = {}, 0, 0
    used = {"act": 0, "dve": 0}
    freed = []
    done_with = {}
    for name, array, cols, _, kind, consumer in weight_jobs():
        kt, wide = K_OF[array], len(cols) // P
        if wide > 1 and block % wide:
            block += wide - block % wide
        j = jobs[name] = Job(name, kind, kt, wide, block, out, consumer, used[consumer])
        for _ in range(j.n_out):
            used[consumer] += 1
            freed.append((consumer, used[consumer]))
        block += j.blocks
        out += j.n_out
        for s in range(j.slab0, j.slab1 + 1):
            done_with[s] = out
    return jobs, freed, done_with, -(-block // BLK)


def vector_columns():
    at, c = {}, 0
    for name, n in [("norm0", 8), ("norm1", 8), ("final1", 8), ("sconv_w", SSM_CT * SSM_TAPS), ("sconv_b", SSM_CT),
                    ("ssm_d", 16), ("ssm_nw", 16), ("dt_bias", 1), ("a_log", 1), ("qnorm", 3), ("kvnorm", 2),
                    ("g_mix", 8), ("pos_k", 16), ("pos_v", 16), ("conv_w", CONV_CT * CONV_TAPS), ("conv_b", 4),
                    ("ln_g", 4), ("ln_b", 4), ("b_co", 8), ("g_ffn", 8), ("fconv_w", 2 * KF * FF_TAPS),
                    ("fconv_b", 2 * KF), ("g_ple", 8), ("g_final", 8)]:
        at[name] = c
        c += n
    return at, c


CONST_COLS = {"ident": 0, "swap": 128, "mask_s": 256, "mask_t": 384, "cmp_add": 768, "cmp_ok": 896,
              "cos": 1024, "sin": 1280}
N_CONST = 1536


def build(nc, slabs_dram, vec_dram, const_dram, x_dram, p_dram, out_dram):
    f32, f32r, bf16 = mybir.dt.float32, mybir.dt.float32r, mybir.dt.bfloat16
    ALU, ACT, AX = mybir.AluOpType, mybir.ActivationFunctionType, mybir.AxisListType
    jobs, freed, done_with, n_slabs = plan()
    VC, n_vec = vector_columns()
    ctx = ExitStack()
    with ctx:
        def sb(name, shape, dt=f32):
            return ctx.enter_context(nc.sbuf_tensor(name, shape, dt))

        raw = sb("raw", [P, RAW_RING, SLAB])
        wh = sb("wh", [P, PART_RING, SLAB], f32r)
        wl = sb("wl", [P, PART_RING, SLAB], f32r)
        h = sb("h", [P, KD, T])
        sq = sb("sq", [P, KD, T])
        vec = sb("vec", [P, n_vec])
        cst = sb("cst", [P, N_CONST])
        ident_b = sb("ident_b", [P, P], bf16)
        mask_s = sb("mask_s", [P, P], bf16)
        mask_t = sb("mask_t", [P, 3 * P], bf16)
        cmp_add = sb("cmp_add", [P, P], bf16)
        ones = sb("ones", [P, P])
        eps = sb("eps", [P, 1])
        lnb = sb("lnb", [P, T])
        rstd = sb("rstd", [P, T])
        ident = cst[:, 0:128]
        swap = cst[:, 128:256]
        cmp_ok = cst[:, 896:1024]
        cos, sin = cst[:, 1024:1280], cst[:, 1280:1536]

        def v(name, i=0, rows=P):
            return vec[0:rows, VC[name] + i:VC[name] + i + 1]

        arena_kb = 103
        arena = sb("arena", [P, arena_kb * 256])
        base = arena_base(nc, arena_kb)
        cursor = [0]

        def phase(start=0):
            cursor[0] = start

        def ar(name, shape, dt=f32):
            n = int(np.prod(shape)) * 4
            t = nc.alloc_sbuf_tensor_at(name, [P] + list(shape), dt, offset=base + cursor[0])
            cursor[0] += -(-n // 32) * 32
            assert cursor[0] <= arena_kb * 1024, (name, cursor[0])
            return t

        phase()
        uh, ul = ar("uh", [KD, T], f32r), ar("ul", [KD, T], f32r)
        after_u = cursor[0]
        ynh, ynl = ar("ynh", [16, T], f32r), ar("ynl", [16, T], f32r)
        xs, bT, cT = ar("xs", [16, T]), ar("bT", [8, T]), ar("cT", [8, T])
        acr, dtT = ar("acr", [3 * P]), ar("dtT", [T])
        dtn, nacn = ar("dtn", [TB, SSM_H]), ar("nacn", [TB, SSM_H])
        expa = ar("expa", [1])
        xdt = ar("xdt", [2, TB, 2, 64])
        gb = ar("gb", [4, T])
        szb = ar("szb", [2, T])
        zb = ar("zb", [T])
        mark = cursor[0]
        sraw = ar("sraw", [4, T + SSM_TAPS - 1])
        scv = ar("scv", [2, T])
        sp = ar("sp", [4, T])
        cursor[0] = mark
        eb, mb, cbs = ar("eb", [2, 3 * P]), ar("mb", [2, 3 * P]), ar("cbs", [2, 3 * P])
        yt = ar("yt", [T])

        phase(after_u)
        ogh, ogl = ar("ogh", [16, T], f32r), ar("ogl", [16, T], f32r)
        vn = ar("vn", [TB, MLA_H * P])
        qr, kr = ar("qr", [8, T]), ar("kr", [T])
        kn, qn = ar("kn", [2, T]), ar("qn", [2, T])
        cqh, cql = ar("cqh", [3, T], f32r), ar("cql", [3, T], f32r)
        ckh, ckl = ar("ckh", [2, T], f32r), ar("ckl", [2, T], f32r)
        mx, nm, rs, rr = ar("mx", [2, 2]), ar("nm", [2, 2]), ar("rs", [2, 2]), ar("rr", [2, 2])
        mzb, mze = ar("mzb", [T]), ar("mze", [T])
        ogt = ar("ogt", [2, T])
        mark = cursor[0]
        cqr, ckr = ar("cqr", [3, T]), ar("ckr", [2, T])
        rx, r1, r2 = ar("rx", [2, T]), ar("r1", [T]), ar("r2", [T])
        cursor[0] = mark
        pn, pT = ar("pn", [2, 3 * P]), ar("pT", [2, 3 * P])

        phase(after_u)
        cpad = ar("cpad", [CONV_CT, T + CONV_TAPS - 1])
        ccv = ar("ccv", [CONV_CT, T])
        csg = ar("csg", [2, T])
        nq = ar("nq", [NSA_J, T])
        ksT, kwT = ar("ksT", [T]), ar("kwT", [T])
        vsw = ar("vsw", [TB, 2 * P])
        gates = ar("gates", [TB, 24])
        gm = ar("gm", [16, T])
        cnh, cnl = ar("cnh", [4, T], f32r), ar("cnl", [4, T], f32r)
        kcT, vcT = ar("kcT", [64]), ar("vcT", [P])
        vc = ar("vc", [TB, P])
        nmx, nnm, nrs, nrr = ar("nmx", [2, 2]), ar("nnm", [2, 2]), ar("nrs", [2, 2]), ar("nrr", [2, 2])
        cmx, crs, crr = ar("cmx", [4]), ar("crs", [4]), ar("crr", [4])
        csc, cpn, cpT = ar("csc", [P]), ar("cpn", [P]), ar("cpT", [P])
        yat = ar("yat", [T])
        mark = cursor[0]
        ce = ar("ce", [2, NSA_G, T])
        cx = ar("cx", [2, 16, 64])
        cxh, cxl = ar("cxh", [2, 16, 64], f32r), ar("cxl", [2, 16, 64], f32r)
        hg = ar("hg", [2, 2, 64])
        hgh, hgl = ar("hgh", [2, 2, 64], f32r), ar("hgl", [2, 2, 64], f32r)
        cursor[0] = mark
        mt = ar("mt", [KD, T])
        onh, onl = ar("onh", [4, T], f32r), ar("onl", [4, T], f32r)
        npn, npT = ar("npn", [2, 3 * P]), ar("npT", [2, 3 * P])
        phase()
        mh, ml = ar("mh", [KD, T], f32r), ar("ml", [KD, T], f32r)

        phase(after_u)
        ffh, ffl = ar("ffh", [KF, T], f32r), ar("ffl", [KF, T], f32r)
        fraw = ar("fraw", [4, T + FF_TAPS - 1])
        fcv = ar("fcv", [4, T])
        fge, fgt = ar("fge", [2, T]), ar("fgt", [2, T])
        pin = ar("pin", [2, T])
        ph, pl = ar("ph", [2, T], f32r), ar("pl", [2, T], f32r)
        psg, pt = ar("psg", [2, T]), ar("pt", [T])
        outb = ar("outb", [KD, T])

        psum = [ctx.enter_context(nc.psum_tensor(f"ps{i}", [P, 512], f32)) for i in range(8)]
        PS_TR, PS_S, PS_Y, PS_M = psum[3], [psum[4], psum[5]], psum[6], psum[7]

        sems = {}

        def sem(name):
            if name not in sems:
                sems[name] = ctx.enter_context(nc.semaphore(name))
            return sems[name]

        def wait(eng, name, value):
            if value > 0:
                eng.wait_ge(sem(name), value)

        class Norm:
            count = tiles = plain = parts = chunks = 0

            def __init__(self, src, kt, width, gain, hi=None, lo=None, out=None, sqb=None, ready=()):
                self.src, self.kt, self.width, self.gain = src, kt, width, gain
                self.hi, self.lo, self.out, self.ready = hi, lo, out, ready
                self.sqb = sqb or (lambda k: sq[:, k, :])
                self.i, self.t0, self.p0 = Norm.count, Norm.tiles, Norm.parts
                Norm.count += 1
                Norm.tiles += kt
                Norm.parts += 0 if out else kt

        tile_of = lambda t: (lambda k: t[:, k, :])
        n_ssm = Norm(tile_of(h), 8, DM, "norm0", tile_of(uh), tile_of(ul), ready=[("x_in", 16)])
        n_grp = []
        for g in range(SSM_G):
            n_grp.append(Norm((lambda k, g=g: gb[:, (2 * g + k) % 4, :]), 2, 256, ("ssm_nw", 2 * g),
                              (lambda k, g=g: ynh[:, 2 * g + k, :]), (lambda k, g=g: ynl[:, 2 * g + k, :]),
                              sqb=(lambda k, g=g: sq[:, (2 * g + k) % 4, :])))
        n_mla = Norm(tile_of(h), 8, DM, "norm1", tile_of(uh), tile_of(ul),
                     ready=[("dve_evac", freed[jobs["so7"].out][1])])
        n_kv = Norm(tile_of(ckr), 2, MLA_KV, "kvnorm", tile_of(ckh), tile_of(ckl),
                    sqb=lambda k: sq[:, 4 + k, :], ready=[("act_evac", freed[jobs["ckv1"].out][1])])
        n_q = Norm(tile_of(cqr), 3, MLA_Q, "qnorm", tile_of(cqh), tile_of(cql),
                   ready=[("act_evac", freed[jobs["cq2"].out][1])])
        n_fin1 = Norm(tile_of(h), 8, DM, "final1", out=tile_of(h), ready=[("dve_evac", freed[jobs["mo7"].out][1])])
        n_mix = Norm(tile_of(h), 8, DM, "g_mix", tile_of(uh), tile_of(ul),
                     ready=[("norm_scaled", n_fin1.t0 + 8)])
        n_ffn = Norm(tile_of(h), 8, DM, "g_ffn", tile_of(uh), tile_of(ul),
                     ready=[("dve_evac", freed[jobs["wo7"].out][1])])
        n_ple = Norm(tile_of(h), 8, DM, "g_ple", tile_of(uh), tile_of(ul),
                     ready=[("dve_evac", freed[jobs["fd7"].out][1])])
        n_fin2 = Norm(tile_of(h), 8, DM, "g_final", out=tile_of(outb), ready=[("ple_added", 8)])

        def gain(n, k):
            name, at = n.gain if isinstance(n.gain, tuple) else (n.gain, 0)
            return v(name, at + k)

        def rope_job(i):
            return f"qr{i - 1}" if i else "kr"

        block = ctx.enter_context(nc.Block())

        @block.sync
        def _(sp_):
            sp_.dma_start(h[:], x_dram).then_inc(sem("x_in"), 16)
            sp_.dma_start(vec[:], vec_dram).then_inc(sem("vec_in"), 16)
            sp_.dma_start(cst[:], const_dram).then_inc(sem("const_in"), 16)
            for s in range(n_slabs):
                wait(sp_, "wl_ready", s - RAW_RING + 1)
                sp_.dma_start(raw[:, s % RAW_RING, :], slabs_dram[s]).then_inc(sem(f"slab_in{s % RAW_RING}"), 16)
                if s == jobs["fg0"].slab0:
                    wait(sp_, "dve_evac", freed[jobs["wo7"].out][1])
                    sp_.dma_start(pin[:], p_dram).then_inc(sem("p_in"), 16)
            wait(sp_, "norm_scaled", n_fin2.t0 + 8)
            sp_.dma_start(out_dram, outb[:]).then_inc(sem("stored"), 16)
            sp_.wait_ge(sem("stored"), 16)

        @block.gpsimd
        def _(pool):
            for s in range(n_slabs):
                pool.wait_ge(sem("wh_ready"), s + 1)
                nc.gpsimd.tensor_tensor(wl[:, s % PART_RING, :], raw[:, s % RAW_RING, :],
                                        wh[:, s % PART_RING, :].bitcast(f32), ALU.subtract).then_inc(sem("wl_ready"), 1)

        @block.tensor
        def _(pe):
            seen = [0]

            def project(name, hi, lo, ready=None):
                j = jobs[name]
                for o in range(j.out, j.out + j.n_out):
                    if o >= PROJ_BANKS:
                        who, n = freed[o - PROJ_BANKS]
                        wait(pe, f"{who}_evac", n)
                outs = [psum[(j.out + t) % PROJ_BANKS] for t in range(j.n_out)]
                n_cols = j.wide * P
                for k in range(j.kt):
                    if ready:
                        ready(k)
                    b = j.block + k * j.wide
                    s = b // BLK
                    if s >= seen[0]:
                        pe.wait_ge(sem("wl_ready"), s + 1)
                        seen[0] = s + 1
                    c = (b % BLK) * P
                    w_h = wh[:, s % PART_RING, c:c + n_cols]
                    w_l = wl[:, s % PART_RING, c:c + n_cols]
                    for t, o in enumerate(outs):
                        first, last = k == 0, k == j.kt - 1
                        if j.kind == "F":
                            a_h, a_l = hi(k), lo(k)
                            res = o[:, 0:a_h.shape[-1]]
                            nc.tensor.matmul(res, w_h, a_h, start=first, stop=False)
                            nc.tensor.matmul(res, w_h, a_l, start=False, stop=False)
                            ins = nc.tensor.matmul(res, w_l, a_h, start=False, stop=last)
                        else:
                            a_h, a_l = hi(k)[:, t * P:(t + 1) * P], lo(k)[:, t * P:(t + 1) * P]
                            res = o[:, 0:n_cols]
                            nc.tensor.matmul(res, a_h, w_h, start=first, stop=False)
                            nc.tensor.matmul(res, a_h, w_l, start=False, stop=False)
                            ins = nc.tensor.matmul(res, a_l, w_h, start=False, stop=last)
                        if last:
                            ins.then_inc(sem("proj_done"), 1)

            def norm(n, bank_free=()):
                for name, value in bank_free:
                    wait(pe, name, value)
                if n.i:
                    wait(pe, "norm_ln", n.i)
                for k in range(n.kt):
                    wait(pe, "norm_sq", n.t0 + k + 1)
                    ins = nc.tensor.matmul(PS_M[:, 0:T], ones[:], n.sqb(k), start=k == 0, stop=k == n.kt - 1)
                ins.then_inc(sem("norm_sum"), 1)

            def parts_ready(n):
                return lambda k: wait(pe, "norm_lo", n.p0 + k + 1)

            u = lambda k: uh[:, k, :]
            u_lo = lambda k: ul[:, k, :]

            wait(pe, "setup", 2)
            norm(n_ssm)
            project("dt", u, u_lo, parts_ready(n_ssm))
            for c in range(SSM_CT):
                project(f"xbc{c}", u, u_lo)
                if c == 9:
                    pe.wait_ge(sem("dt_scan"), 2)
                    for i, src in enumerate((dtT, acr)):
                        for b in range(TB):
                            o = PS_TR[:, (2 * i + b) * SSM_H:(2 * i + b + 1) * SSM_H]
                            ins = nc.tensor.transpose(o, src[0:SSM_H, b * P:(b + 1) * P], ident[0:SSM_H, 0:SSM_H])
                    ins.then_inc(sem("dt_tr"), 1)

            def x_transpose(j):
                wait(pe, "ssm_silu", 16 + j + 1)
                wait(pe, "xdt", j)
                if j == 0:
                    wait(pe, "dt_tok", 2)
                for b in range(TB):
                    ins = nc.tensor.transpose(PS_TR[:, b * P:(b + 1) * P], xs[:, j, b * P:(b + 1) * P], ident)
                ins.then_inc(sem("x_tr"), 1)

            def decay(hd):
                wait(pe, "decay_exp", hd - 1)
                o = PS_S[hd % 2][:, 0:3 * P]
                sel = ident[0:SSM_H, hd:hd + 1].broadcast_to([SSM_H, P])
                nc.tensor.matmul(o, sel, acr[0:SSM_H, :], start=True, stop=False)
                nc.tensor.matmul(o, ident_b[:], mask_t[:], start=False, stop=True).then_inc(sem("decay"), 1)

            def cb_scores(g):
                wait(pe, "cb_evac", g)
                wait(pe, "norm_ln", n_ssm.i + 1 + max(0, g - 1))
                nc.tensor.matmul(PS_M[:, 0:T], bT[:, g, 0:P], cT[:, g, :], start=True, stop=True)
                nc.tensor.matmul(PS_M[:, T:T + P], bT[:, g, P:T], cT[:, g, P:T], start=True, stop=True,
                                 skip_group_check=True).then_inc(sem("cb"), 1)

            def head_out(hd):
                j, e = divmod(hd, 2)
                wait(pe, "decayed", hd + 1)
                wait(pe, "xdt", j + 1)
                if e == 0:
                    wait(pe, "y_read", j)
                o = PS_Y[64 * e:64 * e + 64, :]
                m = mb[:, hd % 2, :]
                nc.tensor.matmul(o[:, 0:T], xdt[:, j % 2, 0, e, :], m[:, 0:T], start=True, stop=False)
                nc.tensor.matmul(o[:, P:T], xdt[:, j % 2, 1, e, :], m[:, T:T + P], start=False, stop=True)\
                    .then_inc(sem("y"), 1)

            wait(pe, "dt_scan", 3)
            x_transpose(0)
            cb_scores(0)
            decay(0)
            decay(1)
            for j in range(SSM_PAIRS):
                project(f"sz{j}", u, u_lo)
                if j % 2 == 0 and j:
                    norm(n_grp[j // 2 - 1], [("cb_evac", j // 2 + 1)])
                if j + 1 < SSM_PAIRS:
                    x_transpose(j + 1)
                    decay(2 * j + 2)
                    decay(2 * j + 3)
                    if j % 2:
                        cb_scores((j + 1) // 2)
                head_out(2 * j)
                head_out(2 * j + 1)
            norm(n_grp[7], [("cb_evac", 8)])
            for n in range(KD):
                project(f"so{n}", tile_of(ynh), tile_of(ynl),
                        (lambda k: wait(pe, "norm_lo", n_grp[0].p0 + k + 1)) if n == 0 else None)

            norm(n_mla)
            for i, n in enumerate(["cq0", "cq1", "cq2", "ckv0", "ckv1", "kr"]):
                project(n, u, u_lo, parts_ready(n_mla) if i == 0 else None)
            norm(n_kv)
            norm(n_q)

            def rope_swap(i):
                pe.wait_ge(sem("act_evac"), freed[jobs[rope_job(i)].out][1])
                wait(pe, "rope_swapped_read", i)
                if i == 0:
                    wait(pe, "xdt", 16)
                nc.tensor.matmul(PS_TR[:, 0:T], swap, rx[:, i % 2, :], start=True, stop=True)\
                    .then_inc(sem("rope_swap"), 1)

            rope_swap(0)
            for n in range(4):
                project(f"v{n}", tile_of(ckh), tile_of(ckl), parts_ready(n_kv) if n == 0 else None)
            for i in range(8):
                project(f"qr{i}", tile_of(cqh), tile_of(cql), parts_ready(n_q) if i == 0 else None)
                if i:
                    rope_swap(i)
            rope_swap(8)

            def scores(hd):
                wait(pe, "act_evac", freed[jobs[f"qn{hd}"].out][1])
                wait(pe, "prob", hd - 1)
                o = PS_S[hd % 2]
                e, i = hd % 2, hd // 2
                rows = slice(64 * e, 64 * e + 64)
                if hd == 0:
                    wait(pe, "decay_exp", SSM_H)
                    wait(pe, "rope_out", 9)
                for b in range(TB):
                    cols = slice(0, P) if b == 0 else slice(P, 3 * P)
                    q_, nk = slice(b * P, (b + 1) * P), (b + 1) * P
                    nc.tensor.matmul(o[:, cols], qn[:, hd % 2, q_], kn[:, hd % 2, 0:nk], start=b == 0, stop=False,
                                     skip_group_check=True)
                    nc.tensor.matmul(o[:, cols], qr[rows, i, q_], kr[rows, 0:nk], start=False, stop=False,
                                     skip_group_check=True)
                    d = o[:, 0:P] if b == 0 else o[:, 2 * P:3 * P]
                    ins = nc.tensor.matmul(d, ident_b[:], mask_s[:], start=False, stop=True, skip_group_check=True)
                ins.then_inc(sem("score"), 1)

            def prob_transpose(hd):
                wait(pe, "prob_norm", hd + 1)
                wait(pe, "prob_tr_read", hd)
                if hd == 0:
                    wait(pe, "rope_swapped_read", 9)
                for c in range(3):
                    ins = nc.tensor.transpose(PS_TR[:, c * P:(c + 1) * P], pn[:, hd % 2, c * P:(c + 1) * P], ident)
                ins.then_inc(sem("prob_tr"), 1)

            def values(hd):
                wait(pe, "prob_tr_read", hd + 1)
                wait(pe, "att_read", hd)
                if hd == 0:
                    wait(pe, "y_read", 16)
                nc.tensor.matmul(PS_Y[:, 0:T], vn[:, 0, hd * P:(hd + 1) * P], pT[:, hd % 2, 0:T], start=True, stop=False)
                nc.tensor.matmul(PS_Y[:, P:T], vn[:, 1, hd * P:(hd + 1) * P], pT[:, hd % 2, T:T + P],
                                 start=False, stop=True).then_inc(sem("att"), 1)

            def head_proj(hd):
                project(f"kn{hd}", tile_of(ckh), tile_of(ckl))
                project(f"qn{hd}", tile_of(cqh), tile_of(cql))

            head_proj(0)
            scores(0)
            for hd in range(MLA_H):
                if hd + 1 < MLA_H:
                    head_proj(hd + 1)
                project(f"mz{hd}", u, u_lo)
                if hd + 1 < MLA_H:
                    scores(hd + 1)
                prob_transpose(hd)
                values(hd)
            for n in range(KD):
                project(f"mo{n}", tile_of(ogh), tile_of(ogl), (lambda k: wait(pe, "att_lo", k + 1)) if n == 0 else None)

            norm(n_fin1)
            norm(n_mix)
            for i in range(CONV_CT):
                project(f"cg{i}", u, u_lo, parts_ready(n_mix) if i == 0 else None)
                project(f"cv{i}", u, u_lo)
            for n in ["kvc0", "kvc1", "nq0", "nq1", "nq2", "nq3", "ks", "kw", "vsw", "gates", "mg0", "mg1", "mg2", "mg3"]:
                project(n, u, u_lo)
            for i, s in enumerate("kv"):
                for n in range(2):
                    project(f"h{s}{n}", (lambda k, i=i: cxh[:, i, k, :]), (lambda k, i=i: cxl[:, i, k, :]),
                            (lambda k, i=i: wait(pe, "cmp_lo", i + 1)) if n == 0 else None)
            for n in range(4, 8):
                project(f"mg{n}", u, u_lo)
            for i, s in enumerate("kv"):
                project(f"c{s}", (lambda k, i=i: hgh[:, i, k, :]), (lambda k, i=i: hgl[:, i, k, :]),
                        (lambda k, i=i: wait(pe, "cmp_hid_lo", i + 1)))
            for n in range(8, 16):
                project(f"mg{n}", u, u_lo)
            pe.wait_ge(sem("act_evac"), freed[jobs["cv"].out][1])
            nc.tensor.transpose(PS_TR[:, 0:P], vcT[:, :], ident).then_inc(sem("vc_tr"), 1)
            wait(pe, "conv_done", CONV_CT)
            wait(pe, "norm_ln", n_mix.i + 1)
            for k in range(CONV_CT):
                ins = nc.tensor.matmul(PS_M[:, 0:T], ones[:], ccv[:, k, :], start=k == 0, stop=k == 3)
            ins.then_inc(sem("ln_sum"), 1)
            wait(pe, "ln_sq", 1)
            for k in range(CONV_CT):
                ins = nc.tensor.matmul(PS_M[:, 0:T], ones[:], sq[:, k, :], start=k == 0, stop=k == 3)
            ins.then_inc(sem("ln_sum"), 1)

            def cmp_scores(j):
                wait(pe, "cmp_read", j)
                wait(pe, "ln_ln", 1)
                for b in range(TB):
                    nc.tensor.matmul(PS_M[:, b * 64:b * 64 + 64], nq[:, j, b * P:(b + 1) * P], kcT[:], start=b == 0,
                                     stop=False, skip_group_check=True)
                nc.tensor.matmul(PS_M[:, 0:P], ident_b[:], cmp_add[:], start=False, stop=True,
                                 skip_group_check=True).then_inc(sem("cmp_score"), 1)

            def unit_scores(x):
                j, g, ty = x // 4, x // 2 % 2, x % 2
                wait(pe, "nprob", x - 1)
                if x == 0:
                    wait(pe, "prob", MLA_H)
                o, key, rows = PS_S[x % 2], (ksT, kwT)[ty], slice(64 * g, 64 * g + 64)
                for b in range(TB):
                    cols = slice(0, P) if b == 0 else slice(P, 3 * P)
                    nc.tensor.matmul(o[:, cols], nq[rows, j, b * P:(b + 1) * P], key[rows, 0:(b + 1) * P],
                                     start=b == 0, stop=False, skip_group_check=True)
                    d = o[:, 0:P] if b == 0 else o[:, 2 * P:3 * P]
                    ins = nc.tensor.matmul(d, ident_b[:], mask_s[:], start=False, stop=True, skip_group_check=True)
                ins.then_inc(sem("nscore"), 1)

            def unit_values(x):
                j, g, ty = x // 4, x // 2 % 2, x % 2
                wait(pe, "nprob_norm", x + 1)
                wait(pe, "nprob_tr_read", x)
                wait(pe, "cmp_tr_read", j)
                if x == 0:
                    wait(pe, "vc_read", 1)
                for c in range(3):
                    ins = nc.tensor.transpose(PS_TR[:, c * P:(c + 1) * P], npn[:, x % 2, c * P:(c + 1) * P], ident)
                ins.then_inc(sem("nprob_tr"), 1)

            def unit_accumulate(x):
                j, g, ty = x // 4, x // 2 % 2, x % 2
                wait(pe, "nprob_tr_read", x + 1)
                if x % 4 == 0:
                    wait(pe, "natt_lo", j)
                    wait(pe, "att_read", MLA_H)
                o = PS_Y[64 * g:64 * g + 64, :]
                vcol = slice(ty * P + 64 * g, ty * P + 64 * g + 64)
                nc.tensor.matmul(o[:, 0:T], vsw[:, 0, vcol], npT[:, x % 2, 0:T], start=ty == 0, stop=False,
                                 skip_group_check=True)
                nc.tensor.matmul(o[:, P:T], vsw[:, 1, vcol], npT[:, x % 2, T:T + P], start=False, stop=False,
                                 skip_group_check=True).then_inc(sem("nvalue"), 1)

            def cmp_values(j):
                wait(pe, "cmp_prob", j + 1)
                wait(pe, "nprob_tr_read", 4 * j + 4)
                nc.tensor.transpose(PS_TR[:, 0:P], cpn[:, :], ident).then_inc(sem("cmp_tr"), 1)
                wait(pe, "cmp_tr_read", j + 1)
                for b in range(TB):
                    ins = nc.tensor.matmul(PS_Y[:, b * P:(b + 1) * P], vc[:, b, :], cpT[:], start=False, stop=b == 1,
                                           skip_group_check=True)
                ins.then_inc(sem("natt"), 1)

            unit_scores(0)
            for x in range(16):
                if x % 4 == 0:
                    cmp_scores(x // 4)
                if x + 1 < 16:
                    unit_scores(x + 1)
                if x % 2 == 0:
                    project(f"yb{x // 2}", tile_of(cnh), tile_of(cnl),
                            (lambda k: wait(pe, "conv_lo", k + 1)) if x == 0 else None)
                unit_values(x)
                unit_accumulate(x)
                if x % 4 == 3:
                    cmp_values(x // 4)
            for n in range(KD):
                project(f"ya{n}", tile_of(onh), tile_of(onl), (lambda k: wait(pe, "natt_lo", k + 1)) if n == 0 else None)
            for n in range(KD):
                project(f"wo{n}", tile_of(mh), tile_of(ml), (lambda k: wait(pe, "merge_lo", k + 1)) if n == 0 else None)

            norm(n_ffn)
            for i in range(KF):
                project(f"fg{i}", u, u_lo, parts_ready(n_ffn) if i == 0 else None)
                project(f"fv{i}", u, u_lo)
            for n in range(KD):
                project(f"fd{n}", tile_of(ffh), tile_of(ffl), (lambda k: wait(pe, "ff_lo", k + 1)) if n == 0 else None)

            norm(n_ple)
            for n in range(KD):
                project(f"pg{n}", u, u_lo, parts_ready(n_ple) if n == 0 else None)
                project(f"pw{n}", tile_of(ph), tile_of(pl), (lambda k: wait(pe, "p_lo", 1)) if n == 0 else None)
            norm(n_fin2)

        @block.scalar
        def _(act):
            split = [0]
            chain = [0]

            def link(ins):
                chain[0] += 1
                ins.then_inc(sem("act_chain"), 1)
                act.wait_ge(sem("act_chain"), chain[0])

            def feed(name):
                last = min(jobs[name].slab0 + PART_RING - 1, n_slabs - 1)
                while split[0] <= last:
                    s = split[0]
                    act.wait_ge(sem(f"slab_in{s % RAW_RING}"), 16 * (s // RAW_RING + 1))
                    if s >= PART_RING:
                        act.wait_ge(sem("proj_done"), done_with[s - PART_RING])
                    nc.scalar.activation(wh[:, s % PART_RING, :], raw[:, s % RAW_RING, :], ACT.Copy)\
                        .then_inc(sem("wh_ready"), 1)
                    split[0] += 1

            def output(name, t=0):
                feed(name)
                o = jobs[name].out + t
                act.wait_ge(sem("proj_done"), o + 1)
                return psum[o % PROJ_BANKS]

            def squares(n):
                for name, value in n.ready:
                    wait(act, name, value)
                for k in range(n.kt):
                    nc.scalar.activation(n.sqb(k), n.src(k), ACT.Square).then_inc(sem("norm_sq"), 1)

            def inverse_root(n):
                act.wait_ge(sem("norm_sum"), n.i + 1)
                wait(act, "norm_scaled", n.t0)
                nc.scalar.activation(lnb[:], PS_M[:, 0:T], ACT.Ln, bias=eps[:], scale=1.0 / n.width)\
                    .then_inc(sem("norm_ln"), 1)
                act.wait_ge(sem("norm_ln"), n.i + 1)
                nc.scalar.activation(rstd[:], lnb[:], ACT.Exp, scale=-0.5).then_inc(sem("norm_root"), 1)

            def high_parts(n):
                for k in range(n.kt):
                    act.wait_ge(sem("norm_scaled"), n.t0 + k + 1)
                    nc.scalar.activation(n.hi(k), n.sqb(k), ACT.Copy).then_inc(sem("norm_hi"), 1)

            def norm(n):
                squares(n)
                inverse_root(n)
                if not n.out:
                    high_parts(n)

            act.wait_ge(sem("const_in"), 16)
            nc.scalar.activation(ident_b[:], ident, ACT.Copy)
            nc.scalar.activation(mask_s[:], cst[:, 256:384], ACT.Copy)
            nc.scalar.activation(mask_t[:], cst[:, 384:768], ACT.Copy)
            nc.scalar.activation(cmp_add[:], cst[:, 768:896], ACT.Copy).then_inc(sem("setup"), 1)
            feed("dt")
            act.wait_ge(sem("memset"), 3)
            norm(n_ssm)
            act.wait_ge(sem("vec_in"), 16)
            nc.scalar.activation(expa[0:SSM_H, :], v("a_log", 0, SSM_H), ACT.Exp).then_inc(sem("exp_a"), 1)
            act.wait_ge(sem("dt_step"), 1)
            link(nc.scalar.activation(sp[0:SSM_H, 2, :], sp[0:SSM_H, 1, :], ACT.Exp))
            nc.scalar.activation(sp[0:SSM_H, 3, :], sp[0:SSM_H, 2, :], ACT.Ln, bias=1.0).then_inc(sem("dt_log"), 1)

            def ssm_silu(c):
                act.wait_ge(sem("ssm_conv"), c + 1)
                dst = bT[:, c, :] if c < 8 else cT[:, c - 8, :] if c < 16 else xs[:, c - 16, :]
                nc.scalar.activation(dst, scv[:, c % 2, :], ACT.Silu, bias=v("sconv_b", c)).then_inc(sem("ssm_silu"), 1)

            for c in range(SSM_CT):
                o = output(f"xbc{c}")
                wait(act, "ssm_conv", c - 3)
                nc.scalar.activation(sraw[:, c % 4, SSM_TAPS - 1:], o[:, 0:T], ACT.Copy).then_inc(sem("act_evac"), 1)
                if c:
                    ssm_silu(c - 1)
            ssm_silu(SSM_CT - 1)

            def cb_evac(g):
                act.wait_ge(sem("cb"), g + 1)
                wait(act, "decayed", 4 * (g - 1))
                nc.scalar.activation(cbs[:, g % 2, :], PS_M[:, 0:3 * P], ACT.Copy).then_inc(sem("cb_evac"), 1)

            def decay_exp(hd):
                act.wait_ge(sem("decay"), hd + 1)
                wait(act, "decayed", hd - 1)
                o = PS_S[hd % 2]
                nc.scalar.activation(eb[:, hd % 2, 0:T], o[:, 0:T], ACT.Exp, bias=nacn[:, 0, hd:hd + 1])
                nc.scalar.activation(eb[:, hd % 2, T:T + P], o[:, T:T + P], ACT.Exp, bias=nacn[:, 1, hd:hd + 1])\
                    .then_inc(sem("decay_exp"), 1)

            def pair_square(j):
                act.wait_ge(sem("gated"), j + 1)
                nc.scalar.activation(sq[:, j % 4, :], gb[:, j % 4, :], ACT.Square).then_inc(sem("norm_sq"), 1)

            feed("sz0")
            act.wait_ge(sem("dt_tok"), 2)
            act.wait_ge(sem("ssm_silu"), SSM_CT)
            cb_evac(0)
            for j in range(SSM_PAIRS):
                o = output(f"sz{j}")
                if j:
                    pair_square(j - 1)
                wait(act, "dve_evac", freed[jobs[f"sz{j}"].out][1] - 1)
                nc.scalar.activation(zb[:], o[:, 0:T], ACT.Exp, scale=-1.0).then_inc(sem("z_exp"), 1)
                if j % 2 == 0 and j:
                    inverse_root(n_grp[j // 2 - 1])
                decay_exp(2 * j)
                decay_exp(2 * j + 1)
                if j % 2 and j + 1 < SSM_PAIRS:
                    cb_evac((j + 1) // 2)
                if j % 2 == 0 and j:
                    high_parts(n_grp[j // 2 - 1])
            feed("so0")
            pair_square(SSM_PAIRS - 1)
            inverse_root(n_grp[7])
            high_parts(n_grp[7])
            for n in range(KD):
                feed(f"so{n}")

            feed("cq0")
            norm(n_mla)
            for n in range(3):
                o = output(f"cq{n}")
                nc.scalar.activation(cqr[:, n, :], o[:, 0:T], ACT.Copy).then_inc(sem("act_evac"), 1)
            for n in range(2):
                o = output(f"ckv{n}")
                nc.scalar.activation(ckr[:, n, :], o[:, 0:T], ACT.Copy).then_inc(sem("act_evac"), 1)

            o = output("kr")
            nc.scalar.activation(rx[:, 0, :], o[:, 0:T], ACT.Copy).then_inc(sem("act_evac"), 1)
            feed("v0")
            act.wait_ge(sem("act_evac"), freed[jobs["ckv1"].out][1])
            squares(n_kv)
            inverse_root(n_kv)
            high_parts(n_kv)
            squares(n_q)
            inverse_root(n_q)
            high_parts(n_q)
            for n in range(4):
                for t in range(TB):
                    o = output(f"v{n}", t)
                    nc.scalar.activation(vn[:, t, n * 512:(n + 1) * 512], o[:, :], ACT.Copy).then_inc(sem("act_evac"), 1)
            for i in range(8):
                o = output(f"qr{i}")
                wait(act, "rope_out", i)
                nc.scalar.activation(rx[:, (i + 1) % 2, :], o[:, 0:T], ACT.Copy).then_inc(sem("act_evac"), 1)

            def evac_head(hd):
                o = output(f"kn{hd}")
                wait(act, "score", hd - 1)
                nc.scalar.activation(kn[:, hd % 2, :], o[:, 0:T], ACT.Copy).then_inc(sem("act_evac"), 1)
                o = output(f"qn{hd}")
                nc.scalar.activation(qn[:, hd % 2, :], o[:, 0:T], ACT.Copy).then_inc(sem("act_evac"), 1)

            def prob(hd):
                act.wait_ge(sem("max"), hd + 1)
                wait(act, "prob_tr", hd - 1)
                o, s = PS_S[hd % 2], (MLA_D + MLA_R) ** -0.5
                for b, c in enumerate((slice(0, P), slice(P, 3 * P))):
                    ins = nc.scalar.activation(pn[:, hd % 2, c], o[:, c], ACT.Exp, bias=nm[:, hd % 2, b:b + 1], scale=s,
                                               accum_out=rs[:, hd % 2, b:b + 1])
                ins.then_inc(sem("prob"), 1)

            evac_head(0)
            for hd in range(MLA_H):
                if hd == 0:
                    act.wait_ge(sem("rope_out"), 9)
                prob(hd)
                if hd + 1 < MLA_H:
                    evac_head(hd + 1)
                o = output(f"mz{hd}")
                wait(act, "dve_evac", freed[jobs[f"mz{hd}"].out][1] - 1)
                nc.scalar.activation(mze[:], o[:, 0:T], ACT.Exp, scale=-1.0).then_inc(sem("mz_exp"), 1)
                act.wait_ge(sem("prob_tr"), hd + 1)
                wait(act, "att", hd - 1)
                nc.scalar.activation(pT[:, hd % 2, :], PS_TR[:, 0:3 * P], ACT.Copy).then_inc(sem("prob_tr_read"), 1)
                act.wait_ge(sem("att_read"), hd + 1)
                nc.scalar.activation(ogh[:, hd, :], ogt[:, hd % 2, :], ACT.Copy).then_inc(sem("att_hi"), 1)
            for n in range(KD):
                feed(f"mo{n}")

            feed("cg0")
            norm(n_fin1)
            norm(n_mix)
            for i in range(CONV_CT):
                o = output(f"cg{i}")
                wait(act, "dve_evac", freed[jobs[f"cv{i}"].out][1] - 2)
                nc.scalar.activation(csg[:, i % 2, :], o[:, 0:T], ACT.Sigmoid).then_inc(sem("act_evac"), 1)
            for i in range(2):
                o = output(f"kvc{i}")
                if i == 0:
                    act.wait_ge(sem("cx_zero"), 1)
                for g in range(NSA_G):
                    r_ = slice(64 * g, 64 * g + 64)
                    nc.scalar.activation(ce[0:64, i, g, :], o[r_, 0:T], ACT.Copy)
                    ins = nc.scalar.activation(ce[64:128, i, g, 0:T - 1], o[r_, 1:T], ACT.Copy)
                ins.then_inc(sem("act_evac"), 1)
            for j in range(NSA_J):
                o = output(f"nq{j}")
                nc.scalar.activation(nq[:, j, :], o[:, 0:T], ACT.Copy).then_inc(sem("act_evac"), 1)
            for name, dst in (("ks", ksT), ("kw", kwT)):
                o = output(name)
                nc.scalar.activation(dst[:], o[:, 0:T], ACT.Copy).then_inc(sem("act_evac"), 1)
            for t in range(TB):
                o = output("vsw", t)
                nc.scalar.activation(vsw[:, t, :], o[:, 0:T], ACT.Copy).then_inc(sem("act_evac"), 1)
            for t in range(TB):
                o = output("gates", t)
                nc.scalar.activation(gates[:, t, :], o[:, 0:24], ACT.Sigmoid).then_inc(sem("act_evac"), 1)
            for n in range(4):
                o = output(f"mg{n}")
                nc.scalar.activation(gm[:, n, :], o[:, 0:T], ACT.Sigmoid).then_inc(sem("act_evac"), 1)
            for i in range(2):
                act.wait_ge(sem("cmp_x"), i + 1)
                nc.scalar.activation(cxh[:, i, :, :], cx[:, i, :, :], ACT.Copy).then_inc(sem("cmp_hi"), 1)
            for i, s in enumerate("kv"):
                for n in range(2):
                    o = output(f"h{s}{n}")
                    nc.scalar.activation(hg[:, i, n, :], o[:, 0:64], ACT.Gelu_apprx_tanh).then_inc(sem("act_evac"), 1)
                act.wait_ge(sem("act_evac"), freed[jobs[f"h{s}1"].out][1])
                nc.scalar.activation(hgh[:, i, :, :], hg[:, i, :, :], ACT.Copy).then_inc(sem("cmp_hid_hi"), 1)
            for n in range(4, 8):
                o = output(f"mg{n}")
                nc.scalar.activation(gm[:, n, :], o[:, 0:T], ACT.Sigmoid).then_inc(sem("act_evac"), 1)
            o = output("ck")
            act.wait_ge(sem("vc_zero"), 2)
            for g in range(NSA_G):
                r_, c_ = slice(64 * g, 64 * g + 64), slice(CPAD * g, CPAD * g + CPAD)
                ins = nc.scalar.activation(kcT[r_, c_], o[r_, c_], ACT.Copy)
            ins.then_inc(sem("act_evac"), 1)
            o = output("cv")
            nc.scalar.activation(vcT[:, 0:64], o[:, 0:64], ACT.Copy)
            nc.scalar.activation(vcT[:, 64:128], o[:, 0:64], ACT.Copy).then_inc(sem("act_evac"), 1)
            for n in range(8, 16):
                o = output(f"mg{n}")
                nc.scalar.activation(gm[:, n, :], o[:, 0:T], ACT.Sigmoid).then_inc(sem("act_evac"), 1)
            act.wait_ge(sem("vc_tr"), 1)
            for b in range(TB):
                for g in range(NSA_G):
                    r_ = slice((b * 2 + g) * CPAD, (b * 2 + g + 1) * CPAD)
                    ins = nc.scalar.activation(vc[r_, b, 64 * g:64 * g + 64], PS_TR[r_, 64 * g:64 * g + 64], ACT.Copy)
            ins.then_inc(sem("vc_read"), 1)
            act.wait_ge(sem("ln_centred"), 1)
            nc.scalar.activation(sq[:, 0:4, :], ccv[:], ACT.Square).then_inc(sem("ln_sq"), 1)
            act.wait_ge(sem("ln_sum"), 2)
            nc.scalar.activation(lnb[:], PS_M[:, 0:T], ACT.Ln, bias=eps[:], scale=1.0 / (CONV_CT * P))\
                .then_inc(sem("ln_ln"), 1)
            act.wait_ge(sem("ln_ln"), 1)
            nc.scalar.activation(rstd[:], lnb[:], ACT.Exp, scale=-0.5).then_inc(sem("ln_root"), 1)
            for k in range(CONV_CT):
                act.wait_ge(sem("ln_scaled"), k + 1)
                nc.scalar.activation(sq[:, 4 + k, :], sq[:, k, :], ACT.Silu, bias=v("ln_b", k)).then_inc(sem("conv_act"), 1)
            for k in range(CONV_CT):
                act.wait_ge(sem("conv_act"), k + 1)
                nc.scalar.activation(cnh[:, k, :], sq[:, 4 + k, :], ACT.Copy).then_inc(sem("conv_hi"), 1)

            def nprob(x):
                act.wait_ge(sem("nmax"), x + 1)
                wait(act, "nprob_tr", x - 1)
                o = PS_S[x % 2]
                for b, c in enumerate((slice(0, P), slice(P, 3 * P))):
                    ins = nc.scalar.activation(npn[:, x % 2, c], o[:, c], ACT.Exp, bias=nnm[:, x % 2, b:b + 1],
                                               scale=NSA_D ** -0.5, accum_out=nrs[:, x % 2, b:b + 1])
                ins.then_inc(sem("nprob"), 1)

            for x in range(16):
                nprob(x)
                if x % 4 == 0:
                    act.wait_ge(sem("cmp_read"), x // 4 + 1)
                    nc.scalar.activation(cpn[:], csc[:], ACT.Exp, scale=NSA_D ** -0.5).then_inc(sem("cmp_exp"), 1)
                if x % 2 == 0:
                    feed(f"yb{x // 2}")
                act.wait_ge(sem("nprob_tr"), x + 1)
                wait(act, "nvalue", x - 1)
                nc.scalar.activation(npT[:, x % 2, :], PS_TR[:, 0:3 * P], ACT.Copy).then_inc(sem("nprob_tr_read"), 1)
                if x % 4 == 3:
                    j = x // 4
                    act.wait_ge(sem("cmp_tr"), j + 1)
                    wait(act, "natt", j)
                    nc.scalar.activation(cpT[:], PS_TR[:, 0:P], ACT.Copy).then_inc(sem("cmp_tr_read"), 1)
                    act.wait_ge(sem("natt"), j + 1)
                    nc.scalar.activation(onh[:, j, :], PS_Y[:, 0:T], ACT.Copy).then_inc(sem("natt_hi"), 1)
            for n in range(KD):
                feed(f"ya{n}")
                act.wait_ge(sem("merged"), n + 1)
                nc.scalar.activation(mh[:, n, :], mt[:, n, :], ACT.Copy).then_inc(sem("merge_hi"), 1)
            for n in range(KD):
                feed(f"wo{n}")

            feed("fg0")
            norm(n_ffn)
            act.wait_ge(sem("p_in"), 16)
            nc.scalar.activation(ph[:], pin[:], ACT.Copy).then_inc(sem("p_hi"), 1)

            def ff_act(i):
                act.wait_ge(sem("ff_conv"), 2 * i + 1)
                wait(act, "ff_gated", i - 1)
                nc.scalar.activation(fge[:, i % 2, :], fcv[:, 2 * i % 4, :], ACT.Gelu_apprx_tanh, bias=v("fconv_b", 2 * i))\
                    .then_inc(sem("ff_gelu"), 1)

            def ff_high(i):
                act.wait_ge(sem("ff_gated"), i + 1)
                nc.scalar.activation(ffh[:, i, :], fgt[:, i % 2, :], ACT.Copy).then_inc(sem("ff_hi"), 1)

            for i in range(KF):
                for e, s in enumerate("gv"):
                    o = output(f"f{s}{i}")
                    if i == 0:
                        act.wait_ge(sem("ff_pad"), 1)
                    wait(act, "ff_conv", 2 * i + e - 3)
                    nc.scalar.activation(fraw[:, (2 * i + e) % 4, FF_TAPS - 1:], o[:, 0:T], ACT.Copy)\
                        .then_inc(sem("act_evac"), 1)
                if i:
                    ff_high(i - 1)
                ff_act(i)
            ff_high(KF - 1)
            for n in range(KD):
                feed(f"fd{n}")

            feed("pg0")
            norm(n_ple)
            for n in range(KD):
                o = output(f"pg{n}")
                wait(act, "ple_added", n - 1)
                nc.scalar.activation(psg[:, n % 2, :], o[:, 0:T], ACT.Sigmoid).then_inc(sem("act_evac"), 1)
                feed(f"pw{n}")
            norm(n_fin2)

        @block.vector
        def _(dve):
            chain = [0]

            def link(ins):
                chain[0] += 1
                ins.then_inc(sem("dve_chain"), 1)
                dve.wait_ge(sem("dve_chain"), chain[0])

            def output(name, t=0):
                o = jobs[name].out + t
                dve.wait_ge(sem("proj_done"), o + 1)
                return psum[o % PROJ_BANKS]

            tt, ts, stt = nc.vector.tensor_tensor, nc.vector.tensor_scalar, nc.vector.scalar_tensor_tensor

            def scale_tiles(n):
                dve.wait_ge(sem("norm_root"), n.i + 1)
                for k in range(n.kt):
                    dst = n.out(k) if n.out else n.sqb(k)
                    stt(dst, n.src(k), gain(n, k), rstd[:], ALU.mult, ALU.mult).then_inc(sem("norm_scaled"), 1)

            def low_parts(n):
                for k in range(n.kt):
                    dve.wait_ge(sem("norm_hi"), n.p0 + k + 1)
                    tt(n.lo(k), n.sqb(k), n.hi(k).bitcast(f32), ALU.subtract).then_inc(sem("norm_lo"), 1)

            def norm(n):
                scale_tiles(n)
                if not n.out:
                    low_parts(n)

            nc.vector.memset(ones[:], 1.0).then_inc(sem("memset"), 1)
            nc.vector.memset(eps[:], EPS).then_inc(sem("memset"), 1)
            nc.vector.memset(sraw[:, :, 0:SSM_TAPS - 1], 0.0).then_inc(sem("memset"), 1)
            dve.wait_ge(sem("memset"), 3)
            dve.sem_inc(sem("setup"), 1)
            dve.wait_ge(sem("vec_in"), 16)
            norm(n_ssm)
            H = slice(0, SSM_H)
            o = output("dt")
            ts(sp[H, 0, :], o[H, 0:T], v("dt_bias", 0, SSM_H), None, ALU.add).then_inc(sem("dve_evac"), 1)
            dve.wait_ge(sem("dve_evac"), 1)
            link(ts(sp[H, 1, :], sp[H, 0, :], -1.0, None, ALU.mult))
            tt(sp[H, 1, :], sp[H, 0, :], sp[H, 1, :], ALU.min).then_inc(sem("dt_step"), 1)
            dve.wait_ge(sem("dt_log"), 1)
            link(ts(dtT[H, :], sp[H, 2, :], 1.0, None, ALU.add))
            link(ts(dtT[H, :], dtT[H, :], -1.0, None, ALU.add))
            link(tt(dtT[H, :], sp[H, 2, :], dtT[H, :], ALU.subtract))
            link(tt(dtT[H, :], dtT[H, :], sp[H, 3, :], ALU.add))
            stt(dtT[H, :], sp[H, 0, :], 0.0, dtT[H, :], ALU.max, ALU.add).then_inc(sem("dt_scan"), 1)
            dve.wait_ge(sem("dt_scan"), 1)
            dve.wait_ge(sem("exp_a"), 1)
            link(ts(sp[H, 1, :], dtT[H, :], expa[H, :], -1.0, ALU.mult, ALU.mult))
            link(ts(sp[H, 0, :], dtT[H, :], 0.0, 1.0, ALU.mult, ALU.add))
            nc.vector.tensor_tensor_scan(acr[H, 0:T], sp[H, 0, :], sp[H, 1, :], 0.0, ALU.mult, ALU.add)\
                .then_inc(sem("dt_scan"), 1)
            dve.wait_ge(sem("dt_scan"), 2)
            nc.vector.tensor_copy(acr[H, T:T + P], acr[H, P:T]).then_inc(sem("dt_scan"), 1)

            def conv(dst, src, taps, weight):
                for i in range(taps):
                    w = weight(i)
                    if i == 0:
                        ins = ts(dst, src(0), w, None, ALU.mult)
                    else:
                        ins = stt(dst, src(i), w, dst, ALU.mult, ALU.add)
                    if i + 1 < taps:
                        link(ins)
                return ins

            for c in range(SSM_CT):
                dve.wait_ge(sem("act_evac"), c + 1)
                wait(dve, "ssm_silu", c - 1)
                conv(scv[:, c % 2, :], lambda i: sraw[:, c % 4, i:i + T], SSM_TAPS,
                     lambda i: v("sconv_w", c * SSM_TAPS + i)).then_inc(sem("ssm_conv"), 1)
                if c == 10:
                    dve.wait_ge(sem("dt_tr"), 1)
                    nc.vector.tensor_copy(dtn[:], PS_TR[:, 0:64].rearrange("p (b h) -> p b h", b=2))\
                        .then_inc(sem("dt_tok"), 1)
                    ts(nacn[:], PS_TR[:, 64:128].rearrange("p (b h) -> p b h", b=2), -1.0, None, ALU.mult)\
                        .then_inc(sem("dt_tok"), 1)

            def scale_x(j):
                dve.wait_ge(sem("x_tr"), j + 1)
                wait(dve, "y", 2 * (j - 1))
                src = PS_TR[:, 0:T].rearrange("p (b e d) -> p b e d", b=2, e=2)
                d = dtn[:, :, 2 * j:2 * j + 2].unsqueeze(3).broadcast_to([P, TB, 2, 64])
                tt(xdt[:, j % 2, :, :, :], src, d, ALU.mult).then_inc(sem("xdt"), 1)

            def decayed(hd):
                g = hd // 4
                dve.wait_ge(sem("decay_exp"), hd + 1)
                dve.wait_ge(sem("cb_evac"), g + 1)
                wait(dve, "y", hd - 1)
                tt(mb[:, hd % 2, :], eb[:, hd % 2, :], cbs[:, g % 2, :], ALU.mult).then_inc(sem("decayed"), 1)

            dve.wait_ge(sem("dt_tok"), 2)
            scale_x(0)
            for j in range(SSM_PAIRS):
                o = output(f"sz{j}")
                dve.wait_ge(sem("z_exp"), j + 1)
                link(ts(szb[:, j % 2, :], zb[:], 1.0, None, ALU.add))
                link(nc.vector.reciprocal(szb[:, j % 2, :], szb[:, j % 2, :]))
                tt(szb[:, j % 2, :], szb[:, j % 2, :], o[:, 0:T], ALU.mult).then_inc(sem("dve_evac"), 1)
                dve.wait_ge(sem("dve_evac"), freed[jobs[f"sz{j}"].out][1])
                if j + 1 < SSM_PAIRS:
                    scale_x(j + 1)
                decayed(2 * j)
                decayed(2 * j + 1)
                if j % 2 == 0 and j:
                    scale_tiles(n_grp[j // 2 - 1])
                    low_parts(n_grp[j // 2 - 1])
                dve.wait_ge(sem("y"), 2 * j + 2)
                stt(yt[:], xs[:, j, :], v("ssm_d", j), PS_Y[:, 0:T], ALU.mult, ALU.add).then_inc(sem("y_read"), 1)
                dve.wait_ge(sem("y_read"), j + 1)
                tt(gb[:, j % 4, :], yt[:], szb[:, j % 2, :], ALU.mult).then_inc(sem("gated"), 1)
            scale_tiles(n_grp[7])
            low_parts(n_grp[7])

            def add_to_residual(prefix):
                for n in range(KD):
                    o = output(f"{prefix}{n}")
                    tt(h[:, n, :], o[:, 0:T], h[:, n, :], ALU.add).then_inc(sem("dve_evac"), 1)

            add_to_residual("so")

            norm(n_mla)

            def rotate(i):
                dst = kr[:] if i == 0 else qr[:, i - 1, :]
                dve.wait_ge(sem("act_evac"), freed[jobs[rope_job(i)].out][1])
                wait(dve, "rope_out", i)
                tt(r2[:], rx[:, i % 2, :], cos, ALU.mult).then_inc(sem("rope_cos"), 1)
                dve.wait_ge(sem("rope_swap"), i + 1)
                tt(r1[:], PS_TR[:, 0:T], sin, ALU.mult).then_inc(sem("rope_swapped_read"), 1)
                dve.wait_ge(sem("rope_swapped_read"), i + 1)
                dve.wait_ge(sem("rope_cos"), i + 1)
                tt(dst, r1[:], r2[:], ALU.add).then_inc(sem("rope_out"), 1)

            scale_tiles(n_kv)
            low_parts(n_kv)
            scale_tiles(n_q)
            low_parts(n_q)
            for i in range(9):
                rotate(i)

            def row_max(bank, m, neg, i, scale, done):
                link(nc.vector.tensor_reduce(m[:, i % 2, 0:1], bank[:, 0:P], AX.X, ALU.max))
                link(nc.vector.tensor_reduce(m[:, i % 2, 1:2], bank[:, P:3 * P], AX.X, ALU.max))
                ts(neg[:, i % 2, :], m[:, i % 2, :], -scale, None, ALU.mult).then_inc(sem(done), 1)

            def mla_max(hd):
                dve.wait_ge(sem("score"), hd + 1)
                row_max(PS_S[hd % 2], mx, nm, hd, (MLA_D + MLA_R) ** -0.5, "max")

            def att_low(hd):
                dve.wait_ge(sem("att_hi"), hd + 1)
                tt(ogl[:, hd, :], ogt[:, hd % 2, :], ogh[:, hd, :].bitcast(f32), ALU.subtract).then_inc(sem("att_lo"), 1)

            mla_max(0)
            for hd in range(MLA_H):
                dve.wait_ge(sem("prob"), hd + 1)
                link(nc.vector.reciprocal(rr[:, hd % 2, :], rs[:, hd % 2, :]))
                ts(pn[:, hd % 2, 0:P], pn[:, hd % 2, 0:P], rr[:, hd % 2, 0:1], None, ALU.mult)
                ts(pn[:, hd % 2, P:3 * P], pn[:, hd % 2, P:3 * P], rr[:, hd % 2, 1:2], None, ALU.mult)\
                    .then_inc(sem("prob_norm"), 1)
                if hd:
                    att_low(hd - 1)
                o = output(f"mz{hd}")
                dve.wait_ge(sem("mz_exp"), hd + 1)
                wait(dve, "att_read", hd)
                link(ts(mzb[:], mze[:], 1.0, None, ALU.add))
                link(nc.vector.reciprocal(mzb[:], mzb[:]))
                tt(mzb[:], mzb[:], o[:, 0:T], ALU.mult).then_inc(sem("dve_evac"), 1)
                dve.wait_ge(sem("dve_evac"), freed[jobs[f"mz{hd}"].out][1])
                if hd + 1 < MLA_H:
                    mla_max(hd + 1)
                dve.wait_ge(sem("att"), hd + 1)
                tt(ogt[:, hd % 2, :], PS_Y[:, 0:T], mzb[:], ALU.mult).then_inc(sem("att_read"), 1)
            att_low(MLA_H - 1)
            add_to_residual("mo")

            norm(n_fin1)
            norm(n_mix)
            link(nc.vector.memset(cpad[:, :, 0:CONV_TAPS - 1], 0.0))
            nc.vector.memset(vc[:], 0.0).then_inc(sem("vc_zero"), 1)
            nc.vector.memset(kcT[:], 0.0).then_inc(sem("vc_zero"), 1)
            link(nc.vector.memset(cx[:], 0.0))
            dve.sem_inc(sem("cx_zero"), 1)
            for i in range(CONV_CT):
                o = output(f"cv{i}")
                dve.wait_ge(sem("act_evac"), freed[jobs[f"cg{i}"].out][1])
                tt(cpad[:, i, CONV_TAPS - 1:], o[:, 0:T], csg[:, i % 2, :], ALU.mult).then_inc(sem("dve_evac"), 1)
            dve.wait_ge(sem("dve_evac"), freed[jobs["cv3"].out][1])

            def conv31(i):
                last = conv(ccv[:, i, :], lambda t: cpad[:, i, t:t + T], CONV_TAPS,
                            lambda t: v("conv_w", i * CONV_TAPS + t))
                link(last)
                ts(ccv[:, i, :], ccv[:, i, :], v("conv_b", i), None, ALU.add).then_inc(sem("conv_done"), 1)

            conv31(0)
            for i, pos in enumerate(("pos_k", "pos_v")):
                dve.wait_ge(sem("act_evac"), freed[jobs[f"kvc{i}"].out][1])
                for g in range(NSA_G):
                    row = ce[:, i, g, :]
                    src = row.rearrange("p (c k e) -> p k c e", k=CMP_STRIDE // 2, e=2)[:, :, :, 0]
                    for half in range(2):
                        s_ = src[:, :, half:half + N_CMP]
                        d_ = cx[:, i, 8 * half:8 * half + 8, g * CPAD:g * CPAD + N_CMP]
                        p_ = vec[:, VC[pos] + 8 * half:VC[pos] + 8 * half + 8].unsqueeze(2).broadcast_to([P, 8, N_CMP])
                        link(tt(d_, s_, p_, ALU.add))
                dve.sem_inc(sem("cmp_x"), 1)
            for i in range(2):
                dve.wait_ge(sem("cmp_hi"), i + 1)
                tt(cxl[:, i, :, :], cx[:, i, :, :], cxh[:, i, :, :].bitcast(f32), ALU.subtract).then_inc(sem("cmp_lo"), 1)
            conv31(1)
            for i in range(2):
                dve.wait_ge(sem("cmp_hid_hi"), i + 1)
                tt(hgl[:, i, :, :], hg[:, i, :, :], hgh[:, i, :, :].bitcast(f32), ALU.subtract)\
                    .then_inc(sem("cmp_hid_lo"), 1)
            conv31(2)
            conv31(3)
            dve.wait_ge(sem("ln_sum"), 1)
            link(ts(yat[:], PS_M[:, 0:T], 1.0 / (CONV_CT * P), None, ALU.mult))
            dve.wait_ge(sem("conv_done"), CONV_CT)
            tt(ccv[:], ccv[:], yat[:].unsqueeze(1).broadcast_to([P, CONV_CT, T]), ALU.subtract)\
                .then_inc(sem("ln_centred"), 1)
            dve.wait_ge(sem("ln_root"), 1)
            for k in range(CONV_CT):
                stt(sq[:, k, :], ccv[:, k, :], v("ln_g", k), rstd[:], ALU.mult, ALU.mult).then_inc(sem("ln_scaled"), 1)
            for k in range(CONV_CT):
                dve.wait_ge(sem("conv_hi"), k + 1)
                tt(cnl[:, k, :], sq[:, 4 + k, :], cnh[:, k, :].bitcast(f32), ALU.subtract).then_inc(sem("conv_lo"), 1)

            def nsa_max(x):
                dve.wait_ge(sem("nscore"), x + 1)
                row_max(PS_S[x % 2], nmx, nnm, x, NSA_D ** -0.5, "nmax")

            four = lambda t: t.rearrange("p (a c) -> p a c", c=CPAD)
            spread = lambda t: t.unsqueeze(2).broadcast_to([P, 4, CPAD])

            nsa_max(0)
            for x in range(16):
                j, g, ty = x // 4, x // 2 % 2, x % 2
                hd = g * NSA_J + j
                if ty == 0 and g == 0:
                    dve.wait_ge(sem("cmp_score"), j + 1)
                    wait(dve, "cmp_tr", j)
                    link(nc.vector.tensor_reduce(cmx[:], four(PS_M[:, 0:P]), AX.X, ALU.max))
                    tt(four(csc[:]), four(PS_M[:, 0:P]), spread(cmx[:]), ALU.subtract).then_inc(sem("cmp_read"), 1)
                dve.wait_ge(sem("nprob"), x + 1)
                link(nc.vector.reciprocal(nrr[:, x % 2, :], nrs[:, x % 2, :]))
                col = (1 + ty) * 8 + hd
                link(tt(nrr[:, x % 2, :], nrr[:, x % 2, :], gates[:, :, col], ALU.mult))
                ts(npn[:, x % 2, 0:P], npn[:, x % 2, 0:P], nrr[:, x % 2, 0:1], None, ALU.mult)
                ts(npn[:, x % 2, P:3 * P], npn[:, x % 2, P:3 * P], nrr[:, x % 2, 1:2], None, ALU.mult)\
                    .then_inc(sem("nprob_norm"), 1)
                if x + 1 < 16:
                    nsa_max(x + 1)
                if x % 4 == 1:
                    dve.wait_ge(sem("cmp_exp"), j + 1)
                    link(tt(cpn[:], cpn[:], cmp_ok, ALU.mult))
                    link(nc.vector.tensor_reduce(crs[:], four(cpn[:]), AX.X, ALU.add))
                    link(ts(crs[:], crs[:], 1e-30, None, ALU.max))
                    link(nc.vector.reciprocal(crr[:], crs[:]))
                    link(tt(crr[:].rearrange("p (b g) -> p b g", b=2), crr[:].rearrange("p (b g) -> p b g", b=2),
                            gates[:, :, j:j + 5:4], ALU.mult))
                    tt(four(cpn[:]), four(cpn[:]), spread(crr[:]), ALU.mult).then_inc(sem("cmp_prob"), 1)
                if x % 2 == 0:
                    n = x // 2
                    o = output(f"yb{n}")
                    stt(mt[:, n, :], o[:, 0:T], v("b_co", n), gm[:, 8 + n, :], ALU.add, ALU.mult).then_inc(sem("dve_evac"), 1)
                if x % 4 == 3:
                    dve.wait_ge(sem("natt_hi"), j + 1)
                    tt(onl[:, j, :], PS_Y[:, 0:T], onh[:, j, :].bitcast(f32), ALU.subtract).then_inc(sem("natt_lo"), 1)

            def merge_low(n):
                dve.wait_ge(sem("merge_hi"), n + 1)
                tt(ml[:, n, :], mt[:, n, :], mh[:, n, :].bitcast(f32), ALU.subtract).then_inc(sem("merge_lo"), 1)

            for n in range(KD):
                o = output(f"ya{n}")
                wait(dve, "merged", n)
                tt(yat[:], o[:, 0:T], gm[:, n, :], ALU.mult).then_inc(sem("dve_evac"), 1)
                dve.wait_ge(sem("dve_evac"), freed[jobs[f"ya{n}"].out][1])
                tt(mt[:, n, :], mt[:, n, :], yat[:], ALU.add).then_inc(sem("merged"), 1)
                if n:
                    merge_low(n - 1)
            merge_low(KD - 1)
            add_to_residual("wo")

            nc.vector.memset(fraw[:, :, 0:FF_TAPS - 1], 0.0).then_inc(sem("ff_pad"), 1)
            norm(n_ffn)
            dve.wait_ge(sem("p_hi"), 1)
            tt(pl[:], pin[:], ph[:].bitcast(f32), ALU.subtract).then_inc(sem("p_lo"), 1)

            def ff_gate(i):
                dve.wait_ge(sem("ff_gelu"), i + 1)
                wait(dve, "ff_lo", i - 1)
                stt(fgt[:, i % 2, :], fcv[:, (2 * i + 1) % 4, :], v("fconv_b", 2 * i + 1), fge[:, i % 2, :],
                    ALU.add, ALU.mult).then_inc(sem("ff_gated"), 1)

            def ff_low(i):
                dve.wait_ge(sem("ff_hi"), i + 1)
                tt(ffl[:, i, :], fgt[:, i % 2, :], ffh[:, i, :].bitcast(f32), ALU.subtract).then_inc(sem("ff_lo"), 1)

            for i in range(KF):
                for e, s in enumerate("gv"):
                    c = 2 * i + e
                    dve.wait_ge(sem("act_evac"), freed[jobs[f"f{s}{i}"].out][1])
                    conv(fcv[:, c % 4, :], lambda t: fraw[:, c % 4, t:t + T], FF_TAPS,
                         lambda t: v("fconv_w", c * FF_TAPS + t)).then_inc(sem("ff_conv"), 1)
                if i:
                    ff_low(i - 1)
                dve.wait_ge(sem("ff_conv"), 2 * i + 2)
                ff_gate(i)
            ff_low(KF - 1)
            add_to_residual("fd")

            norm(n_ple)
            for n in range(KD):
                o = output(f"pw{n}")
                dve.wait_ge(sem("act_evac"), freed[jobs[f"pg{n}"].out][1])
                wait(dve, "ple_added", n)
                tt(pt[:], o[:, 0:T], psg[:, n % 2, :], ALU.mult).then_inc(sem("dve_evac"), 1)
                dve.wait_ge(sem("dve_evac"), freed[jobs[f"pw{n}"].out][1])
                tt(h[:, n, :], h[:, n, :], pt[:], ALU.add).then_inc(sem("ple_added"), 1)
            norm(n_fin2)


def arena_base(nc, kb):
    return nc.sbuf_base - kb * 1024


def shape_constants():
    c = np.zeros((P, N_CONST), np.float32)
    i = np.arange(P)
    c[:, 0:128] = np.eye(P)
    s = np.zeros((P, P))
    s[i ^ 32, i] = 1.0
    c[:, 128:256] = s
    c[:, 256:384] = np.where(i[None, :] > i[:, None], NEG, 0.0)
    tri = np.where(i[None, :] < i[:, None], NEG, 0.0)
    c[:, 384:512] = tri
    c[:, 640:768] = tri
    tok = np.arange(TB)[None, :, None, None] * P + i[:, None, None, None]
    key = np.arange(CPAD)[None, None, None, :]
    ok = (key * CMP_STRIDE + CMP_LEN - 1 <= tok) & (key < N_CMP)
    ok = np.broadcast_to(ok, (P, TB, NSA_G, CPAD)).reshape(P, P)
    c[:, 768:896] = np.where(ok, 0.0, NEG)
    c[:, 896:1024] = ok
    half = MLA_R // 2
    freq = np.float32(500000.0) ** (-np.arange(half, dtype=np.float32) / half)
    ang = np.arange(T, dtype=np.float32)[None, :] * freq[i % half][:, None]
    c[:, 1024:1280] = np.cos(ang)
    c[:, 1280:1536] = np.where((i // half % 2 == 0)[:, None], -np.sin(ang), np.sin(ang))
    return c


def pack_weights(inputs):
    jobs, _, _, n_slabs = plan()
    stream = np.zeros((n_slabs * BLK, P, P), np.float32)
    flat = {}
    for name, array, cols, rows, kind, _ in weight_jobs():
        if array not in flat:
            w = np.asarray(inputs[array])[0]
            flat[array] = np.concatenate([w, np.zeros((w.shape[0], 1), w.dtype)], axis=1)
        w = flat[array][:, cols]
        if rows is not None:
            w = w[rows]
        j = jobs[name]
        blocks = w.reshape(j.kt, P, j.wide, P).transpose(0, 2, 1, 3).reshape(j.blocks, P, P)
        stream[j.block:j.block + j.blocks] = blocks
    return np.ascontiguousarray(stream.reshape(n_slabs, BLK, P, P).transpose(0, 2, 1, 3).reshape(n_slabs, P, SLAB))


def pack_vectors(inputs):
    VC, n = vector_columns()
    vec = np.zeros((P, n), np.float32)

    def put(name, a):
        a = np.asarray(a).reshape(-1, P)
        vec[:, VC[name]:VC[name] + a.shape[0]] = a.T

    g = {k: np.asarray(x) for k, x in inputs.items()}
    put("norm0", g["norm_w"][0])
    put("norm1", g["norm_w"][1])
    put("final1", g["final_norm_w"])
    order = [conv_tile(c) for c in range(SSM_CT)]
    put("sconv_w", g["ssm_conv_w"][0].reshape(SSM_TAPS, SSM_CT, P)[:, order].transpose(1, 0, 2))
    put("sconv_b", g["ssm_conv_b"][0].reshape(SSM_CT, P)[order])
    put("ssm_d", np.repeat(g["ssm_D"][0], 64))
    put("ssm_nw", g["ssm_norm_w"][0])
    vec[0:SSM_H, VC["dt_bias"]] = g["ssm_dt_bias"][0]
    vec[0:SSM_H, VC["a_log"]] = g["ssm_A_log"][0]
    put("qnorm", g["mla_q_norm_w"][0])
    put("kvnorm", g["mla_kv_norm_w"][0])
    put("g_mix", g["g_mix_2"][0])
    put("pos_k", g["cmp_pos_k_2"][0])
    put("pos_v", g["cmp_pos_v_2"][0])
    put("conv_w", g["conv_w_2"][0].reshape(CONV_TAPS, CONV_CT, P).transpose(1, 0, 2))
    put("conv_b", g["conv_b_2"][0])
    put("ln_g", g["conv_ln_g_2"][0])
    put("ln_b", g["conv_ln_b_2"][0])
    put("b_co", g["b_conv_out_2"][0])
    put("g_ffn", g["g_ffn_2"][0])
    put("fconv_w", g["ffn_conv_w_2"][0].reshape(FF_TAPS, 2, KF, P).transpose(2, 1, 0, 3))
    put("fconv_b", g["ffn_conv_b_2"][0].reshape(2, KF, P).transpose(1, 0, 2))
    put("g_ple", g["g_ple_2"][0])
    put("g_final", g["g_final_2"])
    return vec


def feature_major(a):
    a = np.asarray(a)
    return np.ascontiguousarray(a.T.reshape(-1, P, T).transpose(1, 0, 2))


def kernel(**inputs):
    import concourse.bacc as bacc
    from concourse.bass_utils import run_bass_kernel_spmd

    arrays = {
        "slabs": pack_weights(inputs),
        "vectors": pack_vectors(inputs),
        "shape_consts": shape_constants(),
        "x_fm": feature_major(np.asarray(inputs["x"])[0]),
        "p_fm": feature_major(np.asarray(inputs["p_2"])[0, 0]),
    }
    nc = bacc.Bacc("TRN2", target_bir_lowering=False, num_devices=1)
    aps = [nc.dram_tensor(n, a.shape, mybir.dt.from_np(a.dtype), kind="ExternalInput").ap() for n, a in arrays.items()]
    out = nc.dram_tensor("out_fm", (P, KD, T), mybir.dt.float32, kind="ExternalOutput").ap()
    build(nc, *aps, out)
    r = run_bass_kernel_spmd(nc, [arrays], core_ids=[0])
    y = r.results[0]["out_fm"]
    return np.ascontiguousarray(y.transpose(1, 0, 2).reshape(DM, T).T).reshape(1, T, DM)
```

```python
from contextlib import ExitStack

import numpy as np

import concourse.bass as bass
from concourse import mybir

P = 128
T = 256
TB = T // P
DM = 1024
KD = DM // P
EPS = 1e-6
SSM_DI, SSM_H, SSM_G, SSM_N = 2048, 32, 8, 128
SSM_PAIRS = SSM_DI // P
SSM_CT = (SSM_DI + 2 * SSM_G * SSM_N) // P
SSM_TAPS = 4
MLA_H, MLA_Q, MLA_KV, MLA_R, MLA_D = 16, 384, 256, 64, 128
NSA_G, NSA_J, NSA_D = 2, 4, 64
CMP_LEN, CMP_STRIDE, CMP_HID = 32, 16, 256
N_CMP = (T - CMP_LEN) // CMP_STRIDE + 1
CPAD = 32
CONV_CT, CONV_TAPS = 4, 31
FF = 2816
KF = FF // P
FF_TAPS = 3
NEG = -1e30

BLK = 8
SLAB = BLK * P
RAW_RING, PART_RING = 6, 6
PROJ_BANKS = 3


def weight_jobs():
    r = np.arange
    jobs = []

    def add(name, array, cols, consumer, kind="F", rows=None):
        jobs.append((name, array, np.asarray(cols), rows, kind, consumer))

    pad = lambda cols: np.concatenate([cols, np.full(P - len(cols), -1)])
    zero = SSM_DI
    add("dt", "ssm_in_w", pad(r(SSM_H) + 2 * SSM_DI + 2 * SSM_G * SSM_N), "dve")
    for c in range(SSM_CT):
        ch = conv_tile(c)
        add(f"xbc{c}", "ssm_in_w", zero + ch * P + r(P), "act")
    for j in range(SSM_PAIRS):
        add(f"sz{j}", "ssm_in_w", j * P + r(P), "dve")
    for n in range(KD):
        add(f"so{n}", "ssm_out_w", n * P + r(P), "dve")
    for n in range(2):
        add(f"ckv{n}", "mla_in_w", MLA_Q + n * P + r(P), "act")
    for n in range(3):
        add(f"cq{n}", "mla_in_w", n * P + r(P), "act")
    kr = MLA_Q + MLA_KV + r(MLA_R)
    add("kr", "mla_in_w", np.concatenate([kr, kr]), "act")
    for n in range(4):
        cols = np.concatenate([(4 * n + i) * 2 * P + P + r(P) for i in range(4)])
        add(f"v{n}", "mla_ukv_w", cols, "act", "V")
    for i in range(MLA_H // 2):
        cols = np.concatenate([(2 * i + e) * 192 + P + r(MLA_R) for e in range(2)])
        add(f"qr{i}", "mla_uq_w", cols, "act")
    zc = MLA_Q + MLA_KV + MLA_R

    def head(h):
        add(f"kn{h}", "mla_ukv_w", h * 2 * P + r(P), "act")
        add(f"qn{h}", "mla_uq_w", h * 192 + r(P), "act")

    head(0)
    head(1)
    for h in range(MLA_H):
        if h + 2 < MLA_H:
            head(h + 2)
        add(f"mz{h}", "mla_in_w", zc + h * P + r(P), "dve")
    for n in range(KD):
        add(f"mo{n}", "mla_out_w", n * P + r(P), "dve")
    conv0 = 512 + 768 + 24
    merge0 = conv0 + 1024
    for i in range(CONV_CT):
        add(f"cg{i}", "w_in_2", conv0 + 512 + i * P + r(P), "act")
        add(f"cv{i}", "w_in_2", conv0 + i * P + r(P), "dve")
    for c in range(2):
        add(f"kvc{c}", "w_in_2", 512 + c * P + r(P), "act")
    for j in range(NSA_J):
        cols = np.concatenate([g * 256 + j * 64 + r(64) for g in range(2)])
        add(f"nq{j}", "w_in_2", cols, "act")
    add("ks", "w_in_2", 512 + 2 * P + r(P), "act")
    add("kw", "w_in_2", 512 + 4 * P + r(P), "act")
    add("vsw", "w_in_2", np.concatenate([512 + 3 * P + r(P), 512 + 5 * P + r(P)]), "act", "V")
    add("gates", "w_in_2", pad(512 + 768 + r(24)), "act", "V")
    for n in range(4):
        add(f"mg{n}", "w_in_2", merge0 + n * P + r(P), "act")
    for s in "kv":
        for n in range(2):
            add(f"h{s}{n}", f"w_cmp_{s}1_2", n * P + r(P), "act")
    for n in range(4, 8):
        add(f"mg{n}", "w_in_2", merge0 + n * P + r(P), "act")
    for s in "kv":
        add(f"c{s}", f"w_cmp_{s}2_2", np.concatenate([r(64), r(64)]), "act")
    for n in range(8, 16):
        add(f"mg{n}", "w_in_2", merge0 + n * P + r(P), "act")
    for n in range(KD):
        add(f"yb{n}", "w_conv_out_2", n * P + r(P), "dve")
    rows = np.concatenate([g * 256 + j * 64 + r(64) for j in range(4) for g in range(2)])
    for n in range(KD):
        add(f"ya{n}", "w_o_nsa_2", n * P + r(P), "dve", rows=rows)
    for n in range(KD):
        add(f"wo{n}", "w_out_2", n * P + r(P), "dve")
    for i in range(KF):
        add(f"fg{i}", "w_up_2", i * P + r(P), "act")
        add(f"fv{i}", "w_up_2", FF + i * P + r(P), "act")
    for n in range(KD):
        add(f"fd{n}", "w_down_2", n * P + r(P), "dve")
    for n in range(KD):
        add(f"pg{n}", "w_ple_gate_2", n * P + r(P), "act")
        add(f"pw{n}", "w_ple_2", n * P + r(P), "dve")
    return jobs


def conv_tile(c):
    return c + SSM_PAIRS if c < 16 else c - 16


K_OF = {"ssm_in_w": 8, "ssm_out_w": 16, "mla_in_w": 8, "mla_uq_w": 3, "mla_ukv_w": 2, "mla_out_w": 16,
        "w_in_2": 8, "w_cmp_k1_2": 16, "w_cmp_v1_2": 16, "w_cmp_k2_2": 2, "w_cmp_v2_2": 2, "w_conv_out_2": 4,
        "w_o_nsa_2": 4, "w_out_2": 8, "w_up_2": 8, "w_down_2": KF, "w_ple_gate_2": 8, "w_ple_2": 2}


class Job:

    def __init__(self, name, kind, kt, wide, block, out, consumer, used):
        self.name, self.kind, self.kt, self.wide, self.block, self.out = name, kind, kt, wide, block, out
        self.consumer, self.used = consumer, used
        self.n_out = 1 if kind == "F" else TB
        self.blocks = kt * wide
        self.slab0, self.slab1 = block // BLK, (block + self.blocks - 1) // BLK


def plan():
    jobs, block, out = {}, 0, 0
    used = {"act": 0, "dve": 0}
    freed = []
    done_with = {}
    for name, array, cols, _, kind, consumer in weight_jobs():
        kt, wide = K_OF[array], len(cols) // P
        if wide > 1 and block % wide:
            block += wide - block % wide
        j = jobs[name] = Job(name, kind, kt, wide, block, out, consumer, used[consumer])
        for _ in range(j.n_out):
            used[consumer] += 1
            freed.append((consumer, used[consumer]))
        block += j.blocks
        out += j.n_out
        for s in range(j.slab0, j.slab1 + 1):
            done_with[s] = out
    return jobs, freed, done_with, -(-block // BLK)


def vector_columns():
    at, c = {}, 0
    for name, n in [("norm0", 8), ("norm1", 8), ("final1", 8), ("sconv_w", SSM_CT * SSM_TAPS), ("sconv_b", SSM_CT),
                    ("ssm_d", 16), ("ssm_nw", 16), ("dt_bias", 1), ("a_log", 1), ("qnorm", 3), ("kvnorm", 2),
                    ("g_mix", 8), ("pos_k", 16), ("pos_v", 16), ("conv_w", CONV_CT * CONV_TAPS), ("conv_b", 4),
                    ("ln_g", 4), ("ln_b", 4), ("b_co", 8), ("g_ffn", 8), ("fconv_w", 2 * KF * FF_TAPS),
                    ("fconv_b", 2 * KF), ("g_ple", 8), ("g_final", 8)]:
        at[name] = c
        c += n
    return at, c


CONST_COLS = {"ident": 0, "swap": 128, "mask_s": 256, "mask_t": 384, "cmp_add": 768, "cmp_ok": 896,
              "cos": 1024, "sin": 1280}
N_CONST = 1536


def build(nc, slabs_dram, vec_dram, const_dram, x_dram, p_dram, out_dram):
    f32, f32r, bf16 = mybir.dt.float32, mybir.dt.float32r, mybir.dt.bfloat16
    ALU, ACT, AX = mybir.AluOpType, mybir.ActivationFunctionType, mybir.AxisListType
    jobs, freed, done_with, n_slabs = plan()
    VC, n_vec = vector_columns()
    ctx = ExitStack()
    with ctx:
        def sb(name, shape, dt=f32):
            return ctx.enter_context(nc.sbuf_tensor(name, shape, dt))

        raw = sb("raw", [P, RAW_RING, SLAB])
        wh = sb("wh", [P, PART_RING, SLAB], f32r)
        wl = sb("wl", [P, PART_RING, SLAB], f32r)
        h = sb("h", [P, KD, T])
        sq = sb("sq", [P, KD, T])
        vec = sb("vec", [P, n_vec])
        cst = sb("cst", [P, N_CONST])
        ident_b = sb("ident_b", [P, P], bf16)
        mask_s = sb("mask_s", [P, P], bf16)
        mask_t = sb("mask_t", [P, 3 * P], bf16)
        cmp_add = sb("cmp_add", [P, P], bf16)
        ones = sb("ones", [P, P])
        eps = sb("eps", [P, 1])
        sqsum = sb("sqsum", [P, T])
        lnb = sb("lnb", [P, T])
        rstd = sb("rstd", [P, T])
        ident = cst[:, 0:128]
        swap = cst[:, 128:256]
        cmp_ok = cst[:, 896:1024]
        cos, sin = cst[:, 1024:1280], cst[:, 1280:1536]

        def v(name, i=0, rows=P):
            return vec[0:rows, VC[name] + i:VC[name] + i + 1]

        arena_kb = 105
        arena = sb("arena", [P, arena_kb * 256])
        base = arena_base(nc, arena_kb)
        cursor = [0]

        def phase(start=0):
            cursor[0] = start

        def ar(name, shape, dt=f32):
            n = int(np.prod(shape)) * 4
            t = nc.alloc_sbuf_tensor_at(name, [P] + list(shape), dt, offset=base + cursor[0])
            cursor[0] += -(-n // 32) * 32
            assert cursor[0] <= arena_kb * 1024, (name, cursor[0])
            return t

        HEADS = 4
        phase()
        uh, ul = ar("uh", [KD, T], f32r), ar("ul", [KD, T], f32r)
        after_u = cursor[0]
        ynh, ynl = ar("ynh", [16, T], f32r), ar("ynl", [16, T], f32r)
        xs, bT, cT = ar("xs", [16, T]), ar("bT", [8, T]), ar("cT", [8, T])
        acp = ar("acp", [3 * P], f32r)
        sel = ar("sel", [SSM_H], f32r)
        dtn, nacn = ar("dtn", [TB, SSM_H]), ar("nacn", [TB, SSM_H])
        expa = ar("expa", [1])
        mark = cursor[0]
        sp = ar("sp", [4, T])
        acr, dtT = ar("acr", [3 * P]), ar("dtT", [T])
        cursor[0] = mark
        xdt = ar("xdt", [2, TB, 2, 64])
        gb = ar("gb", [4, T])
        szb = ar("szb", [2, T])
        zb = ar("zb", [T])
        mark = cursor[0]
        sraw = ar("sraw", [4, T + SSM_TAPS - 1])
        scv = ar("scv", [2, T])
        cursor[0] = mark
        eb, mb, cbs = ar("eb", [2, 3 * P]), ar("mb", [HEADS, 3 * P]), ar("cbs", [2, 3 * P])
        yt = ar("yt", [T])

        phase(after_u)
        ogh, ogl = ar("ogh", [16, T], f32r), ar("ogl", [16, T], f32r)
        vn = ar("vn", [TB, MLA_H * P])
        qr, kr = ar("qr", [8, T]), ar("kr", [T])
        kn, qn = ar("kn", [2, T]), ar("qn", [2, T])
        cqh, cql = ar("cqh", [3, T], f32r), ar("cql", [3, T], f32r)
        ckh, ckl = ar("ckh", [2, T], f32r), ar("ckl", [2, T], f32r)
        mx, nm, rs, rr = ar("mx", [2, 2]), ar("nm", [2, 2]), ar("rs", [2, 2]), ar("rr", [2, 2])
        mzb, mze = ar("mzb", [T]), ar("mze", [T])
        ogt = ar("ogt", [2, T])
        mark = cursor[0]
        cqr, ckr = ar("cqr", [3, T]), ar("ckr", [2, T])
        rx, r1, r2 = ar("rx", [2, T]), ar("r1", [T]), ar("r2", [T])
        cursor[0] = mark
        pn, pT = ar("pn", [2, 3 * P]), ar("pT", [2, 3 * P])

        phase(after_u)
        cpad = ar("cpad", [CONV_CT, T + CONV_TAPS - 1])
        ccv = ar("ccv", [CONV_CT, T])
        csg = ar("csg", [2, T])
        nq = ar("nq", [NSA_J, T])
        ksT, kwT = ar("ksT", [T]), ar("kwT", [T])
        vsw = ar("vsw", [TB, 2 * P])
        gates = ar("gates", [TB, 24])
        gm = ar("gm", [16, T])
        cnh, cnl = ar("cnh", [4, T], f32r), ar("cnl", [4, T], f32r)
        kcT, vcT = ar("kcT", [64]), ar("vcT", [P])
        vc = ar("vc", [TB, P])
        nmx, nnm, nrs, nrr = ar("nmx", [2, 2]), ar("nnm", [2, 2]), ar("nrs", [2, 2]), ar("nrr", [2, 2])
        cmx, crs, crr = ar("cmx", [4]), ar("crs", [4]), ar("crr", [4])
        csc, cpn, cpT = ar("csc", [P]), ar("cpn", [P]), ar("cpT", [P])
        yat = ar("yat", [T])
        mark = cursor[0]
        ce = ar("ce", [2, NSA_G, T])
        cx = ar("cx", [2, 16, 64])
        cxh, cxl = ar("cxh", [2, 16, 64], f32r), ar("cxl", [2, 16, 64], f32r)
        hg = ar("hg", [2, 2, 64])
        hgh, hgl = ar("hgh", [2, 2, 64], f32r), ar("hgl", [2, 2, 64], f32r)
        cursor[0] = mark
        mt = ar("mt", [KD, T])
        onh, onl = ar("onh", [4, T], f32r), ar("onl", [4, T], f32r)
        npn, npT = ar("npn", [2, 3 * P]), ar("npT", [2, 3 * P])
        phase()
        mh, ml = ar("mh", [KD, T], f32r), ar("ml", [KD, T], f32r)

        phase(after_u)
        ffh, ffl = ar("ffh", [KF, T], f32r), ar("ffl", [KF, T], f32r)
        fraw = ar("fraw", [4, T + FF_TAPS - 1])
        fcv = ar("fcv", [4, T])
        fge, fgt = ar("fge", [2, T]), ar("fgt", [2, T])
        pin = ar("pin", [2, T])
        ph, pl = ar("ph", [2, T], f32r), ar("pl", [2, T], f32r)
        psg, pt = ar("psg", [2, T]), ar("pt", [T])
        outb = ar("outb", [KD, T])

        psum = [ctx.enter_context(nc.psum_tensor(f"ps{i}", [P, 512], f32)) for i in range(8)]
        PS_TR, PS_S, PS_Y, PS_M = psum[3], [psum[4], psum[5]], psum[6], psum[7]

        sems = {}

        def sem(name):
            if name not in sems:
                sems[name] = ctx.enter_context(nc.semaphore(name))
            return sems[name]

        def wait(eng, name, value):
            if value > 0:
                eng.wait_ge(sem(name), value)

        class Norm:
            count = tiles = parts = sums = 0

            def __init__(self, src, kt, width, gain, ready, hi=None, lo=None, out=None, sqb=None, summed=False):
                self.src, self.kt, self.width, self.gain, self.ready = src, kt, width, gain, ready
                self.hi, self.lo, self.out, self.summed = hi, lo, out, summed
                self.sqb = sqb or (lambda k: sq[:, k, :])
                self.i, self.t0, self.p0, self.s0 = Norm.count, Norm.tiles, Norm.parts, Norm.sums
                Norm.count += 1
                Norm.tiles += kt
                Norm.parts += 0 if out else kt
                Norm.sums += summed

        tile_of = lambda t: (lambda k: t[:, k, :])

        def evac(name, engine="dve"):
            return lambda k: (f"{engine}_evac", freed[jobs[f"{name}{k}"].out][1])

        n_ssm = Norm(tile_of(h), 8, DM, "norm0", lambda k: ("x_in", 16), tile_of(uh), tile_of(ul))
        n_grp = []
        for g in range(SSM_G):
            n_grp.append(Norm((lambda k, g=g: gb[:, (2 * g + k) % 4, :]), 2, 256, ("ssm_nw", 2 * g),
                              (lambda k, g=g: ("gated", 2 * g + k + 1)),
                              (lambda k, g=g: ynh[:, 2 * g + k, :]), (lambda k, g=g: ynl[:, 2 * g + k, :]),
                              sqb=(lambda k, g=g: sq[:, (2 * g + k) % 4, :])))
        n_mla = Norm(tile_of(h), 8, DM, "norm1", evac("so"), tile_of(uh), tile_of(ul), summed=True)
        n_kv = Norm(tile_of(ckr), 2, MLA_KV, "kvnorm", evac("ckv", "act"), tile_of(ckh), tile_of(ckl),
                    sqb=lambda k: sq[:, 4 + k, :])
        n_q = Norm(tile_of(cqr), 3, MLA_Q, "qnorm", evac("cq", "act"), tile_of(cqh), tile_of(cql))
        n_fin1 = Norm(tile_of(h), 8, DM, "final1", evac("mo"), out=tile_of(h), summed=True)
        n_mix = Norm(tile_of(h), 8, DM, "g_mix", lambda k: ("norm_scaled", n_fin1.t0 + k + 1), tile_of(uh), tile_of(ul))
        n_ffn = Norm(tile_of(h), 8, DM, "g_ffn", evac("wo"), tile_of(uh), tile_of(ul), summed=True)
        n_ple = Norm(tile_of(h), 8, DM, "g_ple", evac("fd"), tile_of(uh), tile_of(ul), summed=True)
        n_fin2 = Norm(tile_of(h), 8, DM, "g_final", lambda k: ("ple_added", k + 1), out=tile_of(outb), summed=True)

        def gain(n, k):
            name, at = n.gain if isinstance(n.gain, tuple) else (n.gain, 0)
            return v(name, at + k)

        def rope_job(i):
            return f"qr{i - 1}" if i else "kr"

        block = ctx.enter_context(nc.Block())

        @block.sync
        def _(sp_):
            sp_.dma_start(h[:], x_dram).then_inc(sem("x_in"), 16)
            sp_.dma_start(vec[:], vec_dram).then_inc(sem("vec_in"), 16)
            sp_.dma_start(cst[:], const_dram).then_inc(sem("const_in"), 16)
            for s in range(n_slabs):
                wait(sp_, "wl_ready", s - RAW_RING + 1)
                sp_.dma_start(raw[:, s % RAW_RING, :], slabs_dram[s]).then_inc(sem(f"slab_in{s % RAW_RING}"), 16)
                if s == jobs["fg8"].slab0:
                    wait(sp_, "dve_evac", freed[jobs["wo7"].out][1])
                    sp_.dma_start(pin[:], p_dram).then_inc(sem("p_in"), 16)
            wait(sp_, "norm_scaled", n_fin2.t0 + 8)
            sp_.dma_start(out_dram, outb[:]).then_inc(sem("stored"), 16)
            sp_.wait_ge(sem("stored"), 16)

        @block.gpsimd
        def _(pool):
            for s in range(n_slabs):
                pool.wait_ge(sem("wh_ready"), s + 1)
                nc.gpsimd.tensor_tensor(wl[:, s % PART_RING, :], raw[:, s % RAW_RING, :],
                                        wh[:, s % PART_RING, :].bitcast(f32), ALU.subtract).then_inc(sem("wl_ready"), 1)

        @block.tensor
        def _(pe):
            seen = [0]

            def project(name, hi, lo, ready=None):
                j = jobs[name]
                for o in range(j.out, j.out + j.n_out):
                    if o >= PROJ_BANKS:
                        who, n = freed[o - PROJ_BANKS]
                        wait(pe, f"{who}_evac", n)
                outs = [psum[(j.out + t) % PROJ_BANKS] for t in range(j.n_out)]
                n_cols = j.wide * P
                for k in range(j.kt):
                    if ready:
                        ready(k)
                    b = j.block + k * j.wide
                    s = b // BLK
                    if s >= seen[0]:
                        pe.wait_ge(sem("wl_ready"), s + 1)
                        seen[0] = s + 1
                    c = (b % BLK) * P
                    w_h = wh[:, s % PART_RING, c:c + n_cols]
                    w_l = wl[:, s % PART_RING, c:c + n_cols]
                    for t, o in enumerate(outs):
                        first, last = k == 0, k == j.kt - 1
                        if j.kind == "F":
                            a_h, a_l = hi(k), lo(k)
                            res = o[:, 0:a_h.shape[-1]]
                            nc.tensor.matmul(res, w_h, a_h, start=first, stop=False)
                            nc.tensor.matmul(res, w_h, a_l, start=False, stop=False)
                            ins = nc.tensor.matmul(res, w_l, a_h, start=False, stop=last)
                        else:
                            a_h, a_l = hi(k)[:, t * P:(t + 1) * P], lo(k)[:, t * P:(t + 1) * P]
                            res = o[:, 0:n_cols]
                            nc.tensor.matmul(res, a_h, w_h, start=first, stop=False)
                            nc.tensor.matmul(res, a_h, w_l, start=False, stop=False)
                            ins = nc.tensor.matmul(res, a_l, w_h, start=False, stop=last)
                        if last:
                            ins.then_inc(sem("proj_done"), 1)

            def norm(n, bank_free=()):
                for name, value in bank_free:
                    wait(pe, name, value)
                if n.i:
                    wait(pe, "norm_ln", n.i)
                if n.summed:
                    pe.wait_ge(sem("norm_acc"), n.s0 + 1)
                    nc.tensor.matmul(PS_M[:, 0:T], ones[:], sqsum[:], start=True, stop=True).then_inc(sem("norm_sum"), 1)
                    return
                for k in range(n.kt):
                    wait(pe, "norm_sq", n.t0 + k + 1)
                    ins = nc.tensor.matmul(PS_M[:, 0:T], ones[:], n.sqb(k), start=k == 0, stop=k == n.kt - 1)
                ins.then_inc(sem("norm_sum"), 1)

            def parts_ready(n):
                return lambda k: wait(pe, "norm_lo", n.p0 + k + 1)

            u = lambda k: uh[:, k, :]
            u_lo = lambda k: ul[:, k, :]

            pe.wait_ge(sem("memset"), 3)
            norm(n_ssm)
            project("dt", u, u_lo, parts_ready(n_ssm))
            for c in range(SSM_CT):
                project(f"xbc{c}", u, u_lo)
                if c == 9:
                    pe.wait_ge(sem("dt_scan"), 2)
                    pe.wait_ge(sem("masks"), 1)
                    for i, src in enumerate((dtT, acr)):
                        for b in range(TB):
                            o = PS_TR[:, (2 * i + b) * SSM_H:(2 * i + b + 1) * SSM_H]
                            ins = nc.tensor.transpose(o, src[0:SSM_H, b * P:(b + 1) * P], ident[0:SSM_H, 0:SSM_H])
                    ins.then_inc(sem("dt_tr"), 1)

            def x_transpose(j):
                wait(pe, "ssm_silu", 16 + j + 1)
                wait(pe, "xdt", j)
                if j == 0:
                    wait(pe, "dt_tok", 2)
                for b in range(TB):
                    ins = nc.tensor.transpose(PS_TR[:, b * P:(b + 1) * P], xs[:, j, b * P:(b + 1) * P], ident)
                ins.then_inc(sem("x_tr"), 1)

            def decay(hd):
                wait(pe, "decay_exp", hd - 1)
                o = PS_S[hd % 2][:, 0:3 * P]
                pick = sel[0:2 * SSM_H, hd:hd + 1].broadcast_to([2 * SSM_H, P])
                nc.tensor.matmul(o, pick, acp[0:2 * SSM_H, :], start=True, stop=False)
                nc.tensor.matmul(o, ident_b[:], mask_t[:], start=False, stop=True).then_inc(sem("decay"), 1)

            def cb_scores(g):
                wait(pe, "cb_evac", g)
                wait(pe, "norm_ln", n_ssm.i + 1 + max(0, g - 1))
                nc.tensor.matmul(PS_M[:, 0:T], bT[:, g, 0:P], cT[:, g, :], start=True, stop=True)
                nc.tensor.matmul(PS_M[:, T:T + P], bT[:, g, P:T], cT[:, g, P:T], start=True, stop=True,
                                 skip_group_check=True).then_inc(sem("cb"), 1)

            def head_out(hd):
                j, e = divmod(hd, 2)
                wait(pe, "decayed", hd + 1)
                wait(pe, "xdt", j + 1)
                if e == 0:
                    wait(pe, "y_read", j)
                o = PS_Y[64 * e:64 * e + 64, :]
                m = mb[:, hd % HEADS, :]
                nc.tensor.matmul(o[:, 0:T], xdt[:, j % 2, 0, e, :], m[:, 0:T], start=True, stop=False)
                nc.tensor.matmul(o[:, P:T], xdt[:, j % 2, 1, e, :], m[:, T:T + P], start=False, stop=True)\
                    .then_inc(sem("y"), 1)

            wait(pe, "decay_parts", 1)
            x_transpose(0)
            cb_scores(0)
            decay(0)
            decay(1)
            for j in range(SSM_PAIRS):
                project(f"sz{j}", u, u_lo)
                if j % 2 == 0 and j:
                    norm(n_grp[j // 2 - 1], [("cb_evac", j // 2 + 1)])
                if j + 1 < SSM_PAIRS:
                    x_transpose(j + 1)
                    decay(2 * j + 2)
                    decay(2 * j + 3)
                    if j % 2:
                        cb_scores((j + 1) // 2)
                head_out(2 * j)
                head_out(2 * j + 1)
            norm(n_grp[7], [("cb_evac", 8)])
            for n in range(KD):
                project(f"so{n}", tile_of(ynh), tile_of(ynl),
                        (lambda k: wait(pe, "norm_lo", n_grp[0].p0 + k + 1)) if n == 0 else None)

            norm(n_mla)
            for i, n in enumerate(["ckv0", "ckv1", "cq0", "cq1", "cq2", "kr"]):
                project(n, u, u_lo, parts_ready(n_mla) if i == 0 else None)
                if n == "cq1":
                    norm(n_kv)
            norm(n_q)

            def rope_swap(i):
                pe.wait_ge(sem("act_evac"), freed[jobs[rope_job(i)].out][1])
                wait(pe, "rope_swapped_read", i)
                if i == 0:
                    wait(pe, "xdt", 16)
                nc.tensor.matmul(PS_TR[:, 0:T], swap, rx[:, i % 2, :], start=True, stop=True)\
                    .then_inc(sem("rope_swap"), 1)

            rope_swap(0)
            for n in range(4):
                project(f"v{n}", tile_of(ckh), tile_of(ckl), parts_ready(n_kv) if n == 0 else None)
            for i in range(8):
                project(f"qr{i}", tile_of(cqh), tile_of(cql), parts_ready(n_q) if i == 0 else None)
                if i:
                    rope_swap(i)
            rope_swap(8)

            def scores(hd):
                wait(pe, "act_evac", freed[jobs[f"qn{hd}"].out][1])
                wait(pe, "prob", hd - 1)
                o = PS_S[hd % 2]
                e, i = hd % 2, hd // 2
                rows = slice(64 * e, 64 * e + 64)
                if hd == 0:
                    wait(pe, "decay_exp", SSM_H)
                    wait(pe, "rope_out", 9)
                for b in range(TB):
                    cols = slice(0, P) if b == 0 else slice(P, 3 * P)
                    q_, nk = slice(b * P, (b + 1) * P), (b + 1) * P
                    nc.tensor.matmul(o[:, cols], qn[:, hd % 2, q_], kn[:, hd % 2, 0:nk], start=b == 0, stop=False,
                                     skip_group_check=True)
                    nc.tensor.matmul(o[:, cols], qr[rows, i, q_], kr[rows, 0:nk], start=False, stop=False,
                                     skip_group_check=True)
                    d = o[:, 0:P] if b == 0 else o[:, 2 * P:3 * P]
                    ins = nc.tensor.matmul(d, ident_b[:], mask_s[:], start=False, stop=True, skip_group_check=True)
                ins.then_inc(sem("score"), 1)

            def prob_transpose(hd):
                wait(pe, "prob_norm", hd + 1)
                wait(pe, "prob_tr_read", hd)
                if hd == 0:
                    wait(pe, "rope_swapped_read", 9)
                for c in range(3):
                    ins = nc.tensor.transpose(PS_TR[:, c * P:(c + 1) * P], pn[:, hd % 2, c * P:(c + 1) * P], ident)
                ins.then_inc(sem("prob_tr"), 1)

            def values(hd):
                wait(pe, "prob_tr_read", hd + 1)
                wait(pe, "att_read", hd)
                if hd == 0:
                    wait(pe, "y_read", 16)
                nc.tensor.matmul(PS_Y[:, 0:T], vn[:, 0, hd * P:(hd + 1) * P], pT[:, hd % 2, 0:T], start=True, stop=False)
                nc.tensor.matmul(PS_Y[:, P:T], vn[:, 1, hd * P:(hd + 1) * P], pT[:, hd % 2, T:T + P],
                                 start=False, stop=True).then_inc(sem("att"), 1)

            def head_proj(hd):
                project(f"kn{hd}", tile_of(ckh), tile_of(ckl))
                project(f"qn{hd}", tile_of(cqh), tile_of(cql))

            head_proj(0)
            scores(0)
            head_proj(1)
            scores(1)
            prob_transpose(0)
            for hd in range(MLA_H):
                if hd + 2 < MLA_H:
                    head_proj(hd + 2)
                    scores(hd + 2)
                project(f"mz{hd}", u, u_lo)
                if hd + 1 < MLA_H:
                    prob_transpose(hd + 1)
                values(hd)
            for n in range(KD):
                project(f"mo{n}", tile_of(ogh), tile_of(ogl), (lambda k: wait(pe, "att_lo", k + 1)) if n == 0 else None)

            norm(n_fin1)
            norm(n_mix)
            for i in range(CONV_CT):
                project(f"cg{i}", u, u_lo, parts_ready(n_mix) if i == 0 else None)
                project(f"cv{i}", u, u_lo)
            for n in ["kvc0", "kvc1", "nq0", "nq1", "nq2", "nq3", "ks", "kw", "vsw", "gates", "mg0", "mg1", "mg2", "mg3"]:
                project(n, u, u_lo)
            for i, s in enumerate("kv"):
                for n in range(2):
                    project(f"h{s}{n}", (lambda k, i=i: cxh[:, i, k, :]), (lambda k, i=i: cxl[:, i, k, :]),
                            (lambda k, i=i: wait(pe, "cmp_lo", i + 1)) if n == 0 else None)
            for n in range(4, 8):
                project(f"mg{n}", u, u_lo)
            for i, s in enumerate("kv"):
                project(f"c{s}", (lambda k, i=i: hgh[:, i, k, :]), (lambda k, i=i: hgl[:, i, k, :]),
                        (lambda k, i=i: wait(pe, "cmp_hid_lo", i + 1)))
            for n in range(8, 16):
                project(f"mg{n}", u, u_lo)
            pe.wait_ge(sem("act_evac"), freed[jobs["cv"].out][1])
            nc.tensor.transpose(PS_TR[:, 0:P], vcT[:, :], ident).then_inc(sem("vc_tr"), 1)
            wait(pe, "conv_done", CONV_CT)
            wait(pe, "norm_ln", n_mix.i + 1)
            for k in range(CONV_CT):
                ins = nc.tensor.matmul(PS_M[:, 0:T], ones[:], ccv[:, k, :], start=k == 0, stop=k == 3)
            ins.then_inc(sem("ln_sum"), 1)
            wait(pe, "ln_sq", 1)
            for k in range(CONV_CT):
                ins = nc.tensor.matmul(PS_M[:, 0:T], ones[:], sq[:, k, :], start=k == 0, stop=k == 3)
            ins.then_inc(sem("ln_sum"), 1)

            def cmp_scores(j):
                wait(pe, "cmp_read", j)
                wait(pe, "ln_ln", 1)
                for b in range(TB):
                    nc.tensor.matmul(PS_M[:, b * 64:b * 64 + 64], nq[:, j, b * P:(b + 1) * P], kcT[:], start=b == 0,
                                     stop=False, skip_group_check=True)
                nc.tensor.matmul(PS_M[:, 0:P], ident_b[:], cmp_add[:], start=False, stop=True,
                                 skip_group_check=True).then_inc(sem("cmp_score"), 1)

            def unit_scores(x):
                j, g, ty = x // 4, x // 2 % 2, x % 2
                wait(pe, "nprob", x - 1)
                if x == 0:
                    wait(pe, "prob", MLA_H)
                o, key, rows = PS_S[x % 2], (ksT, kwT)[ty], slice(64 * g, 64 * g + 64)
                for b in range(TB):
                    cols = slice(0, P) if b == 0 else slice(P, 3 * P)
                    nc.tensor.matmul(o[:, cols], nq[rows, j, b * P:(b + 1) * P], key[rows, 0:(b + 1) * P],
                                     start=b == 0, stop=False, skip_group_check=True)
                    d = o[:, 0:P] if b == 0 else o[:, 2 * P:3 * P]
                    ins = nc.tensor.matmul(d, ident_b[:], mask_s[:], start=False, stop=True, skip_group_check=True)
                ins.then_inc(sem("nscore"), 1)

            def unit_transpose(x):
                j, g, ty = x // 4, x // 2 % 2, x % 2
                wait(pe, "nprob_norm", x + 1)
                wait(pe, "nprob_tr_read", x)
                wait(pe, "cmp_tr_read", (x + 1) // 4)
                if x == 0:
                    wait(pe, "vc_read", 1)
                for c in range(3):
                    ins = nc.tensor.transpose(PS_TR[:, c * P:(c + 1) * P], npn[:, x % 2, c * P:(c + 1) * P], ident)
                ins.then_inc(sem("nprob_tr"), 1)

            def unit_accumulate(x):
                j, g, ty = x // 4, x // 2 % 2, x % 2
                wait(pe, "nprob_tr_read", x + 1)
                if x % 4 == 0:
                    wait(pe, "natt_lo", j)
                    wait(pe, "att_read", MLA_H)
                o = PS_Y[64 * g:64 * g + 64, :]
                vcol = slice(ty * P + 64 * g, ty * P + 64 * g + 64)
                nc.tensor.matmul(o[:, 0:T], vsw[:, 0, vcol], npT[:, x % 2, 0:T], start=ty == 0, stop=False,
                                 skip_group_check=True)
                nc.tensor.matmul(o[:, P:T], vsw[:, 1, vcol], npT[:, x % 2, T:T + P], start=False, stop=False,
                                 skip_group_check=True).then_inc(sem("nvalue"), 1)

            def cmp_transpose(j):
                wait(pe, "cmp_prob", j + 1)
                wait(pe, "nprob_tr_read", 4 * j + 3)
                nc.tensor.transpose(PS_TR[:, 0:P], cpn[:, :], ident).then_inc(sem("cmp_tr"), 1)

            def cmp_values(j):
                wait(pe, "cmp_tr_read", j + 1)
                for b in range(TB):
                    ins = nc.tensor.matmul(PS_Y[:, b * P:(b + 1) * P], vc[:, b, :], cpT[:], start=False, stop=b == 1,
                                           skip_group_check=True)
                ins.then_inc(sem("natt"), 1)

            unit_scores(0)
            unit_scores(1)
            unit_transpose(0)
            for x in range(16):
                if x % 4 == 0:
                    cmp_scores(x // 4)
                if x + 2 < 16:
                    unit_scores(x + 2)
                if x % 2 == 0:
                    project(f"yb{x // 2}", tile_of(cnh), tile_of(cnl),
                            (lambda k: wait(pe, "conv_lo", k + 1)) if x == 0 else None)
                if x % 4 == 2:
                    cmp_transpose(x // 4)
                if x + 1 < 16:
                    unit_transpose(x + 1)
                unit_accumulate(x)
                if x % 4 == 3:
                    cmp_values(x // 4)
            for n in range(KD):
                project(f"ya{n}", tile_of(onh), tile_of(onl), (lambda k: wait(pe, "natt_lo", k + 1)) if n == 0 else None)
            for n in range(KD):
                project(f"wo{n}", tile_of(mh), tile_of(ml), (lambda k: wait(pe, "merge_lo", k + 1)) if n == 0 else None)

            norm(n_ffn)
            for i in range(KF):
                project(f"fg{i}", u, u_lo, parts_ready(n_ffn) if i == 0 else None)
                project(f"fv{i}", u, u_lo)
            for n in range(KD):
                project(f"fd{n}", tile_of(ffh), tile_of(ffl), (lambda k: wait(pe, "ff_lo", k + 1)) if n == 0 else None)

            norm(n_ple)
            for n in range(KD):
                project(f"pg{n}", u, u_lo, parts_ready(n_ple) if n == 0 else None)
                project(f"pw{n}", tile_of(ph), tile_of(pl), (lambda k: wait(pe, "p_lo", 1)) if n == 0 else None)
            norm(n_fin2)

        @block.scalar
        def _(act):
            split = [0]
            chain = [0]

            def link(ins):
                chain[0] += 1
                ins.then_inc(sem("act_chain"), 1)
                act.wait_ge(sem("act_chain"), chain[0])

            def feed(name):
                last = min(jobs[name].slab0 + PART_RING - 1, n_slabs - 1)
                while split[0] <= last:
                    s = split[0]
                    act.wait_ge(sem(f"slab_in{s % RAW_RING}"), 16 * (s // RAW_RING + 1))
                    if s >= PART_RING:
                        act.wait_ge(sem("proj_done"), done_with[s - PART_RING])
                    nc.scalar.activation(wh[:, s % PART_RING, :], raw[:, s % RAW_RING, :], ACT.Copy)\
                        .then_inc(sem("wh_ready"), 1)
                    split[0] += 1

            def output(name, t=0):
                feed(name)
                o = jobs[name].out + t
                act.wait_ge(sem("proj_done"), o + 1)
                return psum[o % PROJ_BANKS]

            def square(n, k):
                wait(act, *n.ready(k))
                nc.scalar.activation(n.sqb(k), n.src(k), ACT.Square).then_inc(sem("norm_sq"), 1)

            def squares(n):
                for k in range(n.kt):
                    square(n, k)

            def feed_and_square(prefix, n):
                for k in range(KD):
                    feed(f"{prefix}{k}")
                    if k:
                        square(n, k - 1)
                square(n, KD - 1)

            def inverse_root(n):
                act.wait_ge(sem("norm_sum"), n.i + 1)
                wait(act, "norm_scaled", n.t0)
                nc.scalar.activation(lnb[:], PS_M[:, 0:T], ACT.Ln, bias=eps[:], scale=1.0 / n.width)\
                    .then_inc(sem("norm_ln"), 1)
                act.wait_ge(sem("norm_ln"), n.i + 1)
                nc.scalar.activation(rstd[:], lnb[:], ACT.Exp, scale=-0.5).then_inc(sem("norm_root"), 1)

            def high_parts(n):
                for k in range(n.kt):
                    act.wait_ge(sem("norm_scaled"), n.t0 + k + 1)
                    nc.scalar.activation(n.hi(k), n.sqb(k), ACT.Copy).then_inc(sem("norm_hi"), 1)

            squares(n_ssm)
            act.wait_ge(sem("memset"), 3)
            inverse_root(n_ssm)
            feed("dt")
            high_parts(n_ssm)
            act.wait_ge(sem("const_in"), 16)
            nc.scalar.activation(ident_b[:], ident, ACT.Copy)
            nc.scalar.activation(mask_s[:], cst[:, 256:384], ACT.Copy)
            nc.scalar.activation(mask_t[:], cst[:, 384:768], ACT.Copy)
            for e in range(2):
                r_ = slice(SSM_H * e, SSM_H * e + SSM_H)
                nc.scalar.activation(sel[r_, :], cst[r_, r_], ACT.Copy)
            nc.scalar.activation(cmp_add[:], cst[:, 768:896], ACT.Copy).then_inc(sem("masks"), 1)
            act.wait_ge(sem("vec_in"), 16)
            nc.scalar.activation(expa[0:SSM_H, :], v("a_log", 0, SSM_H), ACT.Exp).then_inc(sem("exp_a"), 1)
            act.wait_ge(sem("dt_step"), 1)
            link(nc.scalar.activation(sp[0:SSM_H, 2, :], sp[0:SSM_H, 1, :], ACT.Exp))
            nc.scalar.activation(sp[0:SSM_H, 3, :], sp[0:SSM_H, 2, :], ACT.Ln, bias=1.0).then_inc(sem("dt_log"), 1)

            def ssm_silu(c):
                act.wait_ge(sem("ssm_conv"), c + 1)
                dst = bT[:, c, :] if c < 8 else cT[:, c - 8, :] if c < 16 else xs[:, c - 16, :]
                nc.scalar.activation(dst, scv[:, c % 2, :], ACT.Silu, bias=v("sconv_b", c)).then_inc(sem("ssm_silu"), 1)

            for c in range(SSM_CT):
                o = output(f"xbc{c}")
                wait(act, "ssm_conv", c - 3)
                nc.scalar.activation(sraw[:, c % 4, SSM_TAPS - 1:], o[:, 0:T], ACT.Copy).then_inc(sem("act_evac"), 1)
                if c:
                    ssm_silu(c - 1)
                if c == 12:
                    act.wait_ge(sem("dt_scan"), 3)
                    nc.scalar.activation(acp[0:SSM_H, :], acr[0:SSM_H, :], ACT.Copy).then_inc(sem("decay_hi"), 1)
            ssm_silu(SSM_CT - 1)

            def cb_evac(g):
                act.wait_ge(sem("cb"), g + 1)
                wait(act, "decayed", 4 * (g - 1))
                nc.scalar.activation(cbs[:, g % 2, :], PS_M[:, 0:3 * P], ACT.Copy).then_inc(sem("cb_evac"), 1)

            def decay_exp(hd):
                act.wait_ge(sem("decay"), hd + 1)
                wait(act, "decayed", hd - 1)
                o = PS_S[hd % 2]
                nc.scalar.activation(eb[:, hd % 2, 0:T], o[:, 0:T], ACT.Exp, bias=nacn[:, 0, hd:hd + 1])
                nc.scalar.activation(eb[:, hd % 2, T:T + P], o[:, T:T + P], ACT.Exp, bias=nacn[:, 1, hd:hd + 1])\
                    .then_inc(sem("decay_exp"), 1)

            feed("sz0")
            act.wait_ge(sem("dt_tok"), 2)
            act.wait_ge(sem("ssm_silu"), SSM_CT)
            cb_evac(0)
            decay_exp(0)
            decay_exp(1)
            for j in range(SSM_PAIRS):
                o = output(f"sz{j}")
                wait(act, "dve_evac", freed[jobs[f"sz{j}"].out][1] - 1)
                nc.scalar.activation(zb[:], o[:, 0:T], ACT.Tanh, scale=0.5).then_inc(sem("z_tanh"), 1)
                if j % 2 == 0 and j:
                    inverse_root(n_grp[j // 2 - 1])
                if j + 1 < SSM_PAIRS:
                    decay_exp(2 * j + 2)
                    decay_exp(2 * j + 3)
                    if j % 2:
                        cb_evac((j + 1) // 2)
                if j % 2 == 0 and j:
                    high_parts(n_grp[j // 2 - 1])
                square(n_grp[j // 2], j % 2)
            feed("so0")
            inverse_root(n_grp[7])
            high_parts(n_grp[7])
            feed_and_square("so", n_mla)

            inverse_root(n_mla)
            feed("ckv0")
            high_parts(n_mla)

            def copy_out(name, dst):
                o = output(name)
                nc.scalar.activation(dst, o[:, 0:T], ACT.Copy).then_inc(sem("act_evac"), 1)

            for n in range(2):
                copy_out(f"ckv{n}", ckr[:, n, :])
            squares(n_kv)
            copy_out("cq0", cqr[:, 0, :])
            copy_out("cq1", cqr[:, 1, :])
            feed("kr")
            inverse_root(n_kv)
            copy_out("cq2", cqr[:, 2, :])
            high_parts(n_kv)
            squares(n_q)
            copy_out("kr", rx[:, 0, :])
            feed("v0")
            inverse_root(n_q)
            high_parts(n_q)
            for n in range(4):
                for t in range(TB):
                    o = output(f"v{n}", t)
                    nc.scalar.activation(vn[:, t, n * 512:(n + 1) * 512], o[:, :], ACT.Copy).then_inc(sem("act_evac"), 1)
            for i in range(8):
                o = output(f"qr{i}")
                wait(act, "rope_out", i)
                nc.scalar.activation(rx[:, (i + 1) % 2, :], o[:, 0:T], ACT.Copy).then_inc(sem("act_evac"), 1)

            def evac_head(hd):
                o = output(f"kn{hd}")
                wait(act, "score", hd - 1)
                nc.scalar.activation(kn[:, hd % 2, :], o[:, 0:T], ACT.Copy).then_inc(sem("act_evac"), 1)
                o = output(f"qn{hd}")
                nc.scalar.activation(qn[:, hd % 2, :], o[:, 0:T], ACT.Copy).then_inc(sem("act_evac"), 1)

            def prob(hd):
                act.wait_ge(sem("max"), hd + 1)
                wait(act, "prob_tr", hd - 1)
                o, s = PS_S[hd % 2], (MLA_D + MLA_R) ** -0.5
                for b, c in enumerate((slice(0, P), slice(P, 3 * P))):
                    ins = nc.scalar.activation(pn[:, hd % 2, c], o[:, c], ACT.Exp, bias=nm[:, hd % 2, b:b + 1], scale=s,
                                               accum_out=rs[:, hd % 2, b:b + 1])
                ins.then_inc(sem("prob"), 1)

            def prob_evac(hd):
                act.wait_ge(sem("prob_tr"), hd + 1)
                wait(act, "att", hd - 1)
                nc.scalar.activation(pT[:, hd % 2, :], PS_TR[:, 0:3 * P], ACT.Copy).then_inc(sem("prob_tr_read"), 1)

            evac_head(0)
            evac_head(1)
            act.wait_ge(sem("rope_out"), 9)
            prob(0)
            prob(1)
            prob_evac(0)
            for hd in range(MLA_H):
                if hd + 2 < MLA_H:
                    evac_head(hd + 2)
                o = output(f"mz{hd}")
                wait(act, "dve_evac", freed[jobs[f"mz{hd}"].out][1] - 1)
                nc.scalar.activation(mze[:], o[:, 0:T], ACT.Tanh, scale=0.5).then_inc(sem("mz_tanh"), 1)
                if hd + 1 < MLA_H:
                    prob_evac(hd + 1)
                if hd + 2 < MLA_H:
                    prob(hd + 2)
                act.wait_ge(sem("att_read"), hd + 1)
                nc.scalar.activation(ogh[:, hd, :], ogt[:, hd % 2, :], ACT.Copy).then_inc(sem("att_hi"), 1)
            feed_and_square("mo", n_fin1)

            inverse_root(n_fin1)
            feed("cg0")
            squares(n_mix)
            inverse_root(n_mix)
            high_parts(n_mix)
            for i in range(CONV_CT):
                o = output(f"cg{i}")
                wait(act, "dve_evac", freed[jobs[f"cv{i}"].out][1] - 2)
                nc.scalar.activation(csg[:, i % 2, :], o[:, 0:T], ACT.Sigmoid).then_inc(sem("act_evac"), 1)
            for i in range(2):
                o = output(f"kvc{i}")
                if i == 0:
                    act.wait_ge(sem("cx_zero"), 1)
                for g in range(NSA_G):
                    r_ = slice(64 * g, 64 * g + 64)
                    nc.scalar.activation(ce[0:64, i, g, :], o[r_, 0:T], ACT.Copy)
                    ins = nc.scalar.activation(ce[64:128, i, g, 0:T - 1], o[r_, 1:T], ACT.Copy)
                ins.then_inc(sem("act_evac"), 1)
            for j in range(NSA_J):
                o = output(f"nq{j}")
                nc.scalar.activation(nq[:, j, :], o[:, 0:T], ACT.Copy).then_inc(sem("act_evac"), 1)
            for name, dst in (("ks", ksT), ("kw", kwT)):
                o = output(name)
                nc.scalar.activation(dst[:], o[:, 0:T], ACT.Copy).then_inc(sem("act_evac"), 1)
            for t in range(TB):
                o = output("vsw", t)
                nc.scalar.activation(vsw[:, t, :], o[:, 0:T], ACT.Copy).then_inc(sem("act_evac"), 1)
            for t in range(TB):
                o = output("gates", t)
                nc.scalar.activation(gates[:, t, :], o[:, 0:24], ACT.Sigmoid).then_inc(sem("act_evac"), 1)
            for n in range(4):
                o = output(f"mg{n}")
                nc.scalar.activation(gm[:, n, :], o[:, 0:T], ACT.Sigmoid).then_inc(sem("act_evac"), 1)
            for i in range(2):
                act.wait_ge(sem("cmp_x"), i + 1)
                nc.scalar.activation(cxh[:, i, :, :], cx[:, i, :, :], ACT.Copy).then_inc(sem("cmp_hi"), 1)
            for i, s in enumerate("kv"):
                for n in range(2):
                    o = output(f"h{s}{n}")
                    nc.scalar.activation(hg[:, i, n, :], o[:, 0:64], ACT.Gelu_apprx_tanh).then_inc(sem("act_evac"), 1)
                act.wait_ge(sem("act_evac"), freed[jobs[f"h{s}1"].out][1])
                nc.scalar.activation(hgh[:, i, :, :], hg[:, i, :, :], ACT.Copy).then_inc(sem("cmp_hid_hi"), 1)
            for n in range(4, 8):
                o = output(f"mg{n}")
                nc.scalar.activation(gm[:, n, :], o[:, 0:T], ACT.Sigmoid).then_inc(sem("act_evac"), 1)
            o = output("ck")
            act.wait_ge(sem("vc_zero"), 2)
            for g in range(NSA_G):
                r_, c_ = slice(64 * g, 64 * g + 64), slice(CPAD * g, CPAD * g + CPAD)
                ins = nc.scalar.activation(kcT[r_, c_], o[r_, c_], ACT.Copy)
            ins.then_inc(sem("act_evac"), 1)
            o = output("cv")
            nc.scalar.activation(vcT[:, 0:64], o[:, 0:64], ACT.Copy)
            nc.scalar.activation(vcT[:, 64:128], o[:, 0:64], ACT.Copy).then_inc(sem("act_evac"), 1)
            for n in range(8, 16):
                o = output(f"mg{n}")
                nc.scalar.activation(gm[:, n, :], o[:, 0:T], ACT.Sigmoid).then_inc(sem("act_evac"), 1)
            act.wait_ge(sem("vc_tr"), 1)
            for b in range(TB):
                for g in range(NSA_G):
                    r_ = slice((b * 2 + g) * CPAD, (b * 2 + g + 1) * CPAD)
                    ins = nc.scalar.activation(vc[r_, b, 64 * g:64 * g + 64], PS_TR[r_, 64 * g:64 * g + 64], ACT.Copy)
            ins.then_inc(sem("vc_read"), 1)
            act.wait_ge(sem("ln_centred"), 1)
            nc.scalar.activation(sq[:, 0:4, :], ccv[:], ACT.Square).then_inc(sem("ln_sq"), 1)
            act.wait_ge(sem("ln_sum"), 2)
            nc.scalar.activation(lnb[:], PS_M[:, 0:T], ACT.Ln, bias=eps[:], scale=1.0 / (CONV_CT * P))\
                .then_inc(sem("ln_ln"), 1)
            act.wait_ge(sem("ln_ln"), 1)
            nc.scalar.activation(rstd[:], lnb[:], ACT.Exp, scale=-0.5).then_inc(sem("ln_root"), 1)
            for k in range(CONV_CT):
                act.wait_ge(sem("ln_scaled"), k + 1)
                nc.scalar.activation(sq[:, 4 + k, :], sq[:, k, :], ACT.Silu, bias=v("ln_b", k)).then_inc(sem("conv_act"), 1)
            for k in range(CONV_CT):
                act.wait_ge(sem("conv_act"), k + 1)
                nc.scalar.activation(cnh[:, k, :], sq[:, 4 + k, :], ACT.Copy).then_inc(sem("conv_hi"), 1)

            def nprob(x):
                act.wait_ge(sem("nmax"), x + 1)
                wait(act, "nprob_tr", x - 1)
                o = PS_S[x % 2]
                for b, c in enumerate((slice(0, P), slice(P, 3 * P))):
                    ins = nc.scalar.activation(npn[:, x % 2, c], o[:, c], ACT.Exp, bias=nnm[:, x % 2, b:b + 1],
                                               scale=NSA_D ** -0.5, accum_out=nrs[:, x % 2, b:b + 1])
                ins.then_inc(sem("nprob"), 1)

            def nprob_evac(x):
                act.wait_ge(sem("nprob_tr"), x + 1)
                wait(act, "nvalue", x - 1)
                nc.scalar.activation(npT[:, x % 2, :], PS_TR[:, 0:3 * P], ACT.Copy).then_inc(sem("nprob_tr_read"), 1)

            nprob(0)
            nprob(1)
            nprob_evac(0)
            for x in range(16):
                if x % 4 == 0:
                    act.wait_ge(sem("cmp_read"), x // 4 + 1)
                    nc.scalar.activation(cpn[:], csc[:], ACT.Exp, scale=NSA_D ** -0.5).then_inc(sem("cmp_exp"), 1)
                if x % 2 == 0:
                    feed(f"yb{x // 2}")
                if x + 2 < 16:
                    nprob(x + 2)
                j = x // 4
                if x % 4 == 2:
                    act.wait_ge(sem("cmp_tr"), j + 1)
                    wait(act, "natt", j)
                    nc.scalar.activation(cpT[:], PS_TR[:, 0:P], ACT.Copy).then_inc(sem("cmp_tr_read"), 1)
                if x + 1 < 16:
                    nprob_evac(x + 1)
                if x % 4 == 3:
                    act.wait_ge(sem("natt"), j + 1)
                    nc.scalar.activation(onh[:, j, :], PS_Y[:, 0:T], ACT.Copy).then_inc(sem("natt_hi"), 1)
            for n in range(KD):
                feed(f"ya{n}")
                act.wait_ge(sem("merged"), n + 1)
                nc.scalar.activation(mh[:, n, :], mt[:, n, :], ACT.Copy).then_inc(sem("merge_hi"), 1)
            feed_and_square("wo", n_ffn)

            inverse_root(n_ffn)
            feed("fg0")
            high_parts(n_ffn)

            def ff_act(i):
                act.wait_ge(sem("ff_conv"), 2 * i + 1)
                wait(act, "ff_gated", i - 1)
                nc.scalar.activation(fge[:, i % 2, :], fcv[:, 2 * i % 4, :], ACT.Gelu_apprx_tanh, bias=v("fconv_b", 2 * i))\
                    .then_inc(sem("ff_gelu"), 1)

            def ff_high(i):
                act.wait_ge(sem("ff_gated"), i + 1)
                nc.scalar.activation(ffh[:, i, :], fgt[:, i % 2, :], ACT.Copy).then_inc(sem("ff_hi"), 1)

            for i in range(KF):
                for e, s in enumerate("gv"):
                    o = output(f"f{s}{i}")
                    if i == 0:
                        act.wait_ge(sem("ff_pad"), 1)
                    wait(act, "ff_conv", 2 * i + e - 3)
                    nc.scalar.activation(fraw[:, (2 * i + e) % 4, FF_TAPS - 1:], o[:, 0:T], ACT.Copy)\
                        .then_inc(sem("act_evac"), 1)
                if i:
                    ff_high(i - 1)
                ff_act(i)
                if i == KF - 4:
                    act.wait_ge(sem("p_in"), 16)
                    nc.scalar.activation(ph[:], pin[:], ACT.Copy).then_inc(sem("p_hi"), 1)
            ff_high(KF - 1)
            feed_and_square("fd", n_ple)

            inverse_root(n_ple)
            feed("pg0")
            high_parts(n_ple)
            for n in range(KD):
                o = output(f"pg{n}")
                wait(act, "ple_added", n - 1)
                nc.scalar.activation(psg[:, n % 2, :], o[:, 0:T], ACT.Sigmoid).then_inc(sem("act_evac"), 1)
                feed(f"pw{n}")
                if n:
                    square(n_fin2, n - 1)
            square(n_fin2, KD - 1)
            inverse_root(n_fin2)

        @block.vector
        def _(dve):
            chain = [0]

            def link(ins):
                chain[0] += 1
                ins.then_inc(sem("dve_chain"), 1)
                dve.wait_ge(sem("dve_chain"), chain[0])

            def output(name, t=0):
                o = jobs[name].out + t
                dve.wait_ge(sem("proj_done"), o + 1)
                return psum[o % PROJ_BANKS]

            tt, ts, stt = nc.vector.tensor_tensor, nc.vector.tensor_scalar, nc.vector.scalar_tensor_tensor

            def scaled(n, k):
                dst = n.out(k) if n.out else n.sqb(k)
                stt(dst, n.src(k), gain(n, k), rstd[:], ALU.mult, ALU.mult).then_inc(sem("norm_scaled"), 1)

            def low_part(n, k):
                dve.wait_ge(sem("norm_hi"), n.p0 + k + 1)
                tt(n.lo(k), n.sqb(k), n.hi(k).bitcast(f32), ALU.subtract).then_inc(sem("norm_lo"), 1)

            def norm(n):
                dve.wait_ge(sem("norm_root"), n.i + 1)
                for k in range(n.kt):
                    scaled(n, k)
                    if not n.out and k >= 2:
                        low_part(n, k - 2)
                if not n.out:
                    for k in range(max(0, n.kt - 2), n.kt):
                        low_part(n, k)

            def add_square(n, k):
                dve.wait_ge(sem("norm_sq"), n.t0 + k + 1)
                if k == 0:
                    return
                ins = tt(sqsum[:], n.sqb(0) if k == 1 else sqsum[:], n.sqb(k), ALU.add)
                if k + 1 < n.kt:
                    link(ins)
                else:
                    ins.then_inc(sem("norm_acc"), 1)

            nc.vector.memset(ones[:], 1.0).then_inc(sem("memset"), 1)
            nc.vector.memset(eps[:], EPS).then_inc(sem("memset"), 1)
            nc.vector.memset(sraw[:, :, 0:SSM_TAPS - 1], 0.0).then_inc(sem("memset"), 1)
            dve.wait_ge(sem("vec_in"), 16)
            norm(n_ssm)
            H = slice(0, SSM_H)
            o = output("dt")
            ts(sp[H, 0, :], o[H, 0:T], v("dt_bias", 0, SSM_H), None, ALU.add).then_inc(sem("dve_evac"), 1)
            dve.wait_ge(sem("dve_evac"), 1)
            link(ts(sp[H, 1, :], sp[H, 0, :], -1.0, None, ALU.mult))
            tt(sp[H, 1, :], sp[H, 0, :], sp[H, 1, :], ALU.min).then_inc(sem("dt_step"), 1)
            dve.wait_ge(sem("dt_log"), 1)
            link(ts(dtT[H, :], sp[H, 2, :], 1.0, None, ALU.add))
            link(ts(dtT[H, :], dtT[H, :], -1.0, None, ALU.add))
            link(tt(dtT[H, :], sp[H, 2, :], dtT[H, :], ALU.subtract))
            link(tt(dtT[H, :], dtT[H, :], sp[H, 3, :], ALU.add))
            stt(dtT[H, :], sp[H, 0, :], 0.0, dtT[H, :], ALU.max, ALU.add).then_inc(sem("dt_scan"), 1)
            dve.wait_ge(sem("dt_scan"), 1)
            dve.wait_ge(sem("exp_a"), 1)
            link(ts(sp[H, 1, :], dtT[H, :], expa[H, :], -1.0, ALU.mult, ALU.mult))
            link(ts(sp[H, 0, :], dtT[H, :], 0.0, 1.0, ALU.mult, ALU.add))
            nc.vector.tensor_tensor_scan(acr[H, 0:T], sp[H, 0, :], sp[H, 1, :], 0.0, ALU.mult, ALU.add)\
                .then_inc(sem("dt_scan"), 1)
            dve.wait_ge(sem("dt_scan"), 2)
            nc.vector.tensor_copy(acr[H, T:T + P], acr[H, P:T]).then_inc(sem("dt_scan"), 1)
            dve.wait_ge(sem("dt_scan"), 3)

            def conv(dst, src, taps, weight):
                for i in range(taps):
                    w = weight(i)
                    if i == 0:
                        ins = ts(dst, src(0), w, None, ALU.mult)
                    else:
                        ins = stt(dst, src(i), w, dst, ALU.mult, ALU.add)
                    if i + 1 < taps:
                        link(ins)
                return ins

            for c in range(SSM_CT):
                dve.wait_ge(sem("act_evac"), c + 1)
                wait(dve, "ssm_silu", c - 1)
                conv(scv[:, c % 2, :], lambda i: sraw[:, c % 4, i:i + T], SSM_TAPS,
                     lambda i: v("sconv_w", c * SSM_TAPS + i)).then_inc(sem("ssm_conv"), 1)
                if c == 15:
                    dve.wait_ge(sem("decay_hi"), 1)
                    tt(acp[SSM_H:2 * SSM_H, :], acr[H, :], acp[H, :].bitcast(f32), ALU.subtract)\
                        .then_inc(sem("decay_parts"), 1)
                if c == 10:
                    dve.wait_ge(sem("dt_tr"), 1)
                    nc.vector.tensor_copy(dtn[:], PS_TR[:, 0:64].rearrange("p (b h) -> p b h", b=2))\
                        .then_inc(sem("dt_tok"), 1)
                    ts(nacn[:], PS_TR[:, 64:128].rearrange("p (b h) -> p b h", b=2), -1.0, None, ALU.mult)\
                        .then_inc(sem("dt_tok"), 1)

            def scale_x(j):
                dve.wait_ge(sem("x_tr"), j + 1)
                wait(dve, "y", 2 * (j - 1))
                src = PS_TR[:, 0:T].rearrange("p (b e d) -> p b e d", b=2, e=2)
                d = dtn[:, :, 2 * j:2 * j + 2].unsqueeze(3).broadcast_to([P, TB, 2, 64])
                tt(xdt[:, j % 2, :, :, :], src, d, ALU.mult).then_inc(sem("xdt"), 1)

            def decayed(hd):
                g = hd // 4
                dve.wait_ge(sem("decay_exp"), hd + 1)
                dve.wait_ge(sem("cb_evac"), g + 1)
                wait(dve, "y", hd - HEADS + 1)
                tt(mb[:, hd % HEADS, :], eb[:, hd % 2, :], cbs[:, g % 2, :], ALU.mult).then_inc(sem("decayed"), 1)

            dve.wait_ge(sem("dt_tok"), 2)
            scale_x(0)
            decayed(0)
            decayed(1)
            for j in range(SSM_PAIRS):
                o = output(f"sz{j}")
                dve.wait_ge(sem("z_tanh"), j + 1)
                stt(szb[:, j % 2, :], zb[:], 1.0, o[:, 0:T], ALU.add, ALU.mult).then_inc(sem("dve_evac"), 1)
                dve.wait_ge(sem("dve_evac"), freed[jobs[f"sz{j}"].out][1])
                if j + 1 < SSM_PAIRS:
                    scale_x(j + 1)
                if j % 2 == 0 and j:
                    norm(n_grp[j // 2 - 1])
                dve.wait_ge(sem("y"), 2 * j + 2)
                stt(yt[:], xs[:, j, :], v("ssm_d", j), PS_Y[:, 0:T], ALU.mult, ALU.add).then_inc(sem("y_read"), 1)
                dve.wait_ge(sem("y_read"), j + 1)
                stt(gb[:, j % 4, :], yt[:], 0.5, szb[:, j % 2, :], ALU.mult, ALU.mult).then_inc(sem("gated"), 1)
                if j + 1 < SSM_PAIRS:
                    decayed(2 * j + 2)
                    decayed(2 * j + 3)
            norm(n_grp[7])

            def add_to_residual(prefix, n=None):
                for k in range(KD):
                    o = output(f"{prefix}{k}")
                    tt(h[:, k, :], o[:, 0:T], h[:, k, :], ALU.add).then_inc(sem("dve_evac"), 1)
                    if k:
                        add_square(n, k - 1)
                add_square(n, KD - 1)

            add_to_residual("so", n_mla)

            norm(n_mla)

            def rotate(i):
                dst = kr[:] if i == 0 else qr[:, i - 1, :]
                dve.wait_ge(sem("act_evac"), freed[jobs[rope_job(i)].out][1])
                wait(dve, "rope_out", i)
                tt(r2[:], rx[:, i % 2, :], cos, ALU.mult).then_inc(sem("rope_cos"), 1)
                dve.wait_ge(sem("rope_swap"), i + 1)
                tt(r1[:], PS_TR[:, 0:T], sin, ALU.mult).then_inc(sem("rope_swapped_read"), 1)
                dve.wait_ge(sem("rope_swapped_read"), i + 1)
                dve.wait_ge(sem("rope_cos"), i + 1)
                tt(dst, r1[:], r2[:], ALU.add).then_inc(sem("rope_out"), 1)

            norm(n_kv)
            norm(n_q)
            for i in range(9):
                rotate(i)

            def row_max(bank, m, neg, i, scale, done):
                link(nc.vector.tensor_reduce(m[:, i % 2, 0:1], bank[:, 0:P], AX.X, ALU.max))
                link(nc.vector.tensor_reduce(m[:, i % 2, 1:2], bank[:, P:3 * P], AX.X, ALU.max))
                ts(neg[:, i % 2, :], m[:, i % 2, :], -scale, None, ALU.mult).then_inc(sem(done), 1)

            def mla_max(hd):
                dve.wait_ge(sem("score"), hd + 1)
                row_max(PS_S[hd % 2], mx, nm, hd, (MLA_D + MLA_R) ** -0.5, "max")

            def att_low(hd):
                dve.wait_ge(sem("att_hi"), hd + 1)
                tt(ogl[:, hd, :], ogt[:, hd % 2, :], ogh[:, hd, :].bitcast(f32), ALU.subtract).then_inc(sem("att_lo"), 1)

            def prob_scale(hd):
                dve.wait_ge(sem("prob"), hd + 1)
                link(nc.vector.reciprocal(rr[:, hd % 2, :], rs[:, hd % 2, :]))
                ts(pn[:, hd % 2, 0:P], pn[:, hd % 2, 0:P], rr[:, hd % 2, 0:1], None, ALU.mult)
                ts(pn[:, hd % 2, P:3 * P], pn[:, hd % 2, P:3 * P], rr[:, hd % 2, 1:2], None, ALU.mult)\
                    .then_inc(sem("prob_norm"), 1)

            mla_max(0)
            prob_scale(0)
            mla_max(1)
            prob_scale(1)
            for hd in range(MLA_H):
                if hd + 2 < MLA_H:
                    mla_max(hd + 2)
                if hd:
                    att_low(hd - 1)
                o = output(f"mz{hd}")
                dve.wait_ge(sem("mz_tanh"), hd + 1)
                wait(dve, "att_read", hd)
                stt(mzb[:], mze[:], 1.0, o[:, 0:T], ALU.add, ALU.mult).then_inc(sem("dve_evac"), 1)
                dve.wait_ge(sem("dve_evac"), freed[jobs[f"mz{hd}"].out][1])
                dve.wait_ge(sem("att"), hd + 1)
                stt(ogt[:, hd % 2, :], PS_Y[:, 0:T], 0.5, mzb[:], ALU.mult, ALU.mult).then_inc(sem("att_read"), 1)
                if hd + 2 < MLA_H:
                    prob_scale(hd + 2)
            att_low(MLA_H - 1)
            add_to_residual("mo", n_fin1)

            norm(n_fin1)
            norm(n_mix)
            link(nc.vector.memset(cpad[:, :, 0:CONV_TAPS - 1], 0.0))
            nc.vector.memset(vc[:], 0.0).then_inc(sem("vc_zero"), 1)
            nc.vector.memset(kcT[:], 0.0).then_inc(sem("vc_zero"), 1)
            link(nc.vector.memset(cx[:], 0.0))
            dve.sem_inc(sem("cx_zero"), 1)
            for i in range(CONV_CT):
                o = output(f"cv{i}")
                dve.wait_ge(sem("act_evac"), freed[jobs[f"cg{i}"].out][1])
                tt(cpad[:, i, CONV_TAPS - 1:], o[:, 0:T], csg[:, i % 2, :], ALU.mult).then_inc(sem("dve_evac"), 1)
            dve.wait_ge(sem("dve_evac"), freed[jobs["cv3"].out][1])

            def conv31(i):
                last = conv(ccv[:, i, :], lambda t: cpad[:, i, t:t + T], CONV_TAPS,
                            lambda t: v("conv_w", i * CONV_TAPS + t))
                link(last)
                ts(ccv[:, i, :], ccv[:, i, :], v("conv_b", i), None, ALU.add).then_inc(sem("conv_done"), 1)

            conv31(0)
            for i, pos in enumerate(("pos_k", "pos_v")):
                dve.wait_ge(sem("act_evac"), freed[jobs[f"kvc{i}"].out][1])
                for g in range(NSA_G):
                    row = ce[:, i, g, :]
                    src = row.rearrange("p (c k e) -> p k c e", k=CMP_STRIDE // 2, e=2)[:, :, :, 0]
                    for half in range(2):
                        s_ = src[:, :, half:half + N_CMP]
                        d_ = cx[:, i, 8 * half:8 * half + 8, g * CPAD:g * CPAD + N_CMP]
                        p_ = vec[:, VC[pos] + 8 * half:VC[pos] + 8 * half + 8].unsqueeze(2).broadcast_to([P, 8, N_CMP])
                        link(tt(d_, s_, p_, ALU.add))
                dve.sem_inc(sem("cmp_x"), 1)
            conv31(1)
            for i in range(2):
                dve.wait_ge(sem("cmp_hi"), i + 1)
                tt(cxl[:, i, :, :], cx[:, i, :, :], cxh[:, i, :, :].bitcast(f32), ALU.subtract).then_inc(sem("cmp_lo"), 1)
            conv31(2)
            for i in range(2):
                dve.wait_ge(sem("cmp_hid_hi"), i + 1)
                tt(hgl[:, i, :, :], hg[:, i, :, :], hgh[:, i, :, :].bitcast(f32), ALU.subtract)\
                    .then_inc(sem("cmp_hid_lo"), 1)
            conv31(3)
            dve.wait_ge(sem("ln_sum"), 1)
            link(ts(yat[:], PS_M[:, 0:T], 1.0 / (CONV_CT * P), None, ALU.mult))
            dve.wait_ge(sem("conv_done"), CONV_CT)
            tt(ccv[:], ccv[:], yat[:].unsqueeze(1).broadcast_to([P, CONV_CT, T]), ALU.subtract)\
                .then_inc(sem("ln_centred"), 1)
            dve.wait_ge(sem("ln_root"), 1)
            for k in range(CONV_CT):
                stt(sq[:, k, :], ccv[:, k, :], v("ln_g", k), rstd[:], ALU.mult, ALU.mult).then_inc(sem("ln_scaled"), 1)
            for k in range(CONV_CT):
                dve.wait_ge(sem("conv_hi"), k + 1)
                tt(cnl[:, k, :], sq[:, 4 + k, :], cnh[:, k, :].bitcast(f32), ALU.subtract).then_inc(sem("conv_lo"), 1)

            def nsa_max(x):
                dve.wait_ge(sem("nscore"), x + 1)
                row_max(PS_S[x % 2], nmx, nnm, x, NSA_D ** -0.5, "nmax")

            four = lambda t: t.rearrange("p (a c) -> p a c", c=CPAD)
            spread = lambda t: t.unsqueeze(2).broadcast_to([P, 4, CPAD])

            def nprob_scale(x):
                j, g, ty = x // 4, x // 2 % 2, x % 2
                dve.wait_ge(sem("nprob"), x + 1)
                link(nc.vector.reciprocal(nrr[:, x % 2, :], nrs[:, x % 2, :]))
                col = (1 + ty) * 8 + g * NSA_J + j
                link(tt(nrr[:, x % 2, :], nrr[:, x % 2, :], gates[:, :, col], ALU.mult))
                ts(npn[:, x % 2, 0:P], npn[:, x % 2, 0:P], nrr[:, x % 2, 0:1], None, ALU.mult)
                ts(npn[:, x % 2, P:3 * P], npn[:, x % 2, P:3 * P], nrr[:, x % 2, 1:2], None, ALU.mult)\
                    .then_inc(sem("nprob_norm"), 1)

            nsa_max(0)
            nprob_scale(0)
            nsa_max(1)
            nprob_scale(1)
            for x in range(16):
                j = x // 4
                if x % 4 == 0:
                    dve.wait_ge(sem("cmp_score"), j + 1)
                    wait(dve, "cmp_tr", j)
                    link(nc.vector.tensor_reduce(cmx[:], four(PS_M[:, 0:P]), AX.X, ALU.max))
                    tt(four(csc[:]), four(PS_M[:, 0:P]), spread(cmx[:]), ALU.subtract).then_inc(sem("cmp_read"), 1)
                if x + 2 < 16:
                    nsa_max(x + 2)
                if x % 4 == 1:
                    dve.wait_ge(sem("cmp_exp"), j + 1)
                    link(tt(cpn[:], cpn[:], cmp_ok, ALU.mult))
                    link(nc.vector.tensor_reduce(crs[:], four(cpn[:]), AX.X, ALU.add))
                    link(ts(crs[:], crs[:], 1e-30, None, ALU.max))
                    link(nc.vector.reciprocal(crr[:], crs[:]))
                    link(tt(crr[:].rearrange("p (b g) -> p b g", b=2), crr[:].rearrange("p (b g) -> p b g", b=2),
                            gates[:, :, j:j + 5:4], ALU.mult))
                    tt(four(cpn[:]), four(cpn[:]), spread(crr[:]), ALU.mult).then_inc(sem("cmp_prob"), 1)
                if x % 2 == 0:
                    n = x // 2
                    o = output(f"yb{n}")
                    stt(mt[:, n, :], o[:, 0:T], v("b_co", n), gm[:, 8 + n, :], ALU.add, ALU.mult).then_inc(sem("dve_evac"), 1)
                if x + 2 < 16:
                    nprob_scale(x + 2)
                if x % 4 == 3:
                    dve.wait_ge(sem("natt_hi"), j + 1)
                    tt(onl[:, j, :], PS_Y[:, 0:T], onh[:, j, :].bitcast(f32), ALU.subtract).then_inc(sem("natt_lo"), 1)

            def merge_low(n):
                dve.wait_ge(sem("merge_hi"), n + 1)
                tt(ml[:, n, :], mt[:, n, :], mh[:, n, :].bitcast(f32), ALU.subtract).then_inc(sem("merge_lo"), 1)

            for n in range(KD):
                o = output(f"ya{n}")
                wait(dve, "merged", n)
                tt(yat[:], o[:, 0:T], gm[:, n, :], ALU.mult).then_inc(sem("dve_evac"), 1)
                dve.wait_ge(sem("dve_evac"), freed[jobs[f"ya{n}"].out][1])
                tt(mt[:, n, :], mt[:, n, :], yat[:], ALU.add).then_inc(sem("merged"), 1)
                if n:
                    merge_low(n - 1)
            merge_low(KD - 1)
            add_to_residual("wo", n_ffn)

            nc.vector.memset(fraw[:, :, 0:FF_TAPS - 1], 0.0).then_inc(sem("ff_pad"), 1)
            norm(n_ffn)

            def ff_gate(i):
                dve.wait_ge(sem("ff_gelu"), i + 1)
                wait(dve, "ff_lo", i - 1)
                stt(fgt[:, i % 2, :], fcv[:, (2 * i + 1) % 4, :], v("fconv_b", 2 * i + 1), fge[:, i % 2, :],
                    ALU.add, ALU.mult).then_inc(sem("ff_gated"), 1)

            def ff_low(i):
                dve.wait_ge(sem("ff_hi"), i + 1)
                tt(ffl[:, i, :], fgt[:, i % 2, :], ffh[:, i, :].bitcast(f32), ALU.subtract).then_inc(sem("ff_lo"), 1)

            for i in range(KF):
                for e, s in enumerate("gv"):
                    c = 2 * i + e
                    dve.wait_ge(sem("act_evac"), freed[jobs[f"f{s}{i}"].out][1])
                    conv(fcv[:, c % 4, :], lambda t: fraw[:, c % 4, t:t + T], FF_TAPS,
                         lambda t: v("fconv_w", c * FF_TAPS + t)).then_inc(sem("ff_conv"), 1)
                if i:
                    ff_low(i - 1)
                dve.wait_ge(sem("ff_conv"), 2 * i + 2)
                ff_gate(i)
            ff_low(KF - 1)
            dve.wait_ge(sem("p_hi"), 1)
            tt(pl[:], pin[:], ph[:].bitcast(f32), ALU.subtract).then_inc(sem("p_lo"), 1)
            add_to_residual("fd", n_ple)

            norm(n_ple)
            for n in range(KD):
                o = output(f"pw{n}")
                dve.wait_ge(sem("act_evac"), freed[jobs[f"pg{n}"].out][1])
                wait(dve, "ple_added", n)
                tt(pt[:], o[:, 0:T], psg[:, n % 2, :], ALU.mult).then_inc(sem("dve_evac"), 1)
                dve.wait_ge(sem("dve_evac"), freed[jobs[f"pw{n}"].out][1])
                tt(h[:, n, :], h[:, n, :], pt[:], ALU.add).then_inc(sem("ple_added"), 1)
                if n:
                    add_square(n_fin2, n - 1)
            add_square(n_fin2, KD - 1)
            norm(n_fin2)


def arena_base(nc, kb):
    return nc.sbuf_base - kb * 1024


def shape_constants():
    c = np.zeros((P, N_CONST), np.float32)
    i = np.arange(P)
    c[:, 0:128] = np.eye(P)
    s = np.zeros((P, P))
    s[i ^ 32, i] = 1.0
    c[:, 128:256] = s
    c[:, 256:384] = np.where(i[None, :] > i[:, None], NEG, 0.0)
    tri = np.where(i[None, :] < i[:, None], NEG, 0.0)
    c[:, 384:512] = tri
    c[:, 640:768] = tri
    tok = np.arange(TB)[None, :, None, None] * P + i[:, None, None, None]
    key = np.arange(CPAD)[None, None, None, :]
    ok = (key * CMP_STRIDE + CMP_LEN - 1 <= tok) & (key < N_CMP)
    ok = np.broadcast_to(ok, (P, TB, NSA_G, CPAD)).reshape(P, P)
    c[:, 768:896] = np.where(ok, 0.0, NEG)
    c[:, 896:1024] = ok
    half = MLA_R // 2
    freq = np.float32(500000.0) ** (-np.arange(half, dtype=np.float32) / half)
    ang = np.arange(T, dtype=np.float32)[None, :] * freq[i % half][:, None]
    c[:, 1024:1280] = np.cos(ang)
    c[:, 1280:1536] = np.where((i // half % 2 == 0)[:, None], -np.sin(ang), np.sin(ang))
    return c


def pack_weights(inputs):
    jobs, _, _, n_slabs = plan()
    stream = np.zeros((n_slabs * BLK, P, P), np.float32)
    flat = {}
    for name, array, cols, rows, kind, _ in weight_jobs():
        if array not in flat:
            w = np.asarray(inputs[array])[0]
            flat[array] = np.concatenate([w, np.zeros((w.shape[0], 1), w.dtype)], axis=1)
        w = flat[array][:, cols]
        if rows is not None:
            w = w[rows]
        j = jobs[name]
        blocks = w.reshape(j.kt, P, j.wide, P).transpose(0, 2, 1, 3).reshape(j.blocks, P, P)
        stream[j.block:j.block + j.blocks] = blocks
    return np.ascontiguousarray(stream.reshape(n_slabs, BLK, P, P).transpose(0, 2, 1, 3).reshape(n_slabs, P, SLAB))


def pack_vectors(inputs):
    VC, n = vector_columns()
    vec = np.zeros((P, n), np.float32)

    def put(name, a):
        a = np.asarray(a).reshape(-1, P)
        vec[:, VC[name]:VC[name] + a.shape[0]] = a.T

    g = {k: np.asarray(x) for k, x in inputs.items()}
    put("norm0", g["norm_w"][0])
    put("norm1", g["norm_w"][1])
    put("final1", g["final_norm_w"])
    order = [conv_tile(c) for c in range(SSM_CT)]
    put("sconv_w", g["ssm_conv_w"][0].reshape(SSM_TAPS, SSM_CT, P)[:, order].transpose(1, 0, 2))
    put("sconv_b", g["ssm_conv_b"][0].reshape(SSM_CT, P)[order])
    put("ssm_d", np.repeat(g["ssm_D"][0], 64))
    put("ssm_nw", g["ssm_norm_w"][0])
    vec[0:SSM_H, VC["dt_bias"]] = g["ssm_dt_bias"][0]
    vec[0:SSM_H, VC["a_log"]] = g["ssm_A_log"][0]
    put("qnorm", g["mla_q_norm_w"][0])
    put("kvnorm", g["mla_kv_norm_w"][0])
    put("g_mix", g["g_mix_2"][0])
    put("pos_k", g["cmp_pos_k_2"][0])
    put("pos_v", g["cmp_pos_v_2"][0])
    put("conv_w", g["conv_w_2"][0].reshape(CONV_TAPS, CONV_CT, P).transpose(1, 0, 2))
    put("conv_b", g["conv_b_2"][0])
    put("ln_g", g["conv_ln_g_2"][0])
    put("ln_b", g["conv_ln_b_2"][0])
    put("b_co", g["b_conv_out_2"][0])
    put("g_ffn", g["g_ffn_2"][0])
    put("fconv_w", g["ffn_conv_w_2"][0].reshape(FF_TAPS, 2, KF, P).transpose(2, 1, 0, 3))
    put("fconv_b", g["ffn_conv_b_2"][0].reshape(2, KF, P).transpose(1, 0, 2))
    put("g_ple", g["g_ple_2"][0])
    put("g_final", g["g_final_2"])
    return vec


def feature_major(a):
    a = np.asarray(a)
    return np.ascontiguousarray(a.T.reshape(-1, P, T).transpose(1, 0, 2))


def kernel(**inputs):
    import concourse.bacc as bacc
    from concourse.bass_utils import run_bass_kernel_spmd

    arrays = {
        "slabs": pack_weights(inputs),
        "vectors": pack_vectors(inputs),
        "shape_consts": shape_constants(),
        "x_fm": feature_major(np.asarray(inputs["x"])[0]),
        "p_fm": feature_major(np.asarray(inputs["p_2"])[0, 0]),
    }
    nc = bacc.Bacc("TRN2", target_bir_lowering=False, num_devices=1)
    aps = [nc.dram_tensor(n, a.shape, mybir.dt.from_np(a.dtype), kind="ExternalInput").ap() for n, a in arrays.items()]
    out = nc.dram_tensor("out_fm", (P, KD, T), mybir.dt.float32, kind="ExternalOutput").ap()
    build(nc, *aps, out)
    r = run_bass_kernel_spmd(nc, [arrays], core_ids=[0])
    y = r.results[0]["out_fm"]
    return np.ascontiguousarray(y.transpose(1, 0, 2).reshape(DM, T).T).reshape(1, T, DM)
```

```python
from contextlib import ExitStack

import numpy as np

import concourse.bass as bass
from concourse import mybir

P = 128
T = 256
TB = T // P
DM = 1024
KD = DM // P
EPS = 1e-6
SSM_DI, SSM_H, SSM_G, SSM_N = 2048, 32, 8, 128
SSM_PAIRS = SSM_DI // P
SSM_CT = (SSM_DI + 2 * SSM_G * SSM_N) // P
SSM_TAPS = 4
MLA_H, MLA_Q, MLA_KV, MLA_R, MLA_D = 16, 384, 256, 64, 128
NSA_G, NSA_J, NSA_D = 2, 4, 64
CMP_LEN, CMP_STRIDE, CMP_HID = 32, 16, 256
N_CMP = (T - CMP_LEN) // CMP_STRIDE + 1
CPAD = 32
NSA_UNITS = 16
GATES_BEFORE = [8, 9, 10, 11, 0, 1, 2, 3]
GATES_BETWEEN = {0: 4, 1: 5, 2: 6, 3: 7, 4: 12, 7: 13, 10: 14, 13: 15}
CONV_BETWEEN = {5: 0, 6: 1, 8: 2, 9: 3, 11: 4, 12: 5, 14: 6, 15: 7}
CONV_CT, CONV_TAPS = 4, 31
FF = 2816
KF = FF // P
FF_TAPS = 3
NEG = -1e30
MIX_TAPS = 5
NEWTON = 3

BLK = 8
SLAB = BLK * P
RAW_RING, PART_RING = 6, 6
PROJ_BANKS = 3
STORE_TILES = 2


def weight_jobs():
    r = np.arange
    jobs = []

    def add(name, array, cols, consumer, kind="F", rows=None):
        jobs.append((name, array, np.asarray(cols), rows, kind, consumer))

    pad = lambda cols: np.concatenate([cols, np.full(P - len(cols), -1)])
    zero = SSM_DI
    add("dt", "ssm_in_w", pad(r(SSM_H) + 2 * SSM_DI + 2 * SSM_G * SSM_N), "dve")
    for c in range(SSM_CT):
        ch = conv_tile(c)
        add(f"xbc{c}", "ssm_in_w", zero + ch * P + r(P), "dve")
    for j in range(SSM_PAIRS):
        add(f"sz{j}", "ssm_in_w", j * P + r(P), "dve")
    for n in range(KD):
        add(f"so{n}", "ssm_out_w", n * P + r(P), "dve")
    for n in range(2):
        add(f"ckv{n}", "mla_in_w", MLA_Q + n * P + r(P), "dve")
    for n in range(3):
        add(f"cq{n}", "mla_in_w", n * P + r(P), "dve")
    kr = MLA_Q + MLA_KV + r(MLA_R)
    add("kr", "mla_in_w", np.concatenate([kr, kr]), "dve")
    zc = MLA_Q + MLA_KV + MLA_R

    def z_gate(h):
        add(f"mz{h}", "mla_in_w", zc + h * P + r(P), "dve")

    z_gate(0)
    z_gate(1)
    for n in range(4):
        cols = np.concatenate([(4 * n + i) * 2 * P + P + r(P) for i in range(4)])
        add(f"v{n}", "mla_ukv_w", cols, "act", "V")
    for i in range(MLA_H // 2):
        cols = np.concatenate([(2 * i + e) * 192 + P + r(MLA_R) for e in range(2)])
        add(f"qr{i}", "mla_uq_w", cols, "act")

    def head(h):
        add(f"kn{h}", "mla_ukv_w", h * 2 * P + r(P), "act")
        add(f"qn{h}", "mla_uq_w", h * 192 + r(P), "act")

    head(0)
    head(1)
    for h in range(MLA_H):
        if h + 2 < MLA_H:
            head(h + 2)
            z_gate(h + 2)
    for n in range(KD):
        add(f"mo{n}", "mla_out_w", n * P + r(P), "dve")
    conv0 = 512 + 768 + 24
    merge0 = conv0 + 1024

    def merge_gate(n):
        add(f"mg{n}", "w_in_2", merge0 + n * P + r(P), "dve")

    for i in range(CONV_CT):
        add(f"cg{i}", "w_in_2", conv0 + 512 + i * P + r(P), "dve")
        add(f"cv{i}", "w_in_2", conv0 + i * P + r(P), "dve")
    for c in range(2):
        add(f"kvc{c}", "w_in_2", 512 + c * P + r(P), "dve")
    for j in range(NSA_J):
        cols = np.concatenate([g * 256 + j * 64 + r(64) for g in range(2)])
        add(f"nq{j}", "w_in_2", cols, "dve")
    add("ks", "w_in_2", 512 + 2 * P + r(P), "dve")
    add("kw", "w_in_2", 512 + 4 * P + r(P), "dve")
    add("vsw", "w_in_2", np.concatenate([512 + 3 * P + r(P), 512 + 5 * P + r(P)]), "act", "V")
    add("gates", "w_in_2", pad(512 + 768 + r(24)), "dve")
    merge_gate(GATES_BEFORE[0])
    add("hk", "w_cmp_k1_2", r(CMP_HID), "act", "C")
    for n in GATES_BEFORE[1:3]:
        merge_gate(n)
    add("hv", "w_cmp_v1_2", r(CMP_HID), "act", "C")
    for n in GATES_BEFORE[3:5]:
        merge_gate(n)
    for s in "kv":
        add(f"c{s}", f"w_cmp_{s}2_2", np.concatenate([r(64), r(64)]), "act")
    for n in GATES_BEFORE[5:]:
        merge_gate(n)
    for x in range(NSA_UNITS):
        if x in CONV_BETWEEN:
            add(f"yb{CONV_BETWEEN[x]}", "w_conv_out_2", CONV_BETWEEN[x] * P + r(P), "dve")
        if x in GATES_BETWEEN:
            merge_gate(GATES_BETWEEN[x])
    rows = np.concatenate([g * 256 + j * 64 + r(64) for j in range(4) for g in range(2)])
    for n in range(KD):
        add(f"ya{n}", "w_o_nsa_2", n * P + r(P), "dve", rows=rows)
    for n in range(KD):
        add(f"wo{n}", "w_out_2", n * P + r(P), "dve")
    for i in range(KF):
        add(f"fg{i}", "w_up_2", i * P + r(P), "dve")
        add(f"fv{i}", "w_up_2", FF + i * P + r(P), "dve")
    for n in range(KD):
        add(f"fd{n}", "w_down_2", n * P + r(P), "dve")
    for n in range(KD):
        add(f"pg{n}", "w_ple_gate_2", n * P + r(P), "dve")
        add(f"pw{n}", "w_ple_2", n * P + r(P), "dve")
    return jobs


def conv_tile(c):
    return c + SSM_PAIRS if c < 16 else c - 16


K_OF = {"ssm_in_w": 8, "ssm_out_w": 16, "mla_in_w": 8, "mla_uq_w": 3, "mla_ukv_w": 2, "mla_out_w": 16,
        "w_in_2": 8, "w_cmp_k1_2": 16, "w_cmp_v1_2": 16, "w_cmp_k2_2": 2, "w_cmp_v2_2": 2, "w_conv_out_2": 4,
        "w_o_nsa_2": 4, "w_out_2": 8, "w_up_2": 8, "w_down_2": KF, "w_ple_gate_2": 8, "w_ple_2": 2}


class Job:

    def __init__(self, name, kind, kt, wide, block, out, consumer, used):
        self.name, self.kind, self.kt, self.wide, self.block, self.out = name, kind, kt, wide, block, out
        self.consumer, self.used = consumer, used
        self.n_out = TB if kind == "V" else 1
        self.blocks = kt * wide
        self.slab0, self.slab1 = block // BLK, (block + self.blocks - 1) // BLK


def plan():
    jobs, block, out = {}, 0, 0
    used = {"act": 0, "dve": 0}
    freed = []
    done_with = {}
    for name, array, cols, _, kind, consumer in weight_jobs():
        kt, wide = K_OF[array], len(cols) // P
        if wide > 1 and block % wide:
            block += wide - block % wide
        j = jobs[name] = Job(name, kind, kt, wide, block, out, consumer, used[consumer])
        for _ in range(j.n_out):
            used[consumer] += 1
            freed.append((consumer, used[consumer]))
        block += j.blocks
        out += j.n_out
        for s in range(j.slab0, j.slab1 + 1):
            done_with[s] = out
    return jobs, freed, done_with, -(-block // BLK)


def vector_columns():
    at, c = {}, 0
    for name, n in [("norm0", 8), ("norm1", 8), ("final1", 8), ("sconv_w", SSM_CT * SSM_TAPS), ("sconv_b", SSM_CT),
                    ("ssm_d", 16), ("ssm_nw", 16), ("dt_bias", 1), ("a_log", 1), ("qnorm", 3), ("kvnorm", 2),
                    ("g_mix", 8), ("pos_k", 16), ("pos_v", 16), ("conv_w", CONV_CT * CONV_TAPS), ("conv_b", 4),
                    ("ln_g", 4), ("ln_b", 4), ("b_co", 8), ("g_ffn", 8), ("fconv_w", 2 * KF * FF_TAPS),
                    ("fconv_b", 2 * KF), ("g_ple", 8), ("g_final", 8)]:
        at[name] = c
        c += n
    return at, c


CONST_COLS = {"ident": 0, "swap": 128, "mask_s": 256, "mask_t": 384, "cmp_add": 768, "cmp_ok": 896,
              "cos": 1024, "sin": 1280}
N_CONST = 1536


def build(nc, slabs_dram, vec_dram, const_dram, x_dram, p_dram, out_dram):
    f32, f32r, bf16, i32 = mybir.dt.float32, mybir.dt.float32r, mybir.dt.bfloat16, mybir.dt.int32
    ALU, ACT, AX = mybir.AluOpType, mybir.ActivationFunctionType, mybir.AxisListType
    jobs, freed, done_with, n_slabs = plan()
    VC, n_vec = vector_columns()
    ctx = ExitStack()
    with ctx:
        def sb(name, shape, dt=f32):
            return ctx.enter_context(nc.sbuf_tensor(name, shape, dt))

        raw = sb("raw", [P, RAW_RING, SLAB])
        wh = sb("wh", [P, PART_RING, SLAB], f32r)
        wl = sb("wl", [P, PART_RING, SLAB], f32r)
        h = sb("h", [P, KD, T])
        sq = sb("sq", [P, KD, T])
        vec = sb("vec", [P, n_vec])
        cst = sb("cst", [P, N_CONST])
        ident_b = sb("ident_b", [P, P], bf16)
        mask_s = sb("mask_s", [P, P], bf16)
        mask_t = sb("mask_t", [P, 3 * P], bf16)
        cmp_add = sb("cmp_add", [P, P], bf16)
        ones = sb("ones", [P, P])
        sqsum = sb("sqsum", [P, 2, T])
        msq, root, step = sb("msq", [P, 2 * TB]), sb("root", [P, 2 * TB]), sb("step", [P, 2 * TB])
        late = sb("late", [P, T])
        late_tok = sb("late_tok", [P, TB])
        root1 = sb("root1", [P, TB])
        gain12 = sb("gain12", [P, KD])
        ident = cst[:, 0:128]
        swap = cst[:, 128:256]
        cmp_ok = cst[:, 896:1024]
        cos, sin = cst[:, 1024:1280], cst[:, 1280:1536]

        def v(name, i=0, rows=P):
            return vec[0:rows, VC[name] + i:VC[name] + i + 1]

        arena_kb = 105
        arena = sb("arena", [P, arena_kb * 256])
        base = arena_base(nc, arena_kb)
        cursor = [0]

        def phase(start=0):
            cursor[0] = start

        def ar(name, shape, dt=f32):
            n = int(np.prod(shape)) * 4
            t = nc.alloc_sbuf_tensor_at(name, [P] + list(shape), dt, offset=base + cursor[0])
            cursor[0] += -(-n // 32) * 32
            assert cursor[0] <= arena_kb * 1024, (name, cursor[0])
            return t

        HEADS = 4
        phase()
        uh, ul = ar("uh", [KD, T], f32r), ar("ul", [KD, T], f32r)
        after_u = cursor[0]
        ynh, ynl = ar("ynh", [16, T], f32r), ar("ynl", [16, T], f32r)
        xs, bT, cT = ar("xs", [16, T]), ar("bT", [8, T]), ar("cT", [8, T])
        acp = ar("acp", [3 * P], f32r)
        sel = ar("sel", [SSM_H], f32r)
        dtn, nacn = ar("dtn", [TB, SSM_H]), ar("nacn", [TB, SSM_H])
        expa = ar("expa", [1])
        mark = cursor[0]
        sp = ar("sp", [4, T])
        acr, dtT = ar("acr", [3 * P]), ar("dtT", [T])
        cursor[0] = mark
        xdt = ar("xdt", [2, TB, 2, 64])
        gb = ar("gb", [4, T])
        szb = ar("szb", [2, T])
        zb = ar("zb", [T])
        mark = cursor[0]
        sraw = ar("sraw", [4, T + SSM_TAPS - 1])
        scv = ar("scv", [2, T])
        cursor[0] = mark
        eb, mb, cbs = ar("eb", [2, 3 * P]), ar("mb", [HEADS, 3 * P]), ar("cbs", [2, 3 * P])
        yt = ar("yt", [T])

        phase(after_u)
        ogh, ogl = ar("ogh", [16, T], f32r), ar("ogl", [16, T], f32r)
        vn = ar("vn", [TB, MLA_H * P])
        qr, kr = ar("qr", [8, T]), ar("kr", [T])
        kn, qn = ar("kn", [2, T]), ar("qn", [2, T])
        cqh, cql = ar("cqh", [3, T], f32r), ar("cql", [3, T], f32r)
        ckh, ckl = ar("ckh", [2, T], f32r), ar("ckl", [2, T], f32r)
        mx, nm, rs, rr = ar("mx", [2, 2]), ar("nm", [2, 2]), ar("rs", [2, 2]), ar("rr", [2, 2])
        mzb, mze = ar("mzb", [3, T]), ar("mze", [T])
        ogt = ar("ogt", [2, T])
        mark = cursor[0]
        cqr, ckr = ar("cqr", [3, T]), ar("ckr", [2, T])
        rx, r1, r2 = ar("rx", [2, T]), ar("r1", [T]), ar("r2", [T])
        cursor[0] = mark
        pn, pT = ar("pn", [2, 3 * P]), ar("pT", [2, 3 * P])

        phase(after_u)
        cpad = ar("cpad", [CONV_CT, T + CONV_TAPS - 1])
        ccv = ar("ccv", [CONV_CT, T])
        csg = ar("csg", [CONV_CT, T])
        nq = ar("nq", [NSA_J, T])
        ksT, kwT = ar("ksT", [T]), ar("kwT", [T])
        vsw = ar("vsw", [TB, 2 * P])
        gT, gates = ar("gT", [T]), ar("gates", [TB, 24])
        gm = ar("gm", [16, T])
        cnh, cnl = ar("cnh", [4, T], f32r), ar("cnl", [4, T], f32r)
        kcT, vcT = ar("kcT", [64]), ar("vcT", [P])
        vc = ar("vc", [TB, P])
        nmx, nnm, nrs, nrr = ar("nmx", [2, 2]), ar("nnm", [2, 2]), ar("nrs", [2, 2]), ar("nrr", [2, 2])
        cmx, crs, crr = ar("cmx", [4]), ar("crs", [4]), ar("crr", [4])
        csc, cpn, cpT = ar("csc", [P]), ar("cpn", [P]), ar("cpT", [P])
        yat = ar("yat", [T])
        mark = cursor[0]
        ce, kvt, cvt = ar("ce", [2, NSA_G, T]), ar("kvt", [2, T]), ar("cvt", [T])
        cx = ar("cx", [16, P])
        cxh, cxl = ar("cxh", [16, P], f32r), ar("cxl", [16, P], f32r)
        hg = ar("hg", [CMP_HID])
        hgh, hgl = ar("hgh", [2, P], f32r), ar("hgl", [2, P], f32r)
        cursor[0] = mark
        mt = ar("mt", [KD, T])
        onh, onl = ar("onh", [4, T], f32r), ar("onl", [4, T], f32r)
        npn, npT = ar("npn", [2, 3 * P]), ar("npT", [2, 3 * P])
        mh, ml = ar("mh", [KD, T], f32r), ar("ml", [KD, T], f32r)

        phase(after_u)
        ffh, ffl = ar("ffh", [KF, T], f32r), ar("ffl", [KF, T], f32r)
        fraw = ar("fraw", [4, T + FF_TAPS - 1])
        fcv = ar("fcv", [4, T])
        fge, fgt = ar("fge", [2, T]), ar("fgt", [2, T])
        pin = ar("pin", [2, T])
        ph, pl = ar("ph", [2, T], f32r), ar("pl", [2, T], f32r)
        psg, pt = ar("psg", [2, T]), ar("pt", [T])
        outb = ar("outb", [KD, T])

        psum = [ctx.enter_context(nc.psum_tensor(f"ps{i}", [P, 512], f32)) for i in range(8)]
        PS_TR, PS_S, PS_Y, PS_M = psum[3], [psum[4], psum[5]], psum[6], psum[7]
        rstd = PS_M[:, T:2 * T]

        sems = {}

        def sem(name):
            if name not in sems:
                sems[name] = ctx.enter_context(nc.semaphore(name))
            return sems[name]

        def wait(eng, name, value):
            if value > 0:
                eng.wait_ge(sem(name), value)

        class Norm:
            count = squares = adds = scaled = parts = 0

            def __init__(self, src, kt, width, gain, ready, hi=None, lo=None, out=None, sqb=None, summed=False,
                         late=False, squared=True, groups=1):
                self.src, self.kt, self.width, self.gain, self.ready = src, kt, width, gain, ready
                self.hi, self.lo, self.out, self.summed, self.late = hi, lo, out, summed, late
                self.groups = groups
                self.sqb = sqb or (lambda k: sq[:, k, :])
                self.sum, self.col, self.root, self.rstd = sqsum[:, 0, :], 0, root, rstd if groups == 1 else PS_M
                self.i, self.spread, self.t0, self.a0 = Norm.count, Norm.count, Norm.squares, Norm.adds
                self.d0, self.p0 = Norm.scaled, Norm.parts
                self.left, self.read = Norm.scaled, Norm.count
                Norm.count += 1
                Norm.squares += kt if squared else 0
                Norm.adds += kt - 1 if summed and squared else 0
                Norm.scaled += 1 if late else kt
                Norm.parts += kt if hi else 0

        tile_of = lambda t: (lambda k: t[:, k, :])

        def evac(name):
            return lambda k: (f"{freed[jobs[f'{name}{k}'].out][0]}_evac", freed[jobs[f"{name}{k}"].out][1])

        into_u = dict(hi=tile_of(uh), lo=tile_of(ul), summed=True, late=True)
        n_ssm = Norm(tile_of(h), 8, DM, "norm0", lambda k: ("x_in", 16), **into_u)
        n_grp = []
        for g in range(SSM_G - 1):
            last = g == SSM_G - 2
            n_grp.append(Norm((lambda k, g=g: gb[:, (2 * g + k) % 4, :]), 4 if last else 2, 256, ("ssm_nw", 2 * g),
                              (lambda k, g=g: ("gated", 2 * g + k + 1)),
                              (lambda k, g=g: ynh[:, 2 * g + k, :]), (lambda k, g=g: ynl[:, 2 * g + k, :]),
                              sqb=(lambda k, g=g: sq[:, (2 * g + k) % 8, :]), groups=2 if last else 1))
        n_mla = Norm(tile_of(h), 8, DM, "norm1", evac("so"), **into_u)
        n_kv = Norm(tile_of(ckr), 2, MLA_KV, "kvnorm", evac("ckv"), tile_of(ckh), tile_of(ckl),
                    sqb=lambda k: sq[:, 4 + k, :])
        n_q = Norm(tile_of(cqr), 3, MLA_Q, "qnorm", evac("cq"), tile_of(cqh), tile_of(cql))
        n_fin1 = Norm(tile_of(h), 8, DM, "final1", evac("mo"), out=tile_of(h), summed=True, squared=False)
        n_mix = Norm(tile_of(h), 8, DM, None, evac("mo"), sqb=lambda k: sq[:, 2 * (k % 4):2 * (k % 4) + 2, :], **into_u)
        n_mix.sum, n_mix.col, n_mix.root, n_fin1.root = sqsum[:, 1, :], TB, late_tok, root1
        n_fin1.t0, n_fin1.a0, n_mix.left, n_mix.read = n_mix.t0, n_mix.a0, n_fin1.left, n_fin1.read
        n_mix.d0, n_fin1.d0 = n_fin1.d0, n_fin1.d0 + 1
        n_mix.spread, n_fin1.spread = n_fin1.i, n_mix.i
        n_fin1.rstd = PS_TR[:, T:2 * T]
        n_ln = Norm(tile_of(ccv), CONV_CT, CONV_CT * P, "ln_g", lambda k: ("ln_centred", 1), out=lambda k: sq[:, k, :],
                    sqb=lambda k: sq[:, 4 + k, :])
        n_ffn = Norm(tile_of(h), 8, DM, "g_ffn", evac("wo"), **into_u)
        n_ple = Norm(tile_of(h), 8, DM, "g_ple", evac("fd"), **into_u)
        n_fin2 = Norm(tile_of(h), 8, DM, "g_final", lambda k: ("ple_added", k + 1), out=tile_of(outb), summed=True)

        def gain(n, k):
            if n is n_mix:
                return gain12[:, k:k + 1]
            name, at = n.gain if isinstance(n.gain, tuple) else (n.gain, 0)
            return v(name, at + k)

        def rope_job(i):
            return f"qr{i - 1}" if i else "kr"

        block = ctx.enter_context(nc.Block())

        @block.sync
        def _(sp_):
            for s in range(n_slabs):
                if s == 1:
                    sp_.dma_start(vec[:], vec_dram).then_inc(sem("vec_in"), 16)
                    sp_.dma_start(h[:], x_dram).then_inc(sem("x_in"), 16)
                elif s == 2:
                    sp_.dma_start(cst[:], const_dram).then_inc(sem("const_in"), 16)
                wait(sp_, "wl_ready", s - RAW_RING + 1)
                sp_.dma_start(raw[:, s % RAW_RING, :], slabs_dram[s]).then_inc(sem(f"slab_in{s % RAW_RING}"), 16)
                if s == jobs["fg8"].slab0:
                    wait(sp_, "dve_evac", freed[jobs["wo7"].out][1])
                    sp_.dma_start(pin[:], p_dram).then_inc(sem("p_in"), 16)
            for k in range(0, KD, STORE_TILES):
                sp_.wait_ge(sem("norm_scaled"), n_fin2.d0 + k + STORE_TILES)
                sp_.dma_start(out_dram[:, k:k + STORE_TILES, :], outb[:, k:k + STORE_TILES, :])\
                    .then_inc(sem("stored"), 16)
            sp_.wait_ge(sem("stored"), 16 * (KD // STORE_TILES))

        @block.gpsimd
        def _(pool):
            for s in range(n_slabs):
                pool.wait_ge(sem("wh_ready"), s + 1)
                nc.gpsimd.tensor_tensor(wl[:, s % PART_RING, :], raw[:, s % RAW_RING, :],
                                        wh[:, s % PART_RING, :].bitcast(f32), ALU.subtract).then_inc(sem("wl_ready"), 1)

        @block.tensor
        def _(pe):
            seen = [0]

            def project(name, hi, lo, ready=None):
                j = jobs[name]
                for o in range(j.out, j.out + j.n_out):
                    if o >= PROJ_BANKS:
                        who, n = freed[o - PROJ_BANKS]
                        wait(pe, f"{who}_evac", n)
                outs = [psum[(j.out + t) % PROJ_BANKS] for t in range(j.n_out)]
                n_cols = j.wide * P
                for k in range(j.kt):
                    if ready:
                        ready(k)
                    b = j.block + k * j.wide
                    s = b // BLK
                    if s >= seen[0]:
                        pe.wait_ge(sem("wl_ready"), s + 1)
                        seen[0] = s + 1
                    c = (b % BLK) * P
                    w_h = wh[:, s % PART_RING, c:c + n_cols]
                    w_l = wl[:, s % PART_RING, c:c + n_cols]
                    for t, o in enumerate(outs):
                        first, last = k == 0, k == j.kt - 1
                        if j.kind == "F":
                            a_h, a_l = hi(k), lo(k)
                            res = o[:, 0:a_h.shape[-1]]
                            nc.tensor.matmul(res, w_h, a_h, start=first, stop=False)
                            nc.tensor.matmul(res, w_h, a_l, start=False, stop=False)
                            ins = nc.tensor.matmul(res, w_l, a_h, start=False, stop=last)
                        else:
                            rows = slice(t * P, (t + 1) * P)
                            a_h, a_l = hi(k)[:, rows], lo(k)[:, rows]
                            res = o[:, 0:n_cols]
                            nc.tensor.matmul(res, a_h, w_h, start=first, stop=False)
                            nc.tensor.matmul(res, a_h, w_l, start=False, stop=False)
                            ins = nc.tensor.matmul(res, a_l, w_h, start=False, stop=last)
                        if last:
                            ins.then_inc(sem("proj_done"), 1)

            def norm_sum(n):
                wait(pe, "norm_scaled", n.left)
                if n.summed:
                    pe.wait_ge(sem("sq_added"), n.a0 + n.kt - 1)
                per = n.kt // n.groups
                for c in range(n.groups * TB):
                    g, b = divmod(c, TB)
                    for k in range(1) if n.summed else range(g * per, (g + 1) * per):
                        if b == 0 and not n.summed:
                            wait(pe, "norm_sq", n.t0 + k + 1)
                        src = n.sum if n.summed else n.sqb(k)
                        ins = nc.tensor.matmul(PS_M[:, n.col + c:n.col + c + 1], src[:, b * P:(b + 1) * P], ones[:, 0:1],
                                               start=n.summed or k == g * per, stop=n.summed or k == (g + 1) * per - 1)
                ins.then_inc(sem("norm_sum"), 1)

            def norm_spread(n):
                pe.wait_ge(sem("norm_root"), n.i + 1)
                for b in range(n.groups * TB):
                    ins = nc.tensor.matmul(n.rstd[:, b * P:(b + 1) * P], n.root[:, b:b + 1].broadcast_to([P, P]), ident,
                                           start=True, stop=True)
                ins.then_inc(sem("norm_spread"), 1)

            def norm(n):
                norm_sum(n)
                norm_spread(n)

            def parts_ready(n):
                return lambda k: wait(pe, "norm_lo", n.p0 + k + 1)

            def parts_then_sum(*norms):
                def ready(k):
                    wait(pe, "norm_lo", norms[-1].p0 + k + 1)
                    if k == KD - 1:
                        for n in norms:
                            norm_sum(n)
                return ready

            u = lambda k: uh[:, k, :]
            u_lo = lambda k: ul[:, k, :]

            pe.wait_ge(sem("memset"), 2)
            project("dt", u, u_lo, parts_ready(n_ssm))
            for c in range(SSM_CT):
                project(f"xbc{c}", u, u_lo)
                if c == 0:
                    norm_sum(n_ssm)
                elif c == 1:
                    pe.wait_ge(sem("const_in"), 16)
                    norm_spread(n_ssm)
                if c == 9:
                    pe.wait_ge(sem("dt_scan"), 2)
                    pe.wait_ge(sem("masks"), 1)
                    for i, src in enumerate((dtT, acr)):
                        for b in range(TB):
                            o = PS_TR[:, (2 * i + b) * SSM_H:(2 * i + b + 1) * SSM_H]
                            ins = nc.tensor.transpose(o, src[0:SSM_H, b * P:(b + 1) * P], ident[0:SSM_H, 0:SSM_H])
                    ins.then_inc(sem("dt_tr"), 1)

            def x_transpose(j):
                wait(pe, "ssm_silu", 16 + j + 1)
                wait(pe, "xdt", j)
                if j == 0:
                    wait(pe, "dt_tok", 2)
                for b in range(TB):
                    ins = nc.tensor.transpose(PS_TR[:, b * P:(b + 1) * P], xs[:, j, b * P:(b + 1) * P], ident)
                ins.then_inc(sem("x_tr"), 1)

            def decay(hd):
                wait(pe, "decay_exp", hd - 1)
                o = PS_S[hd % 2][:, 0:3 * P]
                pick = sel[0:2 * SSM_H, hd:hd + 1].broadcast_to([2 * SSM_H, P])
                nc.tensor.matmul(o, pick, acp[0:2 * SSM_H, :], start=True, stop=False)
                nc.tensor.matmul(o, ident_b[:], mask_t[:], start=False, stop=True).then_inc(sem("decay"), 1)

            def cb_scores(g):
                wait(pe, "cb_evac", g)
                wait(pe, "norm_scaled", n_grp[g - 3].d0 + 2 if g >= 3 else 1)
                nc.tensor.matmul(PS_M[:, 0:T], bT[:, g, 0:P], cT[:, g, :], start=True, stop=True)
                nc.tensor.matmul(PS_M[:, T:T + P], bT[:, g, P:T], cT[:, g, P:T], start=True, stop=True,
                                 skip_group_check=True).then_inc(sem("cb"), 1)

            def head_out(hd):
                j, e = divmod(hd, 2)
                wait(pe, "decayed", hd + 1)
                wait(pe, "xdt", j + 1)
                if e == 0:
                    wait(pe, "y_read", j)
                o = PS_Y[64 * e:64 * e + 64, :]
                m = mb[:, hd % HEADS, :]
                nc.tensor.matmul(o[:, 0:T], xdt[:, j % 2, 0, e, :], m[:, 0:T], start=True, stop=False)
                nc.tensor.matmul(o[:, P:T], xdt[:, j % 2, 1, e, :], m[:, T:T + P], start=False, stop=True)\
                    .then_inc(sem("y"), 1)

            wait(pe, "decay_parts", 1)
            x_transpose(0)
            cb_scores(0)
            decay(0)
            decay(1)
            project("sz0", u, u_lo)
            for j in range(SSM_PAIRS - 1):
                project(f"sz{j + 1}", u, u_lo)
                if j % 2:
                    cb_scores((j + 1) // 2)
                x_transpose(j + 1)
                decay(2 * j + 2)
                decay(2 * j + 3)
                if j % 2 and j >= 3:
                    wait(pe, "cb_evac", (j + 3) // 2)
                    norm_sum(n_grp[(j - 3) // 2])
                if j % 2 == 0 and j >= 4:
                    norm_spread(n_grp[(j - 4) // 2])
                head_out(2 * j)
                head_out(2 * j + 1)

            def last_groups(k):
                if k == 5:
                    head_out(2 * SSM_PAIRS - 2)
                    head_out(2 * SSM_PAIRS - 1)
                elif k == 8:
                    norm_sum(n_grp[6])
                elif k == 12:
                    norm_spread(n_grp[6])
                wait(pe, "norm_lo", n_grp[0].p0 + k + 1)

            for n in range(KD):
                project(f"so{n}", tile_of(ynh), tile_of(ynl), last_groups if n == 0 else None)

            for i, n in enumerate(["ckv0", "ckv1", "cq0", "cq1", "cq2", "kr"]):
                project(n, u, u_lo, parts_then_sum(n_mla) if i == 0 else None)
                if n == "ckv1":
                    norm_spread(n_mla)
                elif n == "cq1":
                    norm_sum(n_kv)
            norm_spread(n_kv)
            project("mz0", u, u_lo)
            norm_sum(n_q)
            project("mz1", u, u_lo)

            def rope_swap(i):
                who, count = freed[jobs[rope_job(i)].out]
                pe.wait_ge(sem(f"{who}_evac"), count)
                wait(pe, "rope_swapped_read", i)
                if i == 0:
                    wait(pe, "xdt", 16)
                nc.tensor.matmul(PS_TR[:, 0:T], swap, rx[:, i % 2, :], start=True, stop=True)\
                    .then_inc(sem("rope_swap"), 1)

            rope_swap(0)
            for n in range(4):
                project(f"v{n}", tile_of(ckh), tile_of(ckl), parts_ready(n_kv) if n == 0 else None)
                if n == 0:
                    norm_spread(n_q)
            for i in range(8):
                project(f"qr{i}", tile_of(cqh), tile_of(cql), parts_ready(n_q) if i == 0 else None)
                if i:
                    rope_swap(i)
            rope_swap(8)

            def scores(hd):
                wait(pe, "act_evac", freed[jobs[f"qn{hd}"].out][1])
                wait(pe, "prob", hd - 1)
                o = PS_S[hd % 2]
                e, i = hd % 2, hd // 2
                rows = slice(64 * e, 64 * e + 64)
                if hd == 0:
                    wait(pe, "decay_exp", SSM_H)
                    wait(pe, "rope_out", 9)
                for b in range(TB):
                    cols = slice(0, P) if b == 0 else slice(P, 3 * P)
                    q_, nk = slice(b * P, (b + 1) * P), (b + 1) * P
                    nc.tensor.matmul(o[:, cols], qn[:, hd % 2, q_], kn[:, hd % 2, 0:nk], start=b == 0, stop=False,
                                     skip_group_check=True)
                    nc.tensor.matmul(o[:, cols], qr[rows, i, q_], kr[rows, 0:nk], start=False, stop=False,
                                     skip_group_check=True)
                    d = o[:, 0:P] if b == 0 else o[:, 2 * P:3 * P]
                    ins = nc.tensor.matmul(d, ident_b[:], mask_s[:], start=False, stop=True, skip_group_check=True)
                ins.then_inc(sem("score"), 1)

            def prob_transpose(hd):
                wait(pe, "prob_norm", hd + 1)
                wait(pe, "prob_tr_read", hd)
                if hd == 0:
                    wait(pe, "rope_swapped_read", 9)
                for c in range(3):
                    ins = nc.tensor.transpose(PS_TR[:, c * P:(c + 1) * P], pn[:, hd % 2, c * P:(c + 1) * P], ident)
                ins.then_inc(sem("prob_tr"), 1)

            def values(hd):
                wait(pe, "prob_tr_read", hd + 1)
                wait(pe, "att_read", hd)
                if hd == 0:
                    wait(pe, "y_read", 16)
                nc.tensor.matmul(PS_Y[:, 0:T], vn[:, 0, hd * P:(hd + 1) * P], pT[:, hd % 2, 0:T], start=True, stop=False)
                nc.tensor.matmul(PS_Y[:, P:T], vn[:, 1, hd * P:(hd + 1) * P], pT[:, hd % 2, T:T + P],
                                 start=False, stop=True).then_inc(sem("att"), 1)

            def head_proj(hd):
                project(f"kn{hd}", tile_of(ckh), tile_of(ckl))
                project(f"qn{hd}", tile_of(cqh), tile_of(cql))

            head_proj(0)
            scores(0)
            head_proj(1)
            scores(1)
            prob_transpose(0)
            for hd in range(MLA_H - 2):
                head_proj(hd + 2)
                project(f"mz{hd + 2}", u, u_lo)
                prob_transpose(hd + 1)
                scores(hd + 2)
                values(hd)

            def last_heads(k):
                if k == 2:
                    values(MLA_H - 2)
                elif k == 6:
                    prob_transpose(MLA_H - 1)
                elif k == 10:
                    values(MLA_H - 1)
                wait(pe, "att_lo", k + 1)

            for n in range(KD):
                project(f"mo{n}", tile_of(ogh), tile_of(ogl), last_heads if n == 0 else None)

            for i in range(CONV_CT):
                project(f"cg{i}", u, u_lo, parts_then_sum(n_fin1, n_mix) if i == 0 else None)
                if i == 1:
                    norm_spread(n_mix)
                project(f"cv{i}", u, u_lo)
                if i == 1:
                    wait(pe, "prob_tr_read", MLA_H)
                    norm_spread(n_fin1)
            for n in ["kvc0", "kvc1", "nq0", "nq1", "nq2", "nq3", "ks", "kw", "vsw", "gates",
                      f"mg{GATES_BEFORE[0]}"]:
                project(n, u, u_lo)
            wait(pe, "norm_scaled", n_fin1.d0 + KD)
            wait(pe, "gates_sig", 1)
            for b in range(TB):
                ins = nc.tensor.transpose(PS_TR[:, b * P:(b + 1) * P], gT[:, b * P:(b + 1) * P], ident)
            ins.then_inc(sem("gates_tr"), 1)
            project("hk", tile_of(cxh), tile_of(cxl), lambda k: pe.wait_ge(sem("cmp_lo"), 1))
            for n in GATES_BEFORE[1:3]:
                project(f"mg{n}", u, u_lo)
            project("hv", tile_of(cxh), tile_of(cxl))
            project(f"mg{GATES_BEFORE[3]}", u, u_lo)
            pe.wait_ge(sem("act_evac"), freed[jobs["hv"].out][1])
            pe.wait_ge(sem("gates_read"), 1)
            for n in range(2):
                ins = nc.tensor.transpose(PS_TR[:, n * P:(n + 1) * P], hg[:, n * P:(n + 1) * P], ident)
            ins.then_inc(sem("cmp_hid_tr"), 1)
            project(f"mg{GATES_BEFORE[4]}", u, u_lo)
            for i, s in enumerate("kv"):
                project(f"c{s}", (lambda k, i=i: hgh[:, k, 64 * i:64 * i + 64]), (lambda k, i=i: hgl[:, k, 64 * i:64 * i + 64]),
                        lambda k: pe.wait_ge(sem("cmp_hid_lo"), 1))
            project(f"mg{GATES_BEFORE[5]}", u, u_lo)
            pe.wait_ge(sem("act_evac"), freed[jobs["cv"].out][1])
            nc.tensor.transpose(PS_TR[:, 0:P], vcT[:, :], ident).then_inc(sem("vc_tr"), 1)

            def conv_mean():
                pe.wait_ge(sem("conv_tap"), CONV_CT * (CONV_TAPS + 1))
                pe.wait_ge(sem("cmp_read"), 1)
                for k in range(CONV_CT):
                    ins = nc.tensor.matmul(PS_M[:, 0:T], ones[:], ccv[:, k, :], start=k == 0, stop=k == 3)
                ins.then_inc(sem("ln_sum"), 1)

            def cmp_scores(j):
                wait(pe, "cmp_read", j)
                pe.wait_ge(sem("norm_scaled"), n_ln.d0 + CONV_CT if j else n_ln.left)
                for b in range(TB):
                    nc.tensor.matmul(PS_M[:, b * 64:b * 64 + 64], nq[:, j, b * P:(b + 1) * P], kcT[:], start=b == 0,
                                     stop=False, skip_group_check=True)
                nc.tensor.matmul(PS_M[:, 0:P], ident_b[:], cmp_add[:], start=False, stop=True,
                                 skip_group_check=True).then_inc(sem("cmp_score"), 1)

            def unit_scores(x):
                j, g, ty = x // 4, x // 2 % 2, x % 2
                wait(pe, "nprob", x - 1)
                if x == 0:
                    for n in ("nq3", "ks", "kw"):
                        wait(pe, "dve_evac", freed[jobs[n].out][1])
                if x == 0:
                    wait(pe, "prob", MLA_H)
                o, key, rows = PS_S[x % 2], (ksT, kwT)[ty], slice(64 * g, 64 * g + 64)
                for b in range(TB):
                    cols = slice(0, P) if b == 0 else slice(P, 3 * P)
                    nc.tensor.matmul(o[:, cols], nq[rows, j, b * P:(b + 1) * P], key[rows, 0:(b + 1) * P],
                                     start=b == 0, stop=False, skip_group_check=True)
                    d = o[:, 0:P] if b == 0 else o[:, 2 * P:3 * P]
                    ins = nc.tensor.matmul(d, ident_b[:], mask_s[:], start=False, stop=True, skip_group_check=True)
                ins.then_inc(sem("nscore"), 1)

            def unit_transpose(x):
                j, g, ty = x // 4, x // 2 % 2, x % 2
                wait(pe, "nprob_norm", x + 1)
                wait(pe, "nprob_tr_read", x)
                wait(pe, "cmp_tr_read", (x + 1) // 4)
                if x == 0:
                    wait(pe, "vc_read", 1)
                for c in range(3):
                    ins = nc.tensor.transpose(PS_TR[:, c * P:(c + 1) * P], npn[:, x % 2, c * P:(c + 1) * P], ident)
                ins.then_inc(sem("nprob_tr"), 1)

            def unit_accumulate(x):
                j, g, ty = x // 4, x // 2 % 2, x % 2
                wait(pe, "nprob_tr_read", x + 1)
                if x % 4 == 0:
                    wait(pe, "natt_lo", j)
                    wait(pe, "att_read", MLA_H)
                o = PS_Y[64 * g:64 * g + 64, :]
                vcol = slice(ty * P + 64 * g, ty * P + 64 * g + 64)
                nc.tensor.matmul(o[:, 0:T], vsw[:, 0, vcol], npT[:, x % 2, 0:T], start=ty == 0, stop=False,
                                 skip_group_check=True)
                nc.tensor.matmul(o[:, P:T], vsw[:, 1, vcol], npT[:, x % 2, T:T + P], start=False, stop=False,
                                 skip_group_check=True).then_inc(sem("nvalue"), 1)

            def cmp_transpose(j):
                wait(pe, "cmp_prob", j + 1)
                wait(pe, "nprob_tr_read", 4 * j + 3)
                nc.tensor.transpose(PS_TR[:, 0:P], cpn[:, :], ident).then_inc(sem("cmp_tr"), 1)

            def cmp_values(j):
                wait(pe, "cmp_tr_read", j + 1)
                for b in range(TB):
                    ins = nc.tensor.matmul(PS_Y[:, b * P:(b + 1) * P], vc[:, b, :], cpT[:], start=False, stop=b == 1,
                                           skip_group_check=True)
                ins.then_inc(sem("natt"), 1)

            unit_scores(0)
            project(f"mg{GATES_BEFORE[6]}", u, u_lo)
            unit_scores(1)
            project(f"mg{GATES_BEFORE[7]}", u, u_lo)
            unit_transpose(0)
            for x in range(NSA_UNITS):
                if x + 2 < NSA_UNITS:
                    unit_scores(x + 2)
                if x in CONV_BETWEEN:
                    project(f"yb{CONV_BETWEEN[x]}", tile_of(cnh), tile_of(cnl),
                            (lambda k: wait(pe, "conv_lo", k + 1)) if CONV_BETWEEN[x] == 0 else None)
                if x in GATES_BETWEEN:
                    project(f"mg{GATES_BETWEEN[x]}", u, u_lo)
                if x % 4 == 0:
                    cmp_scores(x // 4)
                if x == 1:
                    conv_mean()
                elif x == 2:
                    norm_sum(n_ln)
                elif x == 3:
                    norm_spread(n_ln)
                if x % 4 == 2:
                    cmp_transpose(x // 4)
                if x + 1 < 16:
                    unit_transpose(x + 1)
                unit_accumulate(x)
                if x % 4 == 3:
                    cmp_values(x // 4)
            for n in range(KD):
                project(f"ya{n}", tile_of(onh), tile_of(onl), (lambda k: wait(pe, "natt_lo", k + 1)) if n == 0 else None)
            for n in range(KD):
                project(f"wo{n}", tile_of(mh), tile_of(ml), (lambda k: wait(pe, "merge_lo", k + 1)) if n == 0 else None)

            for i in range(KF):
                project(f"fg{i}", u, u_lo, parts_then_sum(n_ffn) if i == 0 else None)
                project(f"fv{i}", u, u_lo)
                if i == 0:
                    norm_spread(n_ffn)
            for n in range(KD):
                project(f"fd{n}", tile_of(ffh), tile_of(ffl), (lambda k: wait(pe, "ff_lo", k + 1)) if n == 0 else None)

            for n in range(KD):
                project(f"pg{n}", u, u_lo, parts_then_sum(n_ple) if n == 0 else None)
                project(f"pw{n}", tile_of(ph), tile_of(pl), (lambda k: wait(pe, "p_lo", 1)) if n == 0 else None)
                if n == 0:
                    norm_spread(n_ple)
            norm(n_fin2)

        @block.scalar
        def _(act):
            split = [0]
            chain = [0]

            def link(ins):
                chain[0] += 1
                ins.then_inc(sem("act_chain"), 1)
                act.wait_ge(sem("act_chain"), chain[0])

            def feed(name):
                feed_slabs(min(jobs[name].slab0 + PART_RING - 1, n_slabs - 1))

            def feed_slabs(last):
                while split[0] <= last:
                    s = split[0]
                    act.wait_ge(sem(f"slab_in{s % RAW_RING}"), 16 * (s // RAW_RING + 1))
                    if s >= PART_RING:
                        act.wait_ge(sem("proj_done"), done_with[s - PART_RING])
                    nc.scalar.activation(wh[:, s % PART_RING, :], raw[:, s % RAW_RING, :], ACT.Copy)\
                        .then_inc(sem("wh_ready"), 1)
                    split[0] += 1

            def output(name, t=0):
                feed(name)
                o = jobs[name].out + t
                act.wait_ge(sem("proj_done"), o + 1)
                return psum[o % PROJ_BANKS]

            def square(n, k):
                wait(act, *n.ready(k))
                nc.scalar.activation(n.sqb(k), n.src(k), ACT.Square).then_inc(sem("norm_sq"), 1)

            def squares(n):
                for k in range(n.kt):
                    square(n, k)

            def high(n, k):
                wait(act, *n.ready(k))
                nc.scalar.activation(n.hi(k), n.src(k), ACT.Copy, scale=gain(n, k)).then_inc(sem("norm_hi"), 1)

            def square_and_high(n, k):
                wait(act, *n.ready(k))
                if n is n_mix:
                    if k >= 4:
                        act.wait_ge(sem("sq_added"), n.a0 + max(1, k - 4))
                    pair = n.sqb(k)
                    nc.scalar.activation(pair[:, 0, :], n.src(k), ACT.Square)
                    nc.scalar.activation(pair[:, 1, :], n.src(k), ACT.Square, scale=gain(n_fin1, k))\
                        .then_inc(sem("norm_sq"), 1)
                else:
                    nc.scalar.activation(n.sqb(k), n.src(k), ACT.Square).then_inc(sem("norm_sq"), 1)
                high(n, k)

            def feed_and_square(prefix, n):
                for k in range(KD):
                    feed(f"{prefix}{k}")
                    if k:
                        square_and_high(n, k - 1)
                square_and_high(n, KD - 1)

            def high_parts(n):
                for k in range(n.kt):
                    act.wait_ge(sem("norm_scaled"), n.d0 + k + 1)
                    nc.scalar.activation(n.hi(k), n.sqb(k), ACT.Copy).then_inc(sem("norm_hi"), 1)

            feed_slabs(0)
            act.wait_ge(sem("vec_in"), 16)
            for k in range(KD):
                high(n_ssm, k)
                if k == 3:
                    feed_slabs(1)
            feed_slabs(2)
            squares(n_ssm)
            feed("dt")
            act.wait_ge(sem("const_in"), 16)
            nc.scalar.activation(ident_b[:], ident, ACT.Copy)
            nc.scalar.activation(mask_s[:], cst[:, 256:384], ACT.Copy)
            nc.scalar.activation(mask_t[:], cst[:, 384:768], ACT.Copy)
            for e in range(2):
                r_ = slice(SSM_H * e, SSM_H * e + SSM_H)
                nc.scalar.activation(sel[r_, :], cst[r_, r_], ACT.Copy)
            nc.scalar.activation(cmp_add[:], cst[:, 768:896], ACT.Copy).then_inc(sem("masks"), 1)
            nc.scalar.activation(expa[0:SSM_H, :], v("a_log", 0, SSM_H), ACT.Exp).then_inc(sem("exp_a"), 1)
            act.wait_ge(sem("dt_step"), 1)
            link(nc.scalar.activation(sp[0:SSM_H, 2, :], sp[0:SSM_H, 1, :], ACT.Exp))
            nc.scalar.activation(sp[0:SSM_H, 3, :], sp[0:SSM_H, 2, :], ACT.Ln, bias=1.0).then_inc(sem("dt_log"), 1)

            def ssm_silu(c):
                act.wait_ge(sem("ssm_conv"), c + 1)
                dst = bT[:, c, :] if c < 8 else cT[:, c - 8, :] if c < 16 else xs[:, c - 16, :]
                nc.scalar.activation(dst, scv[:, c % 2, :], ACT.Silu, bias=v("sconv_b", c)).then_inc(sem("ssm_silu"), 1)

            for c in range(SSM_CT):
                feed(f"xbc{c}")
                if c:
                    ssm_silu(c - 1)
                if c == 12:
                    act.wait_ge(sem("dt_scan"), 3)
                    nc.scalar.activation(acp[0:SSM_H, :], acr[0:SSM_H, :], ACT.Copy).then_inc(sem("decay_hi"), 1)
            ssm_silu(SSM_CT - 1)

            def cb_evac(g):
                act.wait_ge(sem("cb"), g + 1)
                wait(act, "decayed", 4 * (g - 1))
                nc.scalar.activation(cbs[:, g % 2, :], PS_M[:, 0:3 * P], ACT.Copy).then_inc(sem("cb_evac"), 1)

            def decay_exp(hd):
                act.wait_ge(sem("decay"), hd + 1)
                wait(act, "decayed", hd - 1)
                o = PS_S[hd % 2]
                nc.scalar.activation(eb[:, hd % 2, 0:T], o[:, 0:T], ACT.Exp, bias=nacn[:, 0, hd:hd + 1])
                nc.scalar.activation(eb[:, hd % 2, T:T + P], o[:, T:T + P], ACT.Exp, bias=nacn[:, 1, hd:hd + 1])\
                    .then_inc(sem("decay_exp"), 1)

            def square_group(t):
                n = n_grp[min(t // 2, SSM_G - 2)]
                square(n, t - 2 * n_grp.index(n))

            feed("sz0")
            act.wait_ge(sem("dt_tok"), 2)
            act.wait_ge(sem("ssm_silu"), SSM_CT)
            cb_evac(0)
            decay_exp(0)
            decay_exp(1)
            for j in range(SSM_PAIRS):
                if j + 1 < SSM_PAIRS:
                    feed(f"sz{j + 1}")
                if j % 2:
                    cb_evac((j + 1) // 2) if j + 1 < SSM_PAIRS else None
                act.wait_ge(sem("dve_evac"), freed[jobs[f"sz{j}"].out][1])
                wait(act, "z_gate", j)
                nc.scalar.activation(zb[:], szb[:, j % 2, :], ACT.Tanh, scale=0.5).then_inc(sem("z_tanh"), 1)
                if j + 1 < SSM_PAIRS:
                    decay_exp(2 * j + 2)
                    decay_exp(2 * j + 3)
                if j:
                    square_group(j - 1)
                if j % 2 == 0 and j >= 4:
                    high_parts(n_grp[(j - 4) // 2])
            feed("so0")
            square_group(SSM_PAIRS - 1)
            high_parts(n_grp[6])
            feed_and_square("so", n_mla)

            feed("cq1")
            squares(n_kv)
            feed("cq2")
            squares(n_q)
            feed("kr")
            high_parts(n_kv)
            feed("v0")
            high_parts(n_q)
            for n in range(4):
                for t in range(TB):
                    o = output(f"v{n}", t)
                    nc.scalar.activation(vn[:, t, n * 512:(n + 1) * 512], o[:, :], ACT.Copy).then_inc(sem("act_evac"), 1)
            for i in range(8):
                o = output(f"qr{i}")
                wait(act, "rope_out", i)
                nc.scalar.activation(rx[:, (i + 1) % 2, :], o[:, 0:T], ACT.Copy).then_inc(sem("act_evac"), 1)

            def evac_head(hd):
                o = output(f"kn{hd}")
                wait(act, "score", hd - 1)
                nc.scalar.activation(kn[:, hd % 2, :], o[:, 0:T], ACT.Copy).then_inc(sem("act_evac"), 1)
                o = output(f"qn{hd}")
                nc.scalar.activation(qn[:, hd % 2, :], o[:, 0:T], ACT.Copy).then_inc(sem("act_evac"), 1)

            def prob(hd):
                act.wait_ge(sem("max"), hd + 1)
                wait(act, "prob_tr", hd - 1)
                o, s = PS_S[hd % 2], (MLA_D + MLA_R) ** -0.5
                for b, c in enumerate((slice(0, P), slice(P, 3 * P))):
                    ins = nc.scalar.activation(pn[:, hd % 2, c], o[:, c], ACT.Exp, bias=nm[:, hd % 2, b:b + 1], scale=s,
                                               accum_out=rs[:, hd % 2, b:b + 1])
                ins.then_inc(sem("prob"), 1)

            def prob_evac(hd):
                act.wait_ge(sem("prob_tr"), hd + 1)
                wait(act, "att", hd - 1)
                nc.scalar.activation(pT[:, hd % 2, :], PS_TR[:, 0:3 * P], ACT.Copy).then_inc(sem("prob_tr_read"), 1)

            evac_head(0)
            evac_head(1)
            act.wait_ge(sem("rope_out"), 9)
            prob(0)
            prob(1)
            prob_evac(0)
            for hd in range(MLA_H):
                if hd + 2 < MLA_H:
                    evac_head(hd + 2)
                if hd + 2 < MLA_H:
                    feed(f"mz{hd + 2}")
                act.wait_ge(sem("dve_evac"), freed[jobs[f"mz{hd}"].out][1])
                wait(act, "mz_gate", hd)
                nc.scalar.activation(mze[:], mzb[:, hd % 3, :], ACT.Tanh, scale=0.5).then_inc(sem("mz_tanh"), 1)
                if hd + 1 < MLA_H:
                    prob_evac(hd + 1)
                if hd + 2 < MLA_H:
                    prob(hd + 2)
                act.wait_ge(sem("att_read"), hd + 1)
                nc.scalar.activation(ogh[:, hd, :], ogt[:, hd % 2, :], ACT.Copy).then_inc(sem("att_hi"), 1)
            feed_and_square("mo", n_mix)

            def scaled_output(name):
                feed(name)
                act.wait_ge(sem("dve_evac"), freed[jobs[name].out][1])

            def merge_gate(n):
                scaled_output(f"mg{n}")
                nc.scalar.activation(gm[:, n, :], gm[:, n, :], ACT.Sigmoid).then_inc(sem("merge_gate"), 1)

            def merge_gate_by_tanh(n):
                scaled_output(f"mg{n}")
                link(nc.scalar.activation(gm[:, n, :], gm[:, n, :], ACT.Tanh, scale=0.5))
                nc.scalar.activation(gm[:, n, :], gm[:, n, :], ACT.Copy, scale=0.5, bias=0.5)\
                    .then_inc(sem("merge_gate"), 1)

            for i in range(CONV_CT):
                scaled_output(f"cg{i}")
                nc.scalar.activation(csg[:, i, :], csg[:, i, :], ACT.Sigmoid).then_inc(sem("conv_gate"), 1)
            for i in range(2):
                scaled_output(f"kvc{i}")
                if i == 0:
                    act.wait_ge(sem("cx_zero"), 1)
                for g in range(NSA_G):
                    r_ = slice(64 * g, 64 * g + 64)
                    nc.scalar.activation(ce[0:64, i, g, :], kvt[r_, i, 0:T], ACT.Copy)
                    ins = nc.scalar.activation(ce[64:128, i, g, 0:T - 1], kvt[r_, i, 1:T], ACT.Copy)
                ins.then_inc(sem("cmp_shift"), 1)
            feed("nq1")
            act.wait_ge(sem("cmp_x"), 1)
            nc.scalar.activation(cxh[:], cx[:], ACT.Copy).then_inc(sem("cmp_hi"), 1)
            for t in range(TB):
                o = output("vsw", t)
                nc.scalar.activation(vsw[:, t, :], o[:, 0:T], ACT.Copy, scale=late_tok[:, t:t + 1])\
                    .then_inc(sem("act_evac"), 1)
            scaled_output("gates")
            nc.scalar.activation(gT[:], gT[:], ACT.Sigmoid).then_inc(sem("gates_sig"), 1)
            merge_gate(GATES_BEFORE[0])
            act.wait_ge(sem("gates_tr"), 1)
            nc.scalar.activation(gates[:], PS_TR[:, 0:T].rearrange("p (b c) -> p b c", b=TB)[:, :, 0:24], ACT.Copy)\
                .then_inc(sem("gates_read"), 1)

            def hidden(i, s):
                o = output(f"h{s}")
                r_ = slice(64 * i, 64 * i + 64)
                nc.scalar.activation(hg[r_, :], o[r_, 0:CMP_HID], ACT.Gelu_apprx_tanh).then_inc(sem("act_evac"), 1)
            hidden(0, "k")
            for n in GATES_BEFORE[1:3]:
                merge_gate_by_tanh(n)
            hidden(1, "v")
            merge_gate_by_tanh(GATES_BEFORE[3])
            act.wait_ge(sem("cmp_hid_tr"), 1)
            nc.scalar.activation(hgh[:], PS_TR[:, 0:2 * P].rearrange("p (n c) -> p n c", n=2), ACT.Copy)\
                .then_inc(sem("cmp_hid_hi"), 1)
            merge_gate_by_tanh(GATES_BEFORE[4])
            o = output("ck")
            act.wait_ge(sem("vc_zero"), 2)
            for g in range(NSA_G):
                r_, c_ = slice(64 * g, 64 * g + 64), slice(CPAD * g, CPAD * g + CPAD)
                ins = nc.scalar.activation(kcT[r_, c_], o[r_, c_], ACT.Copy)
            ins.then_inc(sem("act_evac"), 1)
            o = output("cv")
            nc.scalar.activation(vcT[:, 0:64], o[:, 0:64], ACT.Copy)
            nc.scalar.activation(vcT[:, 64:128], o[:, 0:64], ACT.Copy).then_inc(sem("act_evac"), 1)
            merge_gate_by_tanh(GATES_BEFORE[5])
            act.wait_ge(sem("vc_tr"), 1)
            for b in range(TB):
                for g in range(NSA_G):
                    r_ = slice((b * 2 + g) * CPAD, (b * 2 + g + 1) * CPAD)
                    ins = nc.scalar.activation(vc[r_, b, 64 * g:64 * g + 64], PS_TR[r_, 64 * g:64 * g + 64], ACT.Copy)
            ins.then_inc(sem("vc_read"), 1)
            def conv_tanh():
                for k in range(CONV_CT):
                    act.wait_ge(sem("conv_normed"), k + 1)
                    nc.scalar.activation(sq[:, 4 + k, :], sq[:, k, :], ACT.Tanh, scale=0.5).then_inc(sem("conv_tanh"), 1)

            def conv_high():
                for k in range(CONV_CT):
                    act.wait_ge(sem("conv_silu"), k + 1)
                    nc.scalar.activation(cnh[:, k, :], sq[:, 4 + k, :], ACT.Copy, scale=0.5).then_inc(sem("conv_hi"), 1)

            def nprob(x):
                act.wait_ge(sem("nmax"), x + 1)
                wait(act, "nprob_tr", x - 1)
                o = PS_S[x % 2]
                for b, c in enumerate((slice(0, P), slice(P, 3 * P))):
                    ins = nc.scalar.activation(npn[:, x % 2, c], o[:, c], ACT.Exp, bias=nnm[:, x % 2, b:b + 1],
                                               scale=NSA_D ** -0.5, accum_out=nrs[:, x % 2, b:b + 1])
                ins.then_inc(sem("nprob"), 1)

            def nprob_evac(x):
                act.wait_ge(sem("nprob_tr"), x + 1)
                wait(act, "nvalue", x - 1)
                nc.scalar.activation(npT[:, x % 2, :], PS_TR[:, 0:3 * P], ACT.Copy).then_inc(sem("nprob_tr_read"), 1)

            feed(f"mg{GATES_BEFORE[6]}")
            nprob(0)
            merge_gate_by_tanh(GATES_BEFORE[6])
            nprob(1)
            merge_gate_by_tanh(GATES_BEFORE[7])
            nprob_evac(0)
            for x in range(NSA_UNITS):
                if x % 4 == 1:
                    act.wait_ge(sem("cmp_read"), x // 4 + 1)
                    nc.scalar.activation(cpn[:], csc[:], ACT.Exp, scale=NSA_D ** -0.5).then_inc(sem("cmp_exp"), 1)
                if x in CONV_BETWEEN:
                    feed(f"yb{CONV_BETWEEN[x]}")
                if x == 2:
                    squares(n_ln)
                elif x == 4:
                    conv_tanh()
                if x + 2 < 16:
                    nprob(x + 2)
                if x in GATES_BETWEEN:
                    feed(f"mg{GATES_BETWEEN[x]}")
                j = x // 4
                if x % 4 == 2:
                    act.wait_ge(sem("cmp_tr"), j + 1)
                    wait(act, "natt", j)
                    nc.scalar.activation(cpT[:], PS_TR[:, 0:P], ACT.Copy).then_inc(sem("cmp_tr_read"), 1)
                if x + 1 < NSA_UNITS:
                    nprob_evac(x + 1)
                if x == 4:
                    conv_high()
                if x in GATES_BETWEEN:
                    merge_gate_by_tanh(GATES_BETWEEN[x])
                if x % 4 == 3:
                    act.wait_ge(sem("natt"), j + 1)
                    nc.scalar.activation(onh[:, j, :], PS_Y[:, 0:T], ACT.Copy).then_inc(sem("natt_hi"), 1)
            for n in range(KD):
                feed(f"ya{n}")
                act.wait_ge(sem("merged"), n + 1)
                nc.scalar.activation(mh[:, n, :], mt[:, n, :], ACT.Copy).then_inc(sem("merge_hi"), 1)
            feed_and_square("wo", n_ffn)

            def ff_act(i):
                act.wait_ge(sem("ff_conv"), 2 * i + 1)
                wait(act, "ff_gated", i - 1)
                nc.scalar.activation(fge[:, i % 2, :], fcv[:, 2 * i % 4, :], ACT.Gelu_apprx_tanh, bias=v("fconv_b", 2 * i))\
                    .then_inc(sem("ff_gelu"), 1)

            def ff_high(i):
                act.wait_ge(sem("ff_gated"), i + 1)
                nc.scalar.activation(ffh[:, i, :], fgt[:, i % 2, :], ACT.Copy).then_inc(sem("ff_hi"), 1)

            for i in range(KF):
                for s in "gv":
                    feed(f"f{s}{i}")
                if i:
                    ff_high(i - 1)
                ff_act(i)
                if i == KF - 4:
                    act.wait_ge(sem("p_in"), 16)
                    nc.scalar.activation(ph[:], pin[:], ACT.Copy).then_inc(sem("p_hi"), 1)
            ff_high(KF - 1)
            feed_and_square("fd", n_ple)

            for n in range(KD):
                scaled_output(f"pg{n}")
                nc.scalar.activation(psg[:, n % 2, :], psg[:, n % 2, :], ACT.Sigmoid).then_inc(sem("ple_gate"), 1)
                feed(f"pw{n}")
                if n:
                    square(n_fin2, n - 1)
            square(n_fin2, KD - 1)

        @block.vector
        def _(dve):
            chain = [0]

            def link(ins):
                chain[0] += 1
                ins.then_inc(sem("dve_chain"), 1)
                dve.wait_ge(sem("dve_chain"), chain[0])

            def output(name, t=0):
                o = jobs[name].out + t
                dve.wait_ge(sem("proj_done"), o + 1)
                return psum[o % PROJ_BANKS]

            tt, ts, stt = nc.vector.tensor_tensor, nc.vector.tensor_scalar, nc.vector.scalar_tensor_tensor

            def scaled(n, k):
                dst = n.out(k) if n.out else n.sqb(k)
                r_ = n.rstd if n.groups == 1 else n.rstd[:, k * n.groups // n.kt * T:][:, 0:T]
                stt(dst, n.src(k), gain(n, k), r_, ALU.mult, ALU.mult).then_inc(sem("norm_scaled"), 1)

            def low_part(n, k):
                dve.wait_ge(sem("norm_hi"), n.p0 + k + 1)
                tt(n.lo(k), n.sqb(k), n.hi(k).bitcast(f32), ALU.subtract).then_inc(sem("norm_lo"), 1)

            def newton(dst):
                m, y = msq[:, 0:dst.shape[-1]], step[:, 0:dst.shape[-1]]
                ts(dst.bitcast(i32), m.bitcast(i32), -0.5, 1597463007.0, ALU.mult, ALU.add)
                link(ts(m, m, -0.5, None, ALU.mult))
                for i in range(NEWTON):
                    link(tt(y, dst, dst, ALU.mult))
                    link(tt(y, y, m, ALU.mult))
                    ins = stt(dst, y, 1.5, dst, ALU.add, ALU.mult)
                    if i + 1 < NEWTON:
                        link(ins)
                return ins

            def inverse_root(n):
                dve.wait_ge(sem("norm_sum"), (n_mix if n is n_fin1 else n).i + 1)
                wait(dve, "norm_spread", n.read)
                sums, width = PS_M[:, n.col:n.col + n.groups * TB], n.groups * TB
                if n is n_mix:
                    dve.wait_ge(sem("norm_root"), n_fin1.i + 1)
                    y = step[:, 0:TB]
                    link(tt(y, root1[:], root1[:], ALU.mult))
                    link(tt(y, y, sums, ALU.mult))
                    sums = y
                link(ts(msq[:, 0:width], sums, 1.0 / n.width, EPS, ALU.mult, ALU.add))
                ins = newton(root1[:] if n is n_fin1 else root[:, 0:width])
                if n is n_mix:
                    link(ins)
                    ins = tt(late_tok[:], root[:, 0:TB], root1[:], ALU.mult)
                ins.then_inc(sem("norm_root"), 1)

            def late_root(n):
                inverse_root(n)
                dve.wait_ge(sem("norm_spread"), n.spread + 1)
                nc.vector.tensor_copy(late[:], n.rstd).then_inc(sem("norm_scaled"), 1)
                dve.wait_ge(sem("norm_scaled"), n.d0 + 1)

            def take(name, dst):
                o = output(name)
                rows = dst.shape[0]
                tt(dst, o[0:rows, 0:T], late[0:rows, :], ALU.mult).then_inc(sem("dve_evac"), 1)

            def taken(name):
                dve.wait_ge(sem("dve_evac"), freed[jobs[name].out][1])

            def norm_tiles(n):
                dve.wait_ge(sem("norm_spread"), n.spread + 1)
                for k in range(n.kt):
                    scaled(n, k)
                    if not n.out and k >= 2:
                        low_part(n, k - 2)
                if not n.out:
                    for k in range(max(0, n.kt - 2), n.kt):
                        low_part(n, k)

            def norm(n):
                inverse_root(n)
                norm_tiles(n)

            def add_square(n, k):
                dve.wait_ge(sem("norm_sq"), n.t0 + k + 1)
                if k == 0:
                    return
                acc = sqsum[:] if n is n_mix else n.sum
                if k > 1:
                    dve.wait_ge(sem("sq_added"), n.a0 + k - 1)
                tt(acc, n.sqb(0) if k == 1 else acc, n.sqb(k), ALU.add).then_inc(sem("sq_added"), 1)

            def late_low(n, k):
                dve.wait_ge(sem("norm_hi"), n.p0 + k + 1)
                stt(n.lo(k), n.src(k), gain(n, k), n.hi(k).bitcast(f32), ALU.mult, ALU.subtract)\
                    .then_inc(sem("norm_lo"), 1)

            nc.vector.memset(ones[:], 1.0).then_inc(sem("memset"), 1)
            nc.vector.memset(sraw[:, :, 0:SSM_TAPS - 1], 0.0).then_inc(sem("memset"), 1)
            dve.wait_ge(sem("vec_in"), 16)
            dve.wait_ge(sem("x_in"), 16)
            tt(gain12[:], vec[:, VC["final1"]:VC["final1"] + KD], vec[:, VC["g_mix"]:VC["g_mix"] + KD], ALU.mult)\
                .then_inc(sem("gain12"), 1)
            for k in range(KD):
                late_low(n_ssm, k)
            for k in range(KD):
                add_square(n_ssm, k)
            late_root(n_ssm)
            H = slice(0, SSM_H)
            take("dt", sp[H, 0, :])
            taken("dt")
            link(ts(sp[H, 0, :], sp[H, 0, :], v("dt_bias", 0, SSM_H), None, ALU.add))
            link(ts(sp[H, 1, :], sp[H, 0, :], -1.0, None, ALU.mult))
            tt(sp[H, 1, :], sp[H, 0, :], sp[H, 1, :], ALU.min).then_inc(sem("dt_step"), 1)

            def take_xbc(c):
                wait(dve, "ssm_conv", c - 3)
                take(f"xbc{c}", sraw[:, c % 4, SSM_TAPS - 1:])

            def dt_scan():
                dve.wait_ge(sem("dt_log"), 1)
                link(ts(dtT[H, :], sp[H, 2, :], 1.0, None, ALU.add))
                link(ts(dtT[H, :], dtT[H, :], -1.0, None, ALU.add))
                link(tt(dtT[H, :], sp[H, 2, :], dtT[H, :], ALU.subtract))
                link(tt(dtT[H, :], dtT[H, :], sp[H, 3, :], ALU.add))
                stt(dtT[H, :], sp[H, 0, :], 0.0, dtT[H, :], ALU.max, ALU.add).then_inc(sem("dt_scan"), 1)
                dve.wait_ge(sem("dt_scan"), 1)
                dve.wait_ge(sem("exp_a"), 1)
                link(ts(sp[H, 1, :], dtT[H, :], expa[H, :], -1.0, ALU.mult, ALU.mult))
                link(ts(sp[H, 0, :], dtT[H, :], 0.0, 1.0, ALU.mult, ALU.add))
                nc.vector.tensor_tensor_scan(acr[H, 0:T], sp[H, 0, :], sp[H, 1, :], 0.0, ALU.mult, ALU.add)\
                    .then_inc(sem("dt_scan"), 1)
                dve.wait_ge(sem("dt_scan"), 2)
                nc.vector.tensor_copy(acr[H, T:T + P], acr[H, P:T]).then_inc(sem("dt_scan"), 1)
                dve.wait_ge(sem("dt_scan"), 3)

            def conv(dst, src, taps, weight):
                for i in range(taps):
                    w = weight(i)
                    if i == 0:
                        ins = ts(dst, src(0), w, None, ALU.mult)
                    else:
                        ins = stt(dst, src(i), w, dst, ALU.mult, ALU.add)
                    if i + 1 < taps:
                        link(ins)
                return ins

            take_xbc(0)
            take_xbc(1)
            for c in range(SSM_CT):
                if c == 1:
                    dt_scan()
                if 2 <= c + 1 < SSM_CT:
                    take_xbc(c + 1)
                taken(f"xbc{c}")
                wait(dve, "ssm_silu", c - 1)
                conv(scv[:, c % 2, :], lambda i: sraw[:, c % 4, i:i + T], SSM_TAPS,
                     lambda i: v("sconv_w", c * SSM_TAPS + i)).then_inc(sem("ssm_conv"), 1)
                if c == 15:
                    dve.wait_ge(sem("decay_hi"), 1)
                    tt(acp[SSM_H:2 * SSM_H, :], acr[H, :], acp[H, :].bitcast(f32), ALU.subtract)\
                        .then_inc(sem("decay_parts"), 1)
                if c == 10:
                    dve.wait_ge(sem("dt_tr"), 1)
                    nc.vector.tensor_copy(dtn[:], PS_TR[:, 0:64].rearrange("p (b h) -> p b h", b=2))\
                        .then_inc(sem("dt_tok"), 1)
                    ts(nacn[:], PS_TR[:, 64:128].rearrange("p (b h) -> p b h", b=2), -1.0, None, ALU.mult)\
                        .then_inc(sem("dt_tok"), 1)

            def scale_x(j):
                dve.wait_ge(sem("x_tr"), j + 1)
                wait(dve, "y", 2 * (j - 1))
                src = PS_TR[:, 0:T].rearrange("p (b e d) -> p b e d", b=2, e=2)
                d = dtn[:, :, 2 * j:2 * j + 2].unsqueeze(3).broadcast_to([P, TB, 2, 64])
                tt(xdt[:, j % 2, :, :, :], src, d, ALU.mult).then_inc(sem("xdt"), 1)

            def decayed(hd):
                g = hd // 4
                dve.wait_ge(sem("decay_exp"), hd + 1)
                dve.wait_ge(sem("cb_evac"), g + 1)
                wait(dve, "y", hd - HEADS + 1)
                tt(mb[:, hd % HEADS, :], eb[:, hd % 2, :], cbs[:, g % 2, :], ALU.mult).then_inc(sem("decayed"), 1)

            dve.wait_ge(sem("dt_tok"), 2)
            take("sz0", szb[:, 0, :])
            scale_x(0)
            decayed(0)
            decayed(1)
            for j in range(SSM_PAIRS):
                if j + 1 < SSM_PAIRS:
                    wait(dve, "gated", j)
                    take(f"sz{j + 1}", szb[:, (j + 1) % 2, :])
                if j + 1 < SSM_PAIRS:
                    scale_x(j + 1)
                if j % 2 == 0 and j >= 4:
                    norm_tiles(n_grp[(j - 4) // 2])
                if j + 1 < SSM_PAIRS:
                    decayed(2 * j + 2)
                    decayed(2 * j + 3)
                dve.wait_ge(sem("z_tanh"), j + 1)
                taken(f"sz{j}")
                stt(szb[:, j % 2, :], zb[:], 1.0, szb[:, j % 2, :], ALU.add, ALU.mult).then_inc(sem("z_gate"), 1)
                dve.wait_ge(sem("y"), 2 * j + 2)
                wait(dve, "gated", j)
                stt(yt[:], xs[:, j, :], v("ssm_d", j), PS_Y[:, 0:T], ALU.mult, ALU.add).then_inc(sem("y_read"), 1)
                if j % 2 and 3 <= j < SSM_PAIRS - 1:
                    inverse_root(n_grp[(j - 3) // 2])
                dve.wait_ge(sem("z_gate"), j + 1)
                dve.wait_ge(sem("y_read"), j + 1)
                stt(gb[:, j % 4, :], yt[:], 0.5, szb[:, j % 2, :], ALU.mult, ALU.mult).then_inc(sem("gated"), 1)
            norm(n_grp[6])

            def add_to_residual(prefix, n):
                for k in range(KD):
                    o = output(f"{prefix}{k}")
                    tt(h[:, k, :], o[:, 0:T], h[:, k, :], ALU.add).then_inc(sem("dve_evac"), 1)
                    if k:
                        add_square(n, k - 1)
                        late_low(n, k - 1)
                add_square(n, KD - 1)
                late_low(n, KD - 1)
                if n is n_mix:
                    inverse_root(n_fin1)
                late_root(n)

            add_to_residual("so", n_mla)

            def rotate(i):
                dst = kr[:] if i == 0 else qr[:, i - 1, :]
                who, count = freed[jobs[rope_job(i)].out]
                dve.wait_ge(sem(f"{who}_evac"), count)
                wait(dve, "rope_out", i)
                tt(r2[:], rx[:, i % 2, :], cos, ALU.mult).then_inc(sem("rope_cos"), 1)
                dve.wait_ge(sem("rope_swap"), i + 1)
                tt(r1[:], PS_TR[:, 0:T], sin, ALU.mult).then_inc(sem("rope_swapped_read"), 1)
                dve.wait_ge(sem("rope_swapped_read"), i + 1)
                dve.wait_ge(sem("rope_cos"), i + 1)
                tt(dst, r1[:], r2[:], ALU.add).then_inc(sem("rope_out"), 1)

            for n in range(2):
                take(f"ckv{n}", ckr[:, n, :])
            for n in range(2):
                take(f"cq{n}", cqr[:, n, :])
            inverse_root(n_kv)
            take("cq2", cqr[:, 2, :])
            take("kr", rx[:, 0, :])
            norm_tiles(n_kv)
            take("mz0", mzb[:, 0, :])
            inverse_root(n_q)
            take("mz1", mzb[:, 1, :])
            norm_tiles(n_q)
            for i in range(9):
                rotate(i)

            def row_max(bank, m, neg, i, scale, done):
                link(nc.vector.tensor_reduce(m[:, i % 2, 0:1], bank[:, 0:P], AX.X, ALU.max))
                link(nc.vector.tensor_reduce(m[:, i % 2, 1:2], bank[:, P:3 * P], AX.X, ALU.max))
                ts(neg[:, i % 2, :], m[:, i % 2, :], -scale, None, ALU.mult).then_inc(sem(done), 1)

            def mla_max(hd):
                dve.wait_ge(sem("score"), hd + 1)
                row_max(PS_S[hd % 2], mx, nm, hd, (MLA_D + MLA_R) ** -0.5, "max")

            def att_low(hd):
                dve.wait_ge(sem("att_hi"), hd + 1)
                tt(ogl[:, hd, :], ogt[:, hd % 2, :], ogh[:, hd, :].bitcast(f32), ALU.subtract).then_inc(sem("att_lo"), 1)

            def prob_scale(hd):
                dve.wait_ge(sem("prob"), hd + 1)
                link(nc.vector.reciprocal(rr[:, hd % 2, :], rs[:, hd % 2, :]))
                ts(pn[:, hd % 2, 0:P], pn[:, hd % 2, 0:P], rr[:, hd % 2, 0:1], None, ALU.mult)
                ts(pn[:, hd % 2, P:3 * P], pn[:, hd % 2, P:3 * P], rr[:, hd % 2, 1:2], None, ALU.mult)\
                    .then_inc(sem("prob_norm"), 1)

            mla_max(0)
            prob_scale(0)
            mla_max(1)
            prob_scale(1)
            for hd in range(MLA_H):
                if hd + 2 < MLA_H:
                    wait(dve, "att_read", hd)
                    take(f"mz{hd + 2}", mzb[:, (hd + 2) % 3, :])
                if hd + 2 < MLA_H:
                    mla_max(hd + 2)
                dve.wait_ge(sem("mz_tanh"), hd + 1)
                taken(f"mz{hd}")
                stt(mzb[:, hd % 3, :], mze[:], 1.0, mzb[:, hd % 3, :], ALU.add, ALU.mult).then_inc(sem("mz_gate"), 1)
                dve.wait_ge(sem("mz_gate"), hd + 1)
                dve.wait_ge(sem("att"), hd + 1)
                stt(ogt[:, hd % 2, :], PS_Y[:, 0:T], 0.5, mzb[:, hd % 3, :], ALU.mult, ALU.mult).then_inc(sem("att_read"), 1)
                if hd + 2 < MLA_H:
                    prob_scale(hd + 2)
                if hd:
                    att_low(hd - 1)
            att_low(MLA_H - 1)
            dve.wait_ge(sem("att"), MLA_H)
            nc.vector.memset(vc[:], 0.0).then_inc(sem("vc_zero"), 1)
            nc.vector.memset(kcT[:], 0.0).then_inc(sem("vc_zero"), 1)
            link(nc.vector.memset(cx[:], 0.0))
            dve.sem_inc(sem("cx_zero"), 1)
            add_to_residual("mo", n_mix)


            taps = [(i + e, t) for i in range(0, CONV_CT, 2) for t in range(CONV_TAPS + 1) for e in range(2)]
            tap_at = [0]

            def conv31(n_taps):
                for i, t in taps[tap_at[0]:tap_at[0] + n_taps]:
                    dst = ccv[:, i, :]
                    if t == 0:
                        dve.wait_ge(sem("conv_in"), i + 1)
                        ins = ts(dst, cpad[:, i, 0:T], v("conv_w", i * CONV_TAPS), None, ALU.mult)
                    else:
                        dve.wait_ge(sem("conv_tap"), tap_at[0] - 1)
                        if t < CONV_TAPS:
                            ins = stt(dst, cpad[:, i, t:t + T], v("conv_w", i * CONV_TAPS + t), dst, ALU.mult, ALU.add)
                        else:
                            ins = ts(dst, dst, v("conv_b", i), None, ALU.add)
                    ins.then_inc(sem("conv_tap"), 1)
                    tap_at[0] += 1

            for i in range(CONV_CT):
                take(f"cg{i}", csg[:, i, :])
                if i == 2:
                    dve.wait_ge(sem("norm_spread"), n_fin1.spread + 1)
                if i >= 2:
                    for k in range(4 * (i - 2), 4 * (i - 1)):
                        scaled(n_fin1, k)
                conv31(3 if i >= 2 else 0)
                wait(dve, "conv_in", i)
                take(f"cv{i}", cvt[:])
                conv31(2 if i >= 2 else 0)
                if i == 0:
                    link(nc.vector.memset(cpad[:, :, 0:CONV_TAPS - 1], 0.0))
                taken(f"cv{i}")
                dve.wait_ge(sem("conv_gate"), i + 1)
                tt(cpad[:, i, CONV_TAPS - 1:], cvt[:], csg[:, i, :], ALU.mult).then_inc(sem("conv_in"), 1)
            for i in range(2):
                take(f"kvc{i}", kvt[:, i, :])
                conv31(MIX_TAPS)
            for j in range(NSA_J):
                take(f"nq{j}", nq[:, j, :])
                conv31(MIX_TAPS)
                if j == 0:
                    for i, pos in enumerate(("pos_k", "pos_v")):
                        dve.wait_ge(sem("cmp_shift"), i + 1)
                        for g in range(NSA_G):
                            row = ce[:, i, g, :]
                            src = row.rearrange("p (c k e) -> p k c e", k=CMP_STRIDE // 2, e=2)[:, :, :, 0]
                            for half in range(2):
                                s_ = src[:, :, half:half + N_CMP]
                                c_ = (2 * i + g) * CPAD
                                d_ = cx[:, 8 * half:8 * half + 8, c_:c_ + N_CMP]
                                p_ = vec[:, VC[pos] + 8 * half:VC[pos] + 8 * half + 8].unsqueeze(2)\
                                    .broadcast_to([P, 8, N_CMP])
                                ins = tt(d_, s_, p_, ALU.add)
                    ins.then_inc(sem("cmp_x"), 1)
            dve.wait_ge(sem("cmp_hi"), 1)
            tt(cxl[:], cx[:], cxh[:].bitcast(f32), ALU.subtract).then_inc(sem("cmp_lo"), 1)
            take("ks", ksT[:])
            conv31(MIX_TAPS)
            take("kw", kwT[:])
            conv31(3 * MIX_TAPS)
            take("gates", gT[:])
            conv31(MIX_TAPS)

            def take_gate(n):
                take(f"mg{n}", gm[:, n, :])

            take_gate(GATES_BEFORE[0])
            conv31(3 * MIX_TAPS)
            for n in GATES_BEFORE[1:3]:
                take_gate(n)
                conv31(MIX_TAPS)
            conv31(2 * MIX_TAPS)
            take_gate(GATES_BEFORE[3])
            dve.wait_ge(sem("cmp_hid_hi"), 1)
            tt(hgl[:], PS_TR[:, 0:2 * P].rearrange("p (n c) -> p n c", n=2), hgh[:].bitcast(f32), ALU.subtract)\
                .then_inc(sem("cmp_hid_lo"), 1)
            conv31(MIX_TAPS)
            for n in GATES_BEFORE[4:6]:
                take_gate(n)
                conv31(MIX_TAPS)

            def conv_centre():
                dve.wait_ge(sem("ln_sum"), 1)
                link(ts(yat[:], PS_M[:, 0:T], 1.0 / (CONV_CT * P), None, ALU.mult))
                dve.wait_ge(sem("conv_tap"), len(taps))
                tt(ccv[:], ccv[:], yat[:].unsqueeze(1).broadcast_to([P, CONV_CT, T]), ALU.subtract)\
                    .then_inc(sem("ln_centred"), 1)

            def conv_bias():
                for k in range(CONV_CT):
                    dve.wait_ge(sem("norm_scaled"), n_ln.d0 + k + 1)
                    ts(sq[:, k, :], sq[:, k, :], v("ln_b", k), None, ALU.add).then_inc(sem("conv_normed"), 1)

            def conv_silu():
                for k in range(CONV_CT):
                    dve.wait_ge(sem("conv_tanh"), k + 1)
                    stt(sq[:, 4 + k, :], sq[:, 4 + k, :], 1.0, sq[:, k, :], ALU.add, ALU.mult)\
                        .then_inc(sem("conv_silu"), 1)
                for k in range(CONV_CT):
                    dve.wait_ge(sem("conv_hi"), k + 1)
                    stt(cnl[:, k, :], sq[:, 4 + k, :], 0.5, cnh[:, k, :].bitcast(f32), ALU.mult, ALU.subtract)\
                        .then_inc(sem("conv_lo"), 1)

            def nsa_max(x):
                dve.wait_ge(sem("nscore"), x + 1)
                row_max(PS_S[x % 2], nmx, nnm, x, NSA_D ** -0.5, "nmax")

            four = lambda t: t.rearrange("p (a c) -> p a c", c=CPAD)
            spread = lambda t: t.unsqueeze(2).broadcast_to([P, 4, CPAD])

            def nprob_scale(x):
                j, g, ty = x // 4, x // 2 % 2, x % 2
                dve.wait_ge(sem("nprob"), x + 1)
                link(nc.vector.reciprocal(nrr[:, x % 2, :], nrs[:, x % 2, :]))
                col = (1 + ty) * 8 + g * NSA_J + j
                link(tt(nrr[:, x % 2, :], nrr[:, x % 2, :], gates[:, :, col], ALU.mult))
                ts(npn[:, x % 2, 0:P], npn[:, x % 2, 0:P], nrr[:, x % 2, 0:1], None, ALU.mult)
                ts(npn[:, x % 2, P:3 * P], npn[:, x % 2, P:3 * P], nrr[:, x % 2, 1:2], None, ALU.mult)\
                    .then_inc(sem("nprob_norm"), 1)

            nsa_max(0)
            take_gate(GATES_BEFORE[6])
            nprob_scale(0)
            conv31(MIX_TAPS)
            nsa_max(1)
            take_gate(GATES_BEFORE[7])
            nprob_scale(1)
            for x in range(NSA_UNITS):
                j = x // 4
                if x + 2 < 16:
                    nsa_max(x + 2)
                if x % 4 == 1:
                    dve.wait_ge(sem("cmp_exp"), j + 1)
                    link(tt(cpn[:], cpn[:], cmp_ok, ALU.mult))
                    link(nc.vector.tensor_reduce(crs[:], four(cpn[:]), AX.X, ALU.add))
                    link(ts(crs[:], crs[:], 1e-30, None, ALU.max))
                    link(nc.vector.reciprocal(crr[:], crs[:]))
                    link(tt(crr[:].rearrange("p (b g) -> p b g", b=2), crr[:].rearrange("p (b g) -> p b g", b=2),
                            gates[:, :, j:j + 5:4], ALU.mult))
                    tt(four(cpn[:]), four(cpn[:]), spread(crr[:]), ALU.mult).then_inc(sem("cmp_prob"), 1)
                if x + 2 < NSA_UNITS:
                    nprob_scale(x + 2)
                if x in CONV_BETWEEN:
                    n = CONV_BETWEEN[x]
                    o = output(f"yb{n}")
                    wait(dve, "merge_gate", len(GATES_BEFORE) + sum(u < x for u in GATES_BETWEEN))
                    stt(mt[:, n, :], o[:, 0:T], v("b_co", n), gm[:, 8 + n, :], ALU.add, ALU.mult).then_inc(sem("dve_evac"), 1)
                if x in GATES_BETWEEN:
                    take_gate(GATES_BETWEEN[x])
                if x % 4 == 0:
                    dve.wait_ge(sem("cmp_score"), j + 1)
                    wait(dve, "cmp_tr", j)
                    link(nc.vector.tensor_reduce(cmx[:], four(PS_M[:, 0:P]), AX.X, ALU.max))
                    tt(four(csc[:]), four(PS_M[:, 0:P]), spread(cmx[:]), ALU.subtract).then_inc(sem("cmp_read"), 1)
                if x == 0:
                    conv31(len(taps))
                elif x == 1:
                    conv_centre()
                elif x == 2:
                    inverse_root(n_ln)
                elif x == 3:
                    norm_tiles(n_ln)
                    conv_bias()
                elif x == 4:
                    conv_silu()
                if x % 4 == 3:
                    dve.wait_ge(sem("natt_hi"), j + 1)
                    tt(onl[:, j, :], PS_Y[:, 0:T], onh[:, j, :].bitcast(f32), ALU.subtract).then_inc(sem("natt_lo"), 1)

            def merge_low(n):
                dve.wait_ge(sem("merge_hi"), n + 1)
                tt(ml[:, n, :], mt[:, n, :], mh[:, n, :].bitcast(f32), ALU.subtract).then_inc(sem("merge_lo"), 1)

            for n in range(KD):
                o = output(f"ya{n}")
                if n == 0:
                    wait(dve, "merge_gate", 2 * KD)
                wait(dve, "merged", n)
                tt(yat[:], o[:, 0:T], gm[:, n, :], ALU.mult).then_inc(sem("dve_evac"), 1)
                dve.wait_ge(sem("dve_evac"), freed[jobs[f"ya{n}"].out][1])
                tt(mt[:, n, :], mt[:, n, :], yat[:], ALU.add).then_inc(sem("merged"), 1)
                if n:
                    merge_low(n - 1)
            merge_low(KD - 1)
            add_to_residual("wo", n_ffn)

            link(nc.vector.memset(fraw[:, :, 0:FF_TAPS - 1], 0.0))

            def take_ff(c):
                wait(dve, "ff_conv", c - 3)
                take(f"f{'gv'[c % 2]}{c // 2}", fraw[:, c % 4, FF_TAPS - 1:])

            take_ff(0)

            def ff_gate(i):
                dve.wait_ge(sem("ff_gelu"), i + 1)
                wait(dve, "ff_lo", i - 1)
                stt(fgt[:, i % 2, :], fcv[:, (2 * i + 1) % 4, :], v("fconv_b", 2 * i + 1), fge[:, i % 2, :],
                    ALU.add, ALU.mult).then_inc(sem("ff_gated"), 1)

            def ff_low(i):
                dve.wait_ge(sem("ff_hi"), i + 1)
                tt(ffl[:, i, :], fgt[:, i % 2, :], ffh[:, i, :].bitcast(f32), ALU.subtract).then_inc(sem("ff_lo"), 1)

            for i in range(KF):
                for e, s in enumerate("gv"):
                    c = 2 * i + e
                    if c + 1 < 2 * KF:
                        take_ff(c + 1)
                    taken(f"f{s}{i}")
                    conv(fcv[:, c % 4, :], lambda t: fraw[:, c % 4, t:t + T], FF_TAPS,
                         lambda t: v("fconv_w", c * FF_TAPS + t)).then_inc(sem("ff_conv"), 1)
                if i:
                    ff_low(i - 1)
                dve.wait_ge(sem("ff_conv"), 2 * i + 2)
                ff_gate(i)
            ff_low(KF - 1)
            dve.wait_ge(sem("p_hi"), 1)
            tt(pl[:], pin[:], ph[:].bitcast(f32), ALU.subtract).then_inc(sem("p_lo"), 1)
            add_to_residual("fd", n_ple)

            for n in range(KD):
                wait(dve, "dve_evac", freed[jobs[f"pw{n - 2}"].out][1] if n >= 2 else 0)
                take(f"pg{n}", psg[:, n % 2, :])
                o = output(f"pw{n}")
                dve.wait_ge(sem("ple_gate"), n + 1)
                wait(dve, "ple_added", n)
                tt(pt[:], o[:, 0:T], psg[:, n % 2, :], ALU.mult).then_inc(sem("dve_evac"), 1)
                dve.wait_ge(sem("dve_evac"), freed[jobs[f"pw{n}"].out][1])
                tt(h[:, n, :], h[:, n, :], pt[:], ALU.add).then_inc(sem("ple_added"), 1)
                if n:
                    add_square(n_fin2, n - 1)
            add_square(n_fin2, KD - 1)
            norm(n_fin2)


def arena_base(nc, kb):
    return nc.sbuf_base - kb * 1024


def shape_constants():
    c = np.zeros((P, N_CONST), np.float32)
    i = np.arange(P)
    c[:, 0:128] = np.eye(P)
    s = np.zeros((P, P))
    s[i ^ 32, i] = 1.0
    c[:, 128:256] = s
    c[:, 256:384] = np.where(i[None, :] > i[:, None], NEG, 0.0)
    tri = np.where(i[None, :] < i[:, None], NEG, 0.0)
    c[:, 384:512] = tri
    c[:, 640:768] = tri
    tok = np.arange(TB)[None, :, None, None] * P + i[:, None, None, None]
    key = np.arange(CPAD)[None, None, None, :]
    ok = (key * CMP_STRIDE + CMP_LEN - 1 <= tok) & (key < N_CMP)
    ok = np.broadcast_to(ok, (P, TB, NSA_G, CPAD)).reshape(P, P)
    c[:, 768:896] = np.where(ok, 0.0, NEG)
    c[:, 896:1024] = ok
    half = MLA_R // 2
    freq = np.float32(500000.0) ** (-np.arange(half, dtype=np.float32) / half)
    ang = np.arange(T, dtype=np.float32)[None, :] * freq[i % half][:, None]
    c[:, 1024:1280] = np.cos(ang)
    c[:, 1280:1536] = np.where((i // half % 2 == 0)[:, None], -np.sin(ang), np.sin(ang))
    return c


def pack_weights(inputs):
    jobs, _, _, n_slabs = plan()
    stream = np.zeros((n_slabs * BLK, P, P), np.float32)
    flat = {}
    for name, array, cols, rows, kind, _ in weight_jobs():
        if array not in flat:
            w = np.asarray(inputs[array])[0]
            flat[array] = np.concatenate([w, np.zeros((w.shape[0], 1), w.dtype)], axis=1)
        w = flat[array][:, cols]
        if rows is not None:
            w = w[rows]
        j = jobs[name]
        blocks = w.reshape(j.kt, P, j.wide, P).transpose(0, 2, 1, 3).reshape(j.blocks, P, P)
        stream[j.block:j.block + j.blocks] = blocks
    return np.ascontiguousarray(stream.reshape(n_slabs, BLK, P, P).transpose(0, 2, 1, 3).reshape(n_slabs, P, SLAB))


def pack_vectors(inputs):
    VC, n = vector_columns()
    vec = np.zeros((P, n), np.float32)

    def put(name, a):
        a = np.asarray(a).reshape(-1, P)
        vec[:, VC[name]:VC[name] + a.shape[0]] = a.T

    g = {k: np.asarray(x) for k, x in inputs.items()}
    put("norm0", g["norm_w"][0])
    put("norm1", g["norm_w"][1])
    put("final1", g["final_norm_w"])
    order = [conv_tile(c) for c in range(SSM_CT)]
    put("sconv_w", g["ssm_conv_w"][0].reshape(SSM_TAPS, SSM_CT, P)[:, order].transpose(1, 0, 2))
    put("sconv_b", g["ssm_conv_b"][0].reshape(SSM_CT, P)[order])
    put("ssm_d", np.repeat(g["ssm_D"][0], 64))
    put("ssm_nw", g["ssm_norm_w"][0])
    vec[0:SSM_H, VC["dt_bias"]] = g["ssm_dt_bias"][0]
    vec[0:SSM_H, VC["a_log"]] = g["ssm_A_log"][0]
    put("qnorm", g["mla_q_norm_w"][0])
    put("kvnorm", g["mla_kv_norm_w"][0])
    put("g_mix", g["g_mix_2"][0])
    put("pos_k", g["cmp_pos_k_2"][0])
    put("pos_v", g["cmp_pos_v_2"][0])
    put("conv_w", g["conv_w_2"][0].reshape(CONV_TAPS, CONV_CT, P).transpose(1, 0, 2))
    put("conv_b", g["conv_b_2"][0])
    put("ln_g", g["conv_ln_g_2"][0])
    put("ln_b", g["conv_ln_b_2"][0])
    put("b_co", g["b_conv_out_2"][0])
    put("g_ffn", g["g_ffn_2"][0])
    put("fconv_w", g["ffn_conv_w_2"][0].reshape(FF_TAPS, 2, KF, P).transpose(2, 1, 0, 3))
    put("fconv_b", g["ffn_conv_b_2"][0].reshape(2, KF, P).transpose(1, 0, 2))
    put("g_ple", g["g_ple_2"][0])
    put("g_final", g["g_final_2"])
    return vec


def feature_major(a):
    a = np.asarray(a)
    return np.ascontiguousarray(a.T.reshape(-1, P, T).transpose(1, 0, 2))


def kernel(**inputs):
    import concourse.bacc as bacc
    from concourse.bass_utils import run_bass_kernel_spmd

    arrays = {
        "slabs": pack_weights(inputs),
        "vectors": pack_vectors(inputs),
        "shape_consts": shape_constants(),
        "x_fm": feature_major(np.asarray(inputs["x"])[0]),
        "p_fm": feature_major(np.asarray(inputs["p_2"])[0, 0]),
    }
    nc = bacc.Bacc("TRN2", target_bir_lowering=False, num_devices=1)
    aps = [nc.dram_tensor(n, a.shape, mybir.dt.from_np(a.dtype), kind="ExternalInput").ap() for n, a in arrays.items()]
    out = nc.dram_tensor("out_fm", (P, KD, T), mybir.dt.float32, kind="ExternalOutput").ap()
    build(nc, *aps, out)
    r = run_bass_kernel_spmd(nc, [arrays], core_ids=[0])
    y = r.results[0]["out_fm"]
    return np.ascontiguousarray(y.transpose(1, 0, 2).reshape(DM, T).T).reshape(1, T, DM)
```
